# Optimizing a Trainium2 kernel written in Bass

```python
import math
import jax
import jax.numpy as jnp
from jax import lax
import numpy as np
import jax, jax.numpy as jnp

D_MODEL = 1024
BATCH = 1
SEQ = 256
DEPTH = 2

GRID_W = 64
CTX_LEN = 256
N_MIXERS = 3
EXPAND = 2
D_INNER = EXPAND * D_MODEL
NORM_EPS = 1e-6

RWKV_HEAD = 64
RWKV_HEADS = D_INNER // RWKV_HEAD
RWKV_DECAY_LORA = 64
RWKV_ICLR_LORA = 64
RWKV_VRES_LORA = 32
RWKV_N_MU = 6
RWKV_GN_EPS = 64e-5

HYENA_EMB = 33
HYENA_FILTER_WIDTH = 64
HYENA_SIN_W = 1.0
HYENA_FAST_DECAY = 0.3
HYENA_SLOW_DECAY = 1.5
HYENA_TARGET = 1e-2

HGRN_KEY = 128
HGRN_HEADS = D_INNER // HGRN_KEY
HGRN_VAL = D_INNER // HGRN_HEADS
HGRN_CHUNK = 32


def rms_norm(x, g, eps=NORM_EPS):
    xf = x.astype(jnp.float32)
    y = xf * lax.rsqrt(jnp.mean(xf * xf, axis=-1, keepdims=True) + eps)
    return (y * g.astype(jnp.float32)).astype(x.dtype)

def adaln(cond, w, b):
    return jnp.split(jax.nn.silu(cond) @ w + b, 3, axis=-1)

def split_heads(a, n_heads):
    return a.reshape(a.shape[:-1] + (n_heads, a.shape[-1] // n_heads))

def merge_heads(a):
    return a.reshape(a.shape[:-2] + (a.shape[-2] * a.shape[-1],))

def grid_shift(h):
    b, t, d = h.shape
    rows = t // GRID_W
    g = h.reshape(b, rows, GRID_W, d)
    q = d // 4
    left = jnp.pad(g[:, :, :-1, :q], ((0, 0), (0, 0), (1, 0), (0, 0)))
    right = jnp.pad(g[:, :, 1:, q:2 * q], ((0, 0), (0, 0), (0, 1), (0, 0)))
    up = jnp.pad(g[:, :-1, :, 2 * q:3 * q], ((0, 0), (1, 0), (0, 0), (0, 0)))
    down = jnp.pad(g[:, 1:, :, 3 * q:], ((0, 0), (0, 1), (0, 0), (0, 0)))
    return jnp.concatenate([left, right, up, down], axis=-1).reshape(b, t, d)

def seq_shift(h):
    half = h.shape[-1] // 2
    prev = jnp.pad(h[:, :-1, :half], ((0, 0), (1, 0), (0, 0)))
    nxt = jnp.pad(h[:, 1:, half:], ((0, 0), (0, 1), (0, 0)))
    return jnp.concatenate([prev, nxt], axis=-1)

def rwkv7_col_groups(vres):
    widths = [D_INNER] * 4 + [RWKV_DECAY_LORA] * 2 + [RWKV_ICLR_LORA] * 2
    groups = [0, 1, 2, 3, 4, 4, 5, 5]
    if vres:
        widths.append(RWKV_VRES_LORA)
        groups.append(2)
    return np.repeat(np.asarray(groups), np.asarray(widths))

def rwkv7_prepare(h, h_shift, p, v_first):
    e = D_INNER
    vres = 'v0' in p
    mu_cols = p['mu'][rwkv7_col_groups(vres)].T
    proj = h @ p['w_in'] + (h_shift - h) @ (p['w_in'] * mu_cols)
    r, k, v, gate = (proj[..., j * e:(j + 1) * e] for j in range(4))
    lo = proj[..., 4 * e:]
    nd, na = 2 * RWKV_DECAY_LORA, 2 * RWKV_ICLR_LORA
    w_lo = split_heads(lo[..., :nd], 2)
    a_lo = split_heads(lo[..., nd:nd + na], 2)
    if vres:
        v = v + (v_first - v) * jax.nn.sigmoid(p['v0'] + lo[..., nd + na:] @ p['v2'])
    else:
        v_first = v
    kk = split_heads(k * p['k_k'], RWKV_HEADS).astype(jnp.float32)
    kk = kk / jnp.maximum(jnp.sqrt(jnp.sum(kk * kk, axis=-1, keepdims=True)), 1e-12)
    return (split_heads(r, RWKV_HEADS), k, split_heads(v, RWKV_HEADS), gate, kk, w_lo, a_lo, v_first)

def rwkv7_direction(k, w_lo, a_lo, p, z):
    w_raw = -jax.nn.softplus(-(p['w0'][z] + jnp.tanh(w_lo[..., z, :]) @ p['w2'][z])) - 0.5
    decay = jnp.exp(-jnp.exp(w_raw.astype(jnp.float32)))
    a = jax.nn.sigmoid(p['a0'][z] + a_lo[..., z, :] @ p['a2'][z])
    k_dir = k * (1.0 + (a - 1.0) * p['k_a'])
    return (split_heads(decay, RWKV_HEADS), split_heads(k_dir, RWKV_HEADS), split_heads(a, RWKV_HEADS))

def rwkv7_scan(r, decay, k, v, kk, a, s0, reverse):
    xs = tuple(jnp.moveaxis(t.astype(jnp.float32), 1, 0) for t in (r, decay, k, v, -kk, kk * a))

    def step(s, inp):
        r_t, w_t, k_t, v_t, a_t, b_t = inp
        sa = jnp.einsum('bhvk,bhk->bhv', s, a_t)
        s = s * w_t[:, :, None, :] + sa[..., None] * b_t[:, :, None, :] + v_t[..., None] * k_t[:, :, None, :]
        return s, jnp.einsum('bhvk,bhk->bhv', s, r_t)

    s_last, ys = lax.scan(step, s0, xs, reverse=reverse)
    return jnp.moveaxis(ys, 0, 1), s_last

def rwkv7_readout(y, bonus, gate, p, dtype):
    mean = jnp.mean(y, axis=-1, keepdims=True)
    var = jnp.mean(jnp.square(y - mean), axis=-1, keepdims=True)
    yn = merge_heads((y - mean) * lax.rsqrt(var + RWKV_GN_EPS))
    yn = yn * p['ln_w'].astype(jnp.float32) + p['ln_b'].astype(jnp.float32)
    return ((yn + merge_heads(bonus)) * jax.nn.silu(gate.astype(jnp.float32))).astype(dtype)

def rwkv7_mixer(hx, hc, p, v_first_x, v_first_c, ctx_out):
    rx, kx, vx, gx, kkx, wlx, alx, v_first_x = rwkv7_prepare(hx, grid_shift(hx), p, v_first_x)
    rc, kc, vc, gc, kkc, wlc, alc, v_first_c = rwkv7_prepare(hc, seq_shift(hc), p, v_first_c)
    s0 = jnp.zeros((hx.shape[0], RWKV_HEADS, RWKV_HEAD, RWKV_HEAD), jnp.float32)
    r_k = p['r_k'].astype(jnp.float32)
    yx = bx = yc = bc = 0.0
    for z in range(2):
        dc, kdc, ac = rwkv7_direction(kc, wlc, alc, p, z)
        dx, kdx, ax = rwkv7_direction(kx, wlx, alx, p, z)
        yc_z, s_ctx = rwkv7_scan(rc, dc, kdc, vc, kkc, ac, s0, z == 1)
        yx_z, _ = rwkv7_scan(rx, dx, kdx, vx, kkx, ax, s_ctx, z == 1)
        yx = yx + yx_z
        bx = bx + jnp.sum(rx * kdx * r_k, axis=-1, keepdims=True) * vx
        if ctx_out:
            yc = yc + yc_z
            bc = bc + jnp.sum(rc * kdc * r_k, axis=-1, keepdims=True) * vc
    ux = rwkv7_readout(yx, bx, gx, p, hx.dtype)
    uc = rwkv7_readout(yc, bc, gc, p, hc.dtype) if ctx_out else None
    return ux, uc, v_first_x, v_first_c

def hyena_filters(length, p):
    f32 = jnp.float32
    t = jnp.linspace(0.0, 1.0, length, dtype=f32)[:, None]
    bands = (HYENA_EMB - 1) // 2
    freqs = jnp.linspace(1e-4, bands - 1, bands, dtype=f32)[None, :]
    ang = (2.0 * math.pi / length) * jnp.arange(length, dtype=f32)[:, None] * freqs
    z = jnp.concatenate([t, jnp.cos(ang), -jnp.sin(ang)], axis=-1)
    sf = p['sin_freq'].astype(f32)
    hdn = jnp.sin(sf * (z @ p['f_w1'].astype(f32) + p['f_b1'].astype(f32)))
    hdn = jnp.sin(sf * (hdn @ p['f_w2'].astype(f32) + p['f_b2'].astype(f32)))
    hdn = jnp.sin(sf * (hdn @ p['f_w3'].astype(f32) + p['f_b3'].astype(f32)))
    filt = hdn @ p['f_w4'].astype(f32)
    deltas = jnp.abs(jnp.linspace(math.log(HYENA_TARGET) / HYENA_SLOW_DECAY,
                                  math.log(HYENA_TARGET) / HYENA_FAST_DECAY, D_INNER, dtype=f32))
    window = jnp.exp(-t * deltas)
    return filt.reshape(length, 2, D_INNER) * window[:, None, :]

def bidir_long_conv(u, filt, skip):
    length = u.shape[1]
    hf, hb = filt[:, 0], filt[:, 1]
    k = jnp.concatenate([hf[:1] + hb[:1], hf[1:], jnp.zeros_like(hf[:1]), hb[:0:-1]], axis=0)
    n = 2 * length
    uf32 = u.astype(jnp.float32)
    uf = jnp.fft.rfft(uf32, n=n, axis=1)
    kf = jnp.fft.rfft(k, n=n, axis=0)
    y = jnp.fft.irfft(uf * kf[None], n=n, axis=1)[:, :length]
    return (y + uf32 * skip.astype(jnp.float32)).astype(u.dtype)

def centred_dwconv3(u, w, b):
    c = u.shape[-1]
    y = lax.conv_general_dilated(u, w[:, None, :].astype(u.dtype), window_strides=(1,), padding=((1, 1),),
                                 dimension_numbers=('NWC', 'WIO', 'NWC'), feature_group_count=c)
    return y + b

def hyena_sequence(h, p):
    e = D_INNER
    proj = h @ p['w_in']
    s = centred_dwconv3(proj[..., :3 * e], p['conv_w'], p['conv_b'])
    x0, x1, v = s[..., :e], s[..., e:2 * e], s[..., 2 * e:]
    v = bidir_long_conv(v * x1, hyena_filters(h.shape[1], p), p['filter_bias'])
    return v * x0 * jax.nn.silu(proj[..., 3 * e:])

def hyena_mixer(hx, hc, p, ctx_out):
    ux = hyena_sequence(hx, p)
    uc = hyena_sequence(hc, p) if ctx_out else None
    return ux, uc

def hgrn2_prepare(h, p, lb):
    e = D_INNER
    proj = h @ p['w_in']
    q = split_heads(jax.nn.silu(proj[..., :e]), HGRN_HEADS)
    i = split_heads(proj[..., 3 * e:4 * e], HGRN_HEADS)
    gate = proj[..., 4 * e:]
    dirs = []
    for z in range(2):
        f = lb + (1.0 - lb) * jax.nn.sigmoid(proj[..., (1 + z) * e:(2 + z) * e].astype(jnp.float32))
        dirs.append((split_heads(1.0 - f, HGRN_HEADS), split_heads(jnp.log(f), HGRN_HEADS)))
    return q, i, gate, dirs

def gla_chunkwise(q, k, v, log_f, s0):
    b, t, h, _ = q.shape
    dv = v.shape[-1]
    n = t // HGRN_CHUNK

    def chunks(a):
        return a.astype(jnp.float32).reshape(b, n, HGRN_CHUNK, h, a.shape[-1]).transpose(1, 0, 3, 2, 4)

    causal = jnp.asarray(np.tril(np.ones((HGRN_CHUNK, HGRN_CHUNK), dtype=bool)))[:, :, None]

    def step(s, inp):
        qc, kc, vc, gc = inp
        cum = jnp.cumsum(gc, axis=2)
        last = cum[:, :, -1:, :]
        o = jnp.einsum('bhck,bhkv->bhcv', qc * jnp.exp(cum), s)
        rel = jnp.exp(jnp.where(causal, cum[:, :, :, None, :] - cum[:, :, None, :, :], -jnp.inf))
        att = jnp.einsum('bhtk,bhsk,bhtsk->bhts', qc, kc, rel)
        o = o + jnp.einsum('bhts,bhsv->bhtv', att, vc)
        s = jnp.exp(last[:, :, 0, :, None]) * s + jnp.einsum('bhsk,bhsv->bhkv', kc * jnp.exp(last - cum), vc)
        return s, o

    s_last, o = lax.scan(step, s0, (chunks(q), chunks(k), chunks(v), chunks(log_f)))
    return o.transpose(1, 0, 3, 2, 4).reshape(b, t, h, dv), s_last

def gla_direction(q, k, v, log_f, s0, reverse):
    if reverse:
        o, s = gla_chunkwise(jnp.flip(q, 1), jnp.flip(k, 1), jnp.flip(v, 1), jnp.flip(log_f, 1), s0)
        return jnp.flip(o, 1), s
    return gla_chunkwise(q, k, v, log_f, s0)

def hgrn2_readout(o, gate, g_norm, dtype):
    o = o * lax.rsqrt(jnp.mean(o * o, axis=-1, keepdims=True) + NORM_EPS) * g_norm.astype(jnp.float32)
    return (merge_heads(o) * jax.nn.silu(gate.astype(jnp.float32))).astype(dtype)

def hgrn2_mixer(hx, hc, p, lb, ctx_out):
    qx, ix, gx, dirs_x = hgrn2_prepare(hx, p, lb)
    qc, ic, gc, dirs_c = hgrn2_prepare(hc, p, lb)
    s0 = jnp.zeros((hx.shape[0], HGRN_HEADS, HGRN_KEY, HGRN_VAL), jnp.float32)
    ox = oc = 0.0
    for z in range(2):
        oc_z, s_ctx = gla_direction(qc, dirs_c[z][0], ic, dirs_c[z][1], s0, z == 1)
        ox_z, _ = gla_direction(qx, dirs_x[z][0], ix, dirs_x[z][1], s_ctx, z == 1)
        ox = ox + ox_z
        if ctx_out:
            oc = oc + oc_z
    ux = hgrn2_readout(ox, gx, p['g_norm'], hx.dtype)
    uc = hgrn2_readout(oc, gc, p['g_norm'], hc.dtype) if ctx_out else None
    return ux, uc

def first_inputs(seed: int = 0) -> dict:
    key = jax.random.key(seed)
    keys = iter(jax.random.split(key, 96))
    f32 = jnp.float32
    e, d = D_INNER, D_MODEL

    def normal(shape, scale):
        return jax.random.normal(next(keys), shape, f32) * scale

    def near_one(shape):
        return 1.0 + normal(shape, 0.05)

    def rwkv(prefix, vres):
        width = 4 * e + 2 * RWKV_DECAY_LORA + 2 * RWKV_ICLR_LORA + (RWKV_VRES_LORA if vres else 0)
        out = {
            prefix + 'w_in': normal((d, width), d ** -0.5),
            prefix + 'mu': jax.random.uniform(next(keys), (RWKV_N_MU, d), f32),
            prefix + 'w0': jnp.linspace(-6.5, -1.5, e, dtype=f32)[None, :] + normal((2, e), 0.1),
            prefix + 'w2': normal((2, RWKV_DECAY_LORA, e), 0.1),
            prefix + 'a0': normal((2, e), 0.1),
            prefix + 'a2': normal((2, RWKV_ICLR_LORA, e), 0.1),
            prefix + 'k_k': 0.85 + normal((e,), 0.05),
            prefix + 'k_a': near_one((e,)),
            prefix + 'r_k': normal((RWKV_HEADS, RWKV_HEAD), 0.1),
            prefix + 'ln_w': near_one((e,)),
            prefix + 'ln_b': normal((e,), 0.02),
        }
        if vres:
            out[prefix + 'v0'] = near_one((e,))
            out[prefix + 'v2'] = normal((RWKV_VRES_LORA, e), 0.1)
        return out

    inputs = {
        'x': normal((BATCH, SEQ, d), 1.0),
        'c': normal((BATCH, d), 1.0),
        'ctx': normal((BATCH, CTX_LEN, d), 1.0),
        'c_ctx': normal((d,), 1.0),
        'ada_w': normal((DEPTH, d, 3 * d), 0.5 * d ** -0.5),
        'ada_b': normal((DEPTH, 3 * d), 0.02),
        'norm_pre': near_one((DEPTH, d)),
        'norm_post': near_one((DEPTH, d)),
        'w_out': normal((DEPTH, e, d), e ** -0.5),
    }
    inputs.update(rwkv('l0_', False))
    inputs.update({
        'l1_w_in': normal((d, 4 * e), d ** -0.5),
        'l1_conv_w': normal((3, 3 * e), 3 ** -0.5),
        'l1_conv_b': normal((3 * e,), 0.02),
        'l1_f_w1': normal((HYENA_EMB, HYENA_FILTER_WIDTH), HYENA_EMB ** -0.5),
        'l1_f_b1': normal((HYENA_FILTER_WIDTH,), 0.1),
        'l1_f_w2': normal((HYENA_FILTER_WIDTH, HYENA_FILTER_WIDTH), HYENA_FILTER_WIDTH ** -0.5),
        'l1_f_b2': normal((HYENA_FILTER_WIDTH,), 0.1),
        'l1_f_w3': normal((HYENA_FILTER_WIDTH, HYENA_FILTER_WIDTH), HYENA_FILTER_WIDTH ** -0.5),
        'l1_f_b3': normal((HYENA_FILTER_WIDTH,), 0.1),
        'l1_f_w4': normal((HYENA_FILTER_WIDTH, 2 * e), HYENA_FILTER_WIDTH ** -0.5),
        'l1_sin_freq': HYENA_SIN_W * near_one((HYENA_FILTER_WIDTH,)),
        'l1_filter_bias': normal((e,), 1.0),
    })
    inputs.update({
        'l2_w_in': normal((d, 5 * e), d ** -0.5),
        'l2_g_norm': near_one((HGRN_VAL,)),
        'hgrn_lb_logits': normal((DEPTH, e), 1.0),
    })
    inputs.update(rwkv('l3_', True))
    return inputs

def first_block(x, c, ctx, c_ctx, ada_w, ada_b, norm_pre, norm_post, w_out,
              l0_w_in, l0_mu, l0_w0, l0_w2, l0_a0, l0_a2, l0_k_k, l0_k_a, l0_r_k, l0_ln_w, l0_ln_b,
              l1_w_in, l1_conv_w, l1_conv_b, l1_f_w1, l1_f_b1, l1_f_w2, l1_f_b2, l1_f_w3, l1_f_b3,
              l1_f_w4, l1_sin_freq, l1_filter_bias,
              l2_w_in, l2_g_norm, hgrn_lb_logits,
              l3_w_in, l3_mu, l3_w0, l3_w2, l3_a0, l3_a2, l3_k_k, l3_k_a, l3_r_k, l3_ln_w, l3_ln_b,
              l3_v0, l3_v2):
    rwkv0 = dict(w_in=l0_w_in, mu=l0_mu, w0=l0_w0, w2=l0_w2, a0=l0_a0, a2=l0_a2, k_k=l0_k_k,
                 k_a=l0_k_a, r_k=l0_r_k, ln_w=l0_ln_w, ln_b=l0_ln_b)
    hyena1 = dict(w_in=l1_w_in, conv_w=l1_conv_w, conv_b=l1_conv_b, f_w1=l1_f_w1, f_b1=l1_f_b1,
                  f_w2=l1_f_w2, f_b2=l1_f_b2, f_w3=l1_f_w3, f_b3=l1_f_b3, f_w4=l1_f_w4,
                  sin_freq=l1_sin_freq, filter_bias=l1_filter_bias)
    hgrn2 = dict(w_in=l2_w_in, g_norm=l2_g_norm)
    rwkv3 = dict(w_in=l3_w_in, mu=l3_mu, w0=l3_w0, w2=l3_w2, a0=l3_a0, a2=l3_a2, k_k=l3_k_k,
                 k_a=l3_k_a, r_k=l3_r_k, ln_w=l3_ln_w, ln_b=l3_ln_b, v0=l3_v0, v2=l3_v2)
    layer_params = [rwkv0, hyena1, hgrn2, rwkv3]

    lb_soft = jax.nn.softmax(hgrn_lb_logits.astype(jnp.float32), axis=0)
    lower_bounds = jnp.cumsum(lb_soft, axis=0) - lb_soft[0]

    v_first_x = None
    v_first_c = None
    for l in range(DEPTH):
        kind = l % N_MIXERS
        p = layer_params[l]
        ctx_out = l < DEPTH - 1
        sh_x, sc_x, gt_x = adaln(c[:, None, :], ada_w[l], ada_b[l])
        sh_c, sc_c, gt_c = adaln(c_ctx[None, None, :], ada_w[l], ada_b[l])
        hx = rms_norm(x, norm_pre[l]) * (1.0 + sc_x) + sh_x
        hc = rms_norm(ctx, norm_pre[l]) * (1.0 + sc_c) + sh_c
        if kind == 0:
            ux, uc, v_first_x, v_first_c = rwkv7_mixer(hx, hc, p, v_first_x, v_first_c, ctx_out)
        elif kind == 1:
            ux, uc = hyena_mixer(hx, hc, p, ctx_out)
        else:
            ux, uc = hgrn2_mixer(hx, hc, p, lower_bounds[l], ctx_out)
        x = x + rms_norm(ux @ w_out[l], norm_post[l]) * gt_x
        if ctx_out:
            ctx = ctx + rms_norm(uc @ w_out[l], norm_post[l]) * gt_c
    return x


D_MIX = D_MODEL
CHUNK = 128
A_GROUPS = 4
A_WIDTH = D_MIX // 4
A_HEAD = A_WIDTH // A_GROUPS
B_GROUPS = 4
B_WIDTH = D_MIX // 4
CONV_W = 3
C_HEADS = 4
C_WIDTH = D_MIX // 2
C_HEAD = C_WIDTH // C_HEADS
ROPE_BASE = 10000.0
D_PROJ = 2 * A_WIDTH + 3 * B_WIDTH + 4 * C_WIDTH
D_FF = 2816
MACARON = 0.5
EPS = 1e-6


def _rmsnorm(x, g):
    xf = x.astype(jnp.float32)
    y = xf * lax.rsqrt(jnp.mean(xf * xf, axis=-1, keepdims=True) + EPS)
    return (y * g.astype(jnp.float32)).astype(x.dtype)

def _group_layernorm(x, g, groups):
    shp = x.shape
    xf = x.astype(jnp.float32).reshape(shp[:-1] + (groups, shp[-1] // groups))
    mu = jnp.mean(xf, axis=-1, keepdims=True)
    var = jnp.mean(jnp.square(xf - mu), axis=-1, keepdims=True)
    y = ((xf - mu) * lax.rsqrt(var + EPS)).reshape(shp)
    return (y * g.astype(jnp.float32)).astype(x.dtype)

def _swiglu(x, w_gate, w_up, w_down):
    return (jax.nn.silu(x @ w_gate) * (x @ w_up)) @ w_down

def _gmlp_mixer(p, v_norm, w_s, b_s):
    bsz, s, _ = p.shape
    nc = s // CHUNK
    z = jax.nn.gelu(p)
    u, v = z[..., :A_WIDTH], z[..., A_WIDTH:]
    v = _group_layernorm(v, v_norm, A_GROUPS)
    v = v.reshape(bsz, nc, CHUNK, A_GROUPS, A_HEAD)
    causal = jnp.tril(jnp.ones((CHUNK, CHUNK), dtype=w_s.dtype))
    ws = w_s * causal[None]
    sv = jnp.einsum('gts,bnsgd->bntgd', ws, v) + b_s.T[None, None, :, :, None]
    return u * sv.reshape(bsz, s, A_WIDTH)

def _shortconv_mixer(p, conv_w):
    s = p.shape[1]
    bg, cg, xin = p[..., :B_WIDTH], p[..., B_WIDTH:2 * B_WIDTH], p[..., 2 * B_WIDTH:]
    z = cg * xin
    zp = jnp.pad(z, ((0, 0), (CONV_W - 1, 0), (0, 0)))
    y = sum(zp[:, i:i + s, :] * conv_w[i] for i in range(CONV_W))
    return bg * y

def _rotary(x, pos):
    half = x.shape[-1] // 2
    inv = ROPE_BASE ** (-jnp.arange(half, dtype=jnp.float32) / half)
    ang = pos[:, None] * inv[None, :]
    cos = jnp.cos(ang)[None, :, None, :]
    sin = jnp.sin(ang)[None, :, None, :]
    x1, x2 = x[..., :half], x[..., half:]
    return jnp.concatenate([x1 * cos - x2 * sin, x2 * cos + x1 * sin], axis=-1)

def _retention_mixer(p, gn):
    dtype = p.dtype
    bsz, s, _ = p.shape
    nc = s // CHUNK
    pf = p.astype(jnp.float32)
    q = pf[..., 0 * C_WIDTH:1 * C_WIDTH].reshape(bsz, s, C_HEADS, C_HEAD)
    k = pf[..., 1 * C_WIDTH:2 * C_WIDTH].reshape(bsz, s, C_HEADS, C_HEAD)
    v = pf[..., 2 * C_WIDTH:3 * C_WIDTH].reshape(bsz, s, C_HEADS, C_HEAD)
    g = p[..., 3 * C_WIDTH:]
    pos = jnp.arange(s, dtype=jnp.float32)
    q = _rotary(q, pos)
    k = _rotary(k, pos) * (C_HEAD ** -0.5)

    log_g = jnp.log1p(-jnp.exp2(-5.0 - jnp.arange(C_HEADS, dtype=jnp.float32)))
    idx = jnp.arange(CHUNK, dtype=jnp.float32)
    diff = idx[:, None] - idx[None, :]
    decay = jnp.where(diff[None] >= 0,
                      jnp.exp(log_g[:, None, None] * jnp.maximum(diff, 0.0)[None]), 0.0)
    zeta = jnp.exp(log_g[None, :] * (CHUNK - 1 - idx)[:, None])
    xi = jnp.exp(log_g[None, :] * (idx + 1.0)[:, None])
    gamma_chunk = jnp.exp(log_g * CHUNK)

    qc = q.reshape(bsz, nc, CHUNK, C_HEADS, C_HEAD)
    kc = k.reshape(bsz, nc, CHUNK, C_HEADS, C_HEAD)
    vc = v.reshape(bsz, nc, CHUNK, C_HEADS, C_HEAD)

    scores = jnp.einsum('bnthd,bnshd->bnhts', qc, kc) * decay[None, None]
    inner = jnp.einsum('bnhts,bnshv->bnthv', scores, vc)

    chunk_kv = jnp.einsum('bnshd,sh,bnshv->bnhdv', kc, zeta, vc)

    def step(state, kv):
        return state * gamma_chunk[None, :, None, None] + kv, state

    init = jnp.zeros((bsz, C_HEADS, C_HEAD, C_HEAD), jnp.float32)
    _, prev = lax.scan(step, init, jnp.moveaxis(chunk_kv, 1, 0))
    cross = jnp.einsum('bnthd,nbhdv,th->bnthv', qc, prev, xi)

    ret = (inner + cross).reshape(bsz, s, C_WIDTH)
    ret = _group_layernorm(ret, gn, C_HEADS).astype(dtype)
    return jax.nn.silu(g) * ret

def _layer(x, ffn1_norm, ffn1_w_gate, ffn1_w_up, ffn1_w_down, mix_norm, w_in,
           gmlp_v_norm, gmlp_w_s, gmlp_b_s, conv_w, ret_gn, w_out,
           ffn2_norm, ffn2_w_gate, ffn2_w_up, ffn2_w_down):
    x = x + MACARON * _swiglu(_rmsnorm(x, ffn1_norm), ffn1_w_gate, ffn1_w_up, ffn1_w_down)
    h = _rmsnorm(x, mix_norm)
    p = h @ w_in
    a_end = 2 * A_WIDTH
    b_end = a_end + 3 * B_WIDTH
    y_a = _gmlp_mixer(p[..., :a_end], gmlp_v_norm, gmlp_w_s, gmlp_b_s)
    y_b = _shortconv_mixer(p[..., a_end:b_end], conv_w)
    y_c = _retention_mixer(p[..., b_end:], ret_gn)
    x = x + jnp.concatenate([y_a, y_b, y_c], axis=-1) @ w_out
    x = x + MACARON * _swiglu(_rmsnorm(x, ffn2_norm), ffn2_w_gate, ffn2_w_up, ffn2_w_down)
    return x

def second_inputs(seed: int = 0) -> dict:
    key = jax.random.key(seed)
    ks = jax.random.split(key, 18)
    f32 = jnp.float32

    def w(k, shape, fan_in):
        return jax.random.normal(k, shape, f32) * (fan_in ** -0.5)

    def gain(k, shape):
        return 1.0 + 0.1 * jax.random.normal(k, shape, f32)

    return {
        "x": jax.random.normal(ks[0], (BATCH, SEQ, D_MODEL), f32),
        "ffn1_norm": gain(ks[1], (DEPTH, D_MODEL)),
        "ffn1_w_gate": w(ks[2], (DEPTH, D_MODEL, D_FF), D_MODEL),
        "ffn1_w_up": w(ks[3], (DEPTH, D_MODEL, D_FF), D_MODEL),
        "ffn1_w_down": w(ks[4], (DEPTH, D_FF, D_MODEL), D_FF),
        "mix_norm": gain(ks[5], (DEPTH, D_MODEL)),
        "w_in": w(ks[6], (DEPTH, D_MODEL, D_PROJ), D_MODEL),
        "gmlp_v_norm": gain(ks[7], (DEPTH, A_WIDTH)),
        "gmlp_w_s": w(ks[8], (DEPTH, A_GROUPS, CHUNK, CHUNK), CHUNK),
        "gmlp_b_s": 1.0 + 0.1 * jax.random.normal(ks[9], (DEPTH, A_GROUPS, CHUNK), f32),
        "conv_w": w(ks[10], (DEPTH, CONV_W, B_WIDTH), CONV_W),
        "ret_gn": gain(ks[11], (DEPTH, C_WIDTH)),
        "w_out": w(ks[12], (DEPTH, D_MIX, D_MODEL), D_MIX),
        "ffn2_norm": gain(ks[13], (DEPTH, D_MODEL)),
        "ffn2_w_gate": w(ks[14], (DEPTH, D_MODEL, D_FF), D_MODEL),
        "ffn2_w_up": w(ks[15], (DEPTH, D_MODEL, D_FF), D_MODEL),
        "ffn2_w_down": w(ks[16], (DEPTH, D_FF, D_MODEL), D_FF),
        "final_norm": gain(ks[17], (D_MODEL,)),
    }

def second_block(x, ffn1_norm, ffn1_w_gate, ffn1_w_up, ffn1_w_down, mix_norm, w_in,
              gmlp_v_norm, gmlp_w_s, gmlp_b_s, conv_w, ret_gn, w_out,
              ffn2_norm, ffn2_w_gate, ffn2_w_up, ffn2_w_down, final_norm):
    for l in range(DEPTH):
        x = _layer(x, ffn1_norm[l], ffn1_w_gate[l], ffn1_w_up[l], ffn1_w_down[l],
                   mix_norm[l], w_in[l], gmlp_v_norm[l], gmlp_w_s[l], gmlp_b_s[l],
                   conv_w[l], ret_gn[l], w_out[l],
                   ffn2_norm[l], ffn2_w_gate[l], ffn2_w_up[l], ffn2_w_down[l])
    return _rmsnorm(x, final_norm)


def setup_inputs(seed=0):
    out = dict(first_inputs(seed))
    for name, value in second_inputs(seed + 1).items():
        if name != "x":
            out[name + "_2"] = value
    return out


def reference(
    x, c, ctx, c_ctx, ada_w, ada_b, norm_pre, norm_post, w_out, l0_w_in, l0_mu, l0_w0, l0_w2,
    l0_a0, l0_a2, l0_k_k, l0_k_a, l0_r_k, l0_ln_w, l0_ln_b, l1_w_in, l1_conv_w, l1_conv_b,
    l1_f_w1, l1_f_b1, l1_f_w2, l1_f_b2, l1_f_w3, l1_f_b3, l1_f_w4, l1_sin_freq, l1_filter_bias,
    l2_w_in, l2_g_norm, hgrn_lb_logits, l3_w_in, l3_mu, l3_w0, l3_w2, l3_a0, l3_a2, l3_k_k,
    l3_k_a, l3_r_k, l3_ln_w, l3_ln_b, l3_v0, l3_v2, ffn1_norm_2, ffn1_w_gate_2, ffn1_w_up_2,
    ffn1_w_down_2, mix_norm_2, w_in_2, gmlp_v_norm_2, gmlp_w_s_2, gmlp_b_s_2, conv_w_2,
    ret_gn_2, w_out_2, ffn2_norm_2, ffn2_w_gate_2, ffn2_w_up_2, ffn2_w_down_2, final_norm_2,
):
    x = first_block(
        x, c, ctx, c_ctx, ada_w, ada_b, norm_pre, norm_post, w_out, l0_w_in, l0_mu, l0_w0,
        l0_w2, l0_a0, l0_a2, l0_k_k, l0_k_a, l0_r_k, l0_ln_w, l0_ln_b, l1_w_in, l1_conv_w,
        l1_conv_b, l1_f_w1, l1_f_b1, l1_f_w2, l1_f_b2, l1_f_w3, l1_f_b3, l1_f_w4, l1_sin_freq,
        l1_filter_bias, l2_w_in, l2_g_norm, hgrn_lb_logits, l3_w_in, l3_mu, l3_w0, l3_w2, l3_a0,
        l3_a2, l3_k_k, l3_k_a, l3_r_k, l3_ln_w, l3_ln_b, l3_v0, l3_v2,
    )
    return second_block(
        x, ffn1_norm_2, ffn1_w_gate_2, ffn1_w_up_2, ffn1_w_down_2, mix_norm_2, w_in_2,
        gmlp_v_norm_2, gmlp_w_s_2, gmlp_b_s_2, conv_w_2, ret_gn_2, w_out_2, ffn2_norm_2,
        ffn2_w_gate_2, ffn2_w_up_2, ffn2_w_down_2, final_norm_2,
    )


_drawn_inputs = setup_inputs


def setup_inputs(seed=0):
    import zlib

    import numpy as np

    out = dict(_drawn_inputs(seed))
    spreads = {}
    factors = {'l0_a0': 3.077, 'l0_ln_b': 6.067}
    for name, (base, spread) in spreads.items():
        noise = np.random.default_rng([zlib.crc32(name.encode()), seed]).standard_normal(out[name].shape)
        drawn = base * np.exp(spread * noise) if base else spread * noise
        out[name] = jnp.asarray(drawn.astype(out[name].dtype))
    for name, factor in factors.items():
        out[name] = (out[name] * factor).astype(out[name].dtype)
    return out
```

```python
from contextlib import ExitStack

import numpy as np

import concourse.bass as bass
from concourse import mybir

ALU = mybir.AluOpType
ACT = mybir.ActivationFunctionType
AX = mybir.AxisListType
F32 = mybir.dt.float32

P = 128
D = 1024
KT = D // P
S = 256
NT = S // P
E = 2 * D
ET = E // P
HEAD = 64
LORA = 64
FF = 2816
FT = FF // P
WIDE = 512
EPS = 1e-6
GN_EPS = 64e-5
CH = 64
AW = 256
CW = 512
CHEADS = 4
PROJ = 2 * AW + 3 * AW + 4 * CW
EMB, HW = 33, 64
SLOTS = 4
SMALL = 16 * 14


class Phase:

    def __init__(self, nc, pool):
        self.nc, self.pool, self.used = nc, pool, {}
        self.stack = ExitStack()

    def __enter__(self):
        self.block = self.stack.enter_context(self.nc.Block())
        return self

    def __getitem__(self, name):
        if name not in self.used:
            self.used[name] = self.pool[len(self.used)]
        return self.used[name]

    def __exit__(self, *exc):
        self.stack.__exit__(*exc)
        if exc[0] is None:
            if self.used:
                self.nc.sync.sem_clear(range(self.pool[0].num, self.pool[len(self.used) - 1].num + 1))
            self.nc.all_engine_barrier()
        return False


class Ring:

    def __init__(self, ph, buf):
        self.ph, self.buf, self.pieces = ph, buf, []
        self.counts = [0] * SLOTS

    def load(self, sp, parts, free):
        i = len(self.pieces)
        slot = i % SLOTS
        if i >= SLOTS:
            sp.wait_ge(*free)
        for dst, src in parts(self.buf[:, slot, :]):
            sp.dma_start(dst, src).then_inc(self.ph[f"panel_landed_{slot}"], 16)
            self.counts[slot] += 16
        self.pieces.append(self.counts[slot])

    def wait(self, pe, i):
        pe.wait_ge(self.ph[f"panel_landed_{i % SLOTS}"], self.pieces[i])
        return self.buf[:, i % SLOTS, :]


def chan(v):
    return v.rearrange("(k p) -> p k", p=P)


class Program:
    def __init__(self, nc, ctx, a, out):
        self.nc, self.a, self.out, self.n = nc, a, out, 0

        def sb(name, *shape):
            return ctx.enter_context(nc.sbuf_tensor(name, [P, *shape], F32))

        self.sems = [ctx.enter_context(nc.semaphore(f"s{i}")) for i in range(90)]
        self.psum = ctx.enter_context(nc.psum_tensor("psum", [P, 8, WIDE], F32))
        self.ring = sb("ring", SLOTS, KT * WIDE)
        self.x = sb("x", NT, D)
        self.xn = sb("xn", NT, D)
        self.hT = sb("hT", KT, 2 * S)
        self.ident = sb("ident", P)
        self.half = sb("half", 16)
        self.ss = sb("ss", 8)
        self.ms = sb("ms", 8)
        self.rstd = sb("rstd", 8)
        self.gain = sb("gain", KT)
        self.cond = sb("cond", KT, 2)
        self.shift, self.scale = sb("shift", 2, KT), sb("scale", 2, KT)
        self.post = sb("post", D)
        self.ones = sb("ones", P)

    def phase(self):
        return Phase(self.nc, self.sems)

    def scratch(self, ctx):
        def sb(*shape):
            self.n += 1
            return ctx.enter_context(self.nc.sbuf_tensor(f"scratch{self.n}", [P, *shape], F32))
        return sb

    def load_start(self):
        nc = self.nc
        with self.phase() as ph:
            @ph.block.sync
            def _(sp):
                sp.dma_start(self.x[:, :, :], self.a["x"][0].rearrange("(t p) d -> p t d", p=P)).then_inc(ph["start"], 16)
                sp.dma_start(self.ident[:, :], self.a["k_ident"]).then_inc(ph["start"], 16)
                sp.wait_ge(ph["start"], 32)

            @ph.block.vector
            def _(dve):
                dve.memset(self.half[:, :], -0.5).then_inc(ph["constants_set"], 1)
                dve.memset(self.ones[:, :], 1.0).then_inc(ph["constants_set"], 1)
                dve.wait_ge(ph["constants_set"], 2)

            @ph.block.scalar
            def _(act):
                with nc.allow_non_contiguous_dma(reason="the two condition vectors, once"):
                    act.dma_start(self.cond[:, :, 0], chan(self.a["c"][0])).then_inc(ph["cond_in"], 16)
                    act.dma_start(self.cond[:, :, 1], chan(self.a["c_ctx"])).then_inc(ph["cond_in"], 16)
                act.wait_ge(ph["cond_in"], 32)
                act.activation(self.cond[:, :, :], self.cond[:, :, :], ACT.Silu).then_inc(ph["cond_ready"], 1)

    def norm_dve_stats(self, ph, dve, x, n=NT):
        for t in range(n):
            dve.tensor_tensor_reduce(out=self.xn[:, t, :], in0=x[:, t, :], in1=x[:, t, :], scale=1.0, scalar=0.0,
                                     op0=ALU.mult, op1=ALU.add, accum_out=self.ss[:, t:t + 1]).then_inc(ph["squares"], 1)
        dve.wait_ge(ph["squares"], n)
        dve.tensor_scalar(self.ms[:, 0:n], self.ss[:, 0:n], 1.0 / D, EPS, ALU.mult, ALU.add).then_inc(ph["mean_square"], 1)

    def norm_pool(self, ph, pool, n=NT):
        pool.wait_ge(ph["mean_square"], 1)
        pool.tensor_tensor(self.rstd[:, 0:n], self.ms[:, 0:n], self.half[:, 0:n], ALU.pow).then_inc(ph["rstd_ready"], 1)

    def norm_dve_scale(self, ph, dve, x, n=NT):
        dve.wait_ge(ph["rstd_ready"], 1)
        for t in range(n):
            dve.tensor_scalar(self.xn[:, t, :], x[:, t, :], self.rstd[:, t:t + 1], None, ALU.mult).then_inc(ph["xn_ready"], 1)

    def norm_pe(self, ph, pe, bank=4):
        pe.wait_ge(ph["xn_ready"], NT)
        for k in range(KT):
            for t in range(NT):
                mm = pe.transpose(self.psum[:, bank + k // 2, (k % 2) * S + t * P:(k % 2) * S + (t + 1) * P],
                                  self.xn[:, t, k * P:(k + 1) * P], self.ident[:, :])
            mm.then_inc(ph["turned"], 1)

    def norm_act(self, ph, act, scale, bias=None, bank=4, at=0):
        for k in range(KT):
            if k // 2 % 2 == 0:
                act.wait_ge(ph["turned"], (k // 2 + 1) * 2)
                act.activation(self.hT[:, k, at:at + S], self.psum[:, bank + k // 2, k % 2 * S:(k % 2 + 1) * S], ACT.Identity,
                               scale=scale[:, k:k + 1], bias=bias[:, k:k + 1] if bias is not None else 0.0).then_inc(ph["h_even"], 1)

    def norm_dve_turn(self, ph, dve, scale, bias=None, bank=4, at=0):
        for k in range(KT):
            if k // 2 % 2 == 1:
                dve.wait_ge(ph["turned"], (k // 2 + 1) * 2)
                src = self.psum[:, bank + k // 2, k % 2 * S:(k % 2 + 1) * S]
                if bias is None:
                    ins = dve.tensor_scalar(self.hT[:, k, at:at + S], src, scale[:, k:k + 1], None, ALU.mult)
                else:
                    ins = dve.tensor_scalar(self.hT[:, k, at:at + S], src, scale[:, k:k + 1], bias[:, k:k + 1], ALU.mult, ALU.add)
                ins.then_inc(ph["h_odd"], 1)

    def norm_wait(self, ph, eng):
        eng.wait_ge(ph["h_even"], KT // 2)
        eng.wait_ge(ph["h_odd"], KT // 2)

    def mixer(self, l):
        a, psum, hT, ident = self.a, self.psum, self.hT, self.ident
        kp = "a (k p) n -> p (a k) n"
        order = [1280, 1792, 2304, 2816, 0, 512, 1024]
        width = [WIDE] * 6 + [AW]
        with ExitStack() as ctx:
            sb = self.scratch(ctx)
            rope = sb(2, 2, NT, P)
            gain_c, gain_a = sb(CW), sb(AW)
            decay, xi, zeta = sb(CHEADS, P), sb(CHEADS, P), sb(CHEADS)
            causal, w_s, wsT, b_s = sb(P), sb(4, P), sb(4, P), sb(2, P)
            conv = sb(2, 3)
            m1, m2 = sb(CW), sb(CW)
            qk = sb(2, NT, CW)
            qkT = sb(2, CHEADS, S)
            qx = sb(CHEADS, P)
            kz, kv = sb(CW), sb(CW)
            v, sg = sb(NT, CW), sb(NT, CW)
            pT = sb(NT, CHEADS, P)
            bn, mv = sb(16, 6), sb(16, 2)
            var, rs = sb(16), sb(16)
            ret = sb(NT, CW)
            uT, va = sb(2, S), sb(NT, AW)
            bcx = sb(6, S)
            z, yb = sb(2, S + 2), sb(2, S)
            yT = sb(KT, S)
            with self.phase() as ph:
                ring = Ring(ph, self.ring)

                @ph.block.sync
                def _(sp):
                    for i, (c, w) in enumerate(zip(order, width)):
                        def parts(slot):
                            yield (slot.rearrange("p (k n) -> p k n", n=WIDE)[:, :, 0:w],
                                   a["w_in_2"][bass.ds(l, 1)].rearrange(kp, p=P)[:, :, c:c + w])
                        ring.load(sp, parts, (ph["proj_ready"], [2, 4, 6, 8][i - SLOTS] if i >= SLOTS else 0))
                    for i in range(2):
                        def parts(slot):
                            yield (slot.rearrange("p (k n) -> p k n", n=D),
                                   a["w_out_2"][bass.ds(l, 1)].rearrange(kp, p=P)[:, 4 * i:4 * i + 4, :])
                        ring.load(sp, parts, (ph["proj_ready"], [8, 12][i]))

                @ph.block.scalar
                def _(act):
                    with self.nc.allow_non_contiguous_dma(reason="small vectors"):
                        act.dma_start(self.gain[:, :], a["mix_norm_2"][bass.ds(l, 1)].rearrange("a (k p) -> p (a k)", p=P)).then_inc(ph["gain_in"], 16)
                        loads = [(conv[:, c, :], a["conv_w_2"][bass.ds(l, 1), :, c * P:(c + 1) * P].rearrange("a i p -> p (a i)")) for c in range(2)]
                        loads += [
                            (rope[:, :, :, :, :], a["k_rope"]),
                            (decay[:, :, :], a["k_decay"]), (xi[:, :, :], a["k_xi"]), (zeta[:, :], a["k_zeta"]), (causal[:, :], a["k_causal"]),
                            (w_s[:, :, :], a["gmlp_w_s_2"][bass.ds(l, 1)].rearrange("a g t s -> t (a g) s")),
                            (gain_c[:, :], a["ret_gn_2"][bass.ds(l, 1)].partition_broadcast(P).rearrange("p a n -> p (a n)")),
                            (gain_a[:, :], a["gmlp_v_norm_2"][bass.ds(l, 1)].partition_broadcast(P).rearrange("p a n -> p (a n)"))]
                        for g in range(4):
                            loads.append((b_s[HEAD * (g % 2):HEAD * (g % 2) + HEAD, g // 2, :],
                                          a["gmlp_b_s_2"][bass.ds(l, 1), g, :].partition_broadcast(HEAD).rearrange("p a n -> p (a n)")))
                        for dst, src in loads:
                            act.dma_start(dst, src).then_inc(ph["small_in"], 16)
                    small = 16 * len(loads)
                    assert small == SMALL
                    act.wait_ge(ph["gain_in"], 16)
                    self.norm_act(ph, act, self.gain)
                    for t in range(NT):
                        act.wait_ge(ph["proj_ready"], 5 + t)
                        act.activation(v[:, t, :], psum[:, t, :], ACT.Copy).then_inc(ph["v_ready"], 1)
                    for t in range(NT):
                        act.wait_ge(ph["proj_ready"], 7 + t)
                        act.activation(sg[:, t, :], psum[:, 2 + t, :], ACT.Silu).then_inc(ph["gate_ready"], 1)
                    act.wait_ge(ph["proj_ready"], 9)
                    act.activation(uT[:, :, :], psum[:, 0, :].rearrange("p (c s) -> p c s", c=2), ACT.Gelu_apprx_tanh).then_inc(ph["u_ready"], 1)
                    act.wait_ge(ph["proj_ready"], 10)
                    act.activation(va[:, :, :], psum[:, 1, :].rearrange("p (t n) -> p t n", t=NT), ACT.Gelu_apprx_tanh).then_inc(ph["va_ready"], 1)
                    for i in range(3):
                        act.wait_ge(ph["proj_ready"], 11 + i)
                        act.activation(bcx[:, 2 * i:2 * i + 2, :], psum[:, [2, 3, 0][i], :].rearrange("p (c s) -> p c s", c=2), ACT.Copy).then_inc(ph["bcx_ready"], 1)

                @ph.block.gpsimd
                def _(pool):
                    self.norm_pool(ph, pool)
                    pool.memset(z[:, :, 0:2], 0.0).then_inc(ph["z_edge"], 1)
                    pool.wait_ge(ph["small_in"], SMALL)
                    for n, (var_in, out_sem, cnt) in enumerate(((ph["var_a"], ph["rs_a"], 8), (ph["var_c"], ph["rs_c"], 8))):
                        pool.wait_ge(var_in, 1)
                        pool.tensor_tensor(rs[:, 8 * n:8 * n + 8], var[:, 8 * n:8 * n + 8], self.half[:, 0:8], ALU.pow).then_inc(out_sem, 1)

                @ph.block.vector
                def _(dve):
                    self.norm_dve_stats(ph, dve, self.x)
                    self.norm_dve_scale(ph, dve, self.x)
                    dve.wait_ge(ph["gain_in"], 16)
                    self.norm_dve_turn(ph, dve, self.gain)
                    dve.wait_ge(ph["small_in"], SMALL)
                    dve.wait_ge(ph["ws_turned"], 1)
                    dve.tensor_tensor(wsT[:, :, :], psum[:, 7, :].rearrange("p (g t) -> p g t", g=4),
                                      causal[:, :].unsqueeze(1).to_broadcast([P, 4, P]), ALU.mult).then_inc(ph["ws_ready"], 1)
                    for i in range(2):
                        for t in range(NT):
                            n = 2 * i + t
                            dve.wait_ge(ph["proj_ready"], n + 1)
                            src = psum[:, n, :].rearrange("p (h d) -> p h d", h=CHEADS)
                            m1v, m2v = (m[:, :].rearrange("p (h d) -> p h d", h=CHEADS) for m in (m1, m2))
                            if n:
                                dve.wait_ge(ph["rotated"], n)
                            dve.tensor_tensor(m1v, src, rope[:, i, 0, t, :].unsqueeze(1).to_broadcast([P, CHEADS, P]), ALU.mult).then_inc(ph["rope_parts"], 1)
                            for o in (0, HEAD):
                                dve.tensor_tensor(m2v[:, :, o:o + HEAD], src[:, :, HEAD - o:P - o],
                                                  rope[:, i, 1, t, o:o + HEAD].unsqueeze(1).to_broadcast([P, CHEADS, HEAD]), ALU.mult).then_inc(ph["rope_parts"], 1)
                            dve.wait_ge(ph["rope_parts"], 3 * (n + 1))
                            dve.tensor_tensor(qk[:, i, t, :], m1[:, :], m2[:, :], ALU.add).then_inc(ph["rotated"], 1)
                    dve.wait_ge(ph["rotated"], 4)
                    dve.tensor_tensor(kz[:, :].rearrange("p (h d) -> p h d", h=CHEADS), qk[:, 1, 0, :].rearrange("p (h d) -> p h d", h=CHEADS),
                                      zeta[:, :].unsqueeze(2).to_broadcast([P, CHEADS, P]), ALU.mult).then_inc(ph["kz_ready"], 1)
                    for i in range(2):
                        for t in range(NT):
                            n = 2 * i + t
                            dve.wait_ge(ph["qk_turned"], n + 1)
                            dve.tensor_copy(qkT[:, i, :, t * P:(t + 1) * P], psum[:, 4 + n, :].rearrange("p (h s) -> p h s", h=CHEADS)).then_inc(ph["qkT_ready"], 1)
                    dve.wait_ge(ph["qkT_ready"], 4)
                    dve.tensor_tensor(qx[:, :, :], qkT[:, 0, :, P:S], xi[:, :, :], ALU.mult).then_inc(ph["qx_ready"], 1)
                    dve.wait_ge(ph["va_ready"], 1)
                    vg = va[:, :, :].rearrange("p t (g d) -> p (t g) d", g=4)
                    self.group_stats(ph, dve, [vg[:, j, :] for j in range(8)], bn, mv, var, 0, ph["var_a"])
                    dve.wait_ge(ph["rs_a"], 1)
                    for j in range(8):
                        dve.tensor_scalar(vg[:, j, :], vg[:, j, :], mv[:, j, 0:1], rs[:, j:j + 1], ALU.subtract, ALU.mult).then_inc(ph["va_scaled"], 1)
                    dve.wait_ge(ph["va_scaled"], 8)
                    dve.tensor_tensor(va[:, :, :], va[:, :, :], gain_a[:, :].unsqueeze(1).to_broadcast([P, NT, AW]), ALU.mult).then_inc(ph["va_normed"], 1)
                    dve.wait_ge(ph["bcx_ready"], 3)
                    dve.wait_ge(ph["z_edge"], 1)
                    dve.tensor_tensor(z[:, :, 2:S + 2], bcx[:, 2:4, :], bcx[:, 4:6, :], ALU.mult).then_inc(ph["z_ready"], 1)
                    dve.wait_ge(ph["z_ready"], 1)
                    for c in range(2):
                        dve.tensor_scalar(yb[:, c, :], z[:, c, 0:S], conv[:, c, 0:1], None, ALU.mult).then_inc(ph["taps"], 1)
                    for i in range(1, 3):
                        for c in range(2):
                            dve.wait_ge(ph["taps"], 2 * i + c - 1)
                            dve.scalar_tensor_tensor(out=yb[:, c, :], in0=z[:, c, i:i + S], scalar=conv[:, c, i:i + 1], in1=yb[:, c, :],
                                                     op0=ALU.mult, op1=ALU.add).then_inc(ph["taps"], 1)
                    dve.wait_ge(ph["taps"], 6)
                    dve.tensor_tensor(yT[:, 2:4, :], yb[:, :, :], bcx[:, 0:2, :], ALU.mult).then_inc(ph["yb_ready"], 1)
                    for t in range(NT):
                        dve.wait_ge(ph["scores_ready"], t + 1)
                        dve.tensor_tensor(pT[:, t, :, :], psum[:, 4 + t, :].rearrange("p (h s) -> p h s", h=CHEADS), decay[:, :, :], ALU.mult).then_inc(ph["pT_ready"], 1)
                    dve.wait_ge(ph["kv_ready"], 1)
                    dve.tensor_copy(kv[:, :], psum[:, 6, :]).then_inc(ph["kv_copied"], 1)
                    dve.wait_ge(ph["spatial_ready"], 1)
                    sv = psum[:, 7, :].rearrange("p (c s) -> p c s", c=2)
                    for t in range(NT):
                        dve.tensor_tensor(yT[:, 0:2, t * P:(t + 1) * P], sv[:, :, t * P:(t + 1) * P], b_s[:, :, :], ALU.add).then_inc(ph["sv_ready"], 1)
                    dve.wait_ge(ph["sv_ready"], 2)
                    dve.wait_ge(ph["u_ready"], 1)
                    dve.tensor_tensor(yT[:, 0:2, :], yT[:, 0:2, :], uT[:, :, :], ALU.mult).then_inc(ph["ya_ready"], 1)
                    for t in range(NT):
                        dve.wait_ge(ph["ret_ready"], t + 1)
                    rg = [psum[:, 2 + t, h * P:(h + 1) * P] for t in range(NT) for h in range(CHEADS)]
                    self.group_stats(ph, dve, rg, bn, mv, var, 8, ph["var_c"])
                    dve.wait_ge(ph["rs_c"], 1)
                    for j in range(8):
                        dve.tensor_scalar(ret[:, j // 4, (j % 4) * P:(j % 4 + 1) * P], rg[j], mv[:, 8 + j, 0:1], rs[:, 8 + j:9 + j],
                                          ALU.subtract, ALU.mult).then_inc(ph["ret_scaled"], 1)
                    dve.wait_ge(ph["gate_ready"], 2)
                    for t in range(NT):
                        dve.wait_ge(ph["ret_scaled"], 4 * t + 4)
                        dve.tensor_tensor(ret[:, t, :], ret[:, t, :], gain_c[:, :], ALU.mult).then_inc(ph["ret_gained"], 1)
                        dve.wait_ge(ph["ret_gained"], t + 1)
                        dve.tensor_tensor(ret[:, t, :], ret[:, t, :], sg[:, t, :], ALU.mult).then_inc(ph["ret_gated"], 1)
                    for t in range(NT):
                        dve.wait_ge(ph["yc_turned"], t + 1)
                        dve.tensor_copy(yT[:, 4:8, t * P:(t + 1) * P], psum[:, 4 + t, :].rearrange("p (h s) -> p h s", h=CHEADS)).then_inc(ph["yc_ready"], 1)
                    for t in range(NT):
                        for n in range(2):
                            dve.wait_ge(ph["out_ready"], 2 * t + n + 1)
                            xs = self.x[:, t, n * WIDE:(n + 1) * WIDE]
                            dve.tensor_tensor(xs, psum[:, 2 * t + n, :], xs, ALU.add).then_inc(ph["x_ready"], 1)

                @ph.block.tensor
                def _(pe):
                    self.norm_pe(ph, pe)
                    self.norm_wait(ph, pe)

                    def panel(i):
                        return ring.wait(pe, i).rearrange("p (k n) -> p k n", n=WIDE)

                    def by_token(i, bank, c0=0, n=WIDE, at=0, one=False):
                        w = panel(i)
                        for t in range(NT):
                            dst = psum[:, bank, at + t * n:at + (t + 1) * n] if one else psum[:, bank + t, :]
                            for k in range(KT):
                                mm = pe.matmul(dst, hT[:, k, t * P:(t + 1) * P], w[:, k, c0:c0 + n], start=(k == 0), stop=(k == KT - 1))
                            if not one or t == NT - 1:
                                mm.then_inc(ph["proj_ready"], 1)

                    def by_channel(i, bank, c0):
                        w = panel(i)
                        for c in range(2):
                            for k in range(KT):
                                mm = pe.matmul(psum[:, bank, c * S:(c + 1) * S], w[:, k, c0 + c * P:c0 + (c + 1) * P], hT[:, k, 0:S],
                                               start=(k == 0), stop=(k == KT - 1))
                        mm.then_inc(ph["proj_ready"], 1)

                    by_token(0, 0)
                    by_token(1, 2)
                    pe.wait_ge(ph["small_in"], SMALL)
                    for g in range(4):
                        mm = pe.transpose(psum[:, 7, g * P:(g + 1) * P], w_s[:, g, :], ident[:, :])
                    mm.then_inc(ph["ws_turned"], 1)
                    pe.wait_ge(ph["rotated"], 2)
                    by_token(2, 0)
                    pe.wait_ge(ph["rotated"], 4)
                    by_token(3, 2)
                    pe.wait_ge(ph["ws_ready"], 1)
                    for i in range(2):
                        for t in range(NT):
                            for h in range(CHEADS):
                                mm = pe.transpose(psum[:, 4 + 2 * i + t, h * P:(h + 1) * P], qk[:, i, t, h * P:(h + 1) * P], ident[:, :])
                            mm.then_inc(ph["qk_turned"], 1)
                    pe.wait_ge(ph["v_ready"], 2)
                    by_channel(4, 0, 0)
                    by_token(4, 1, AW, AW, one=True)
                    pe.wait_ge(ph["gate_ready"], 2)
                    by_channel(5, 2, 0)
                    by_channel(5, 3, AW)
                    pe.wait_ge(ph["u_ready"], 1)
                    by_channel(6, 0, 0)
                    pe.wait_ge(ph["qkT_ready"], 4)
                    for t in range(NT):
                        for h in range(CHEADS):
                            mm = pe.matmul(psum[:, 4 + t, h * P:(h + 1) * P], qkT[:, 1, h, t * P:(t + 1) * P], qkT[:, 0, h, t * P:(t + 1) * P],
                                           start=True, stop=True)
                        mm.then_inc(ph["scores_ready"], 1)
                    pe.wait_ge(ph["kz_ready"], 1)
                    for h in range(CHEADS):
                        mm = pe.matmul(psum[:, 6, h * P:(h + 1) * P], kz[:, h * P:(h + 1) * P], v[:, 0, h * P:(h + 1) * P], start=True, stop=True)
                    mm.then_inc(ph["kv_ready"], 1)
                    pe.wait_ge(ph["va_normed"], 1)
                    for t in range(NT):
                        for g in range(4):
                            o = HEAD * (g % 2)
                            mm = pe.matmul(psum[o:o + HEAD, 7, (g // 2) * S + t * P:(g // 2) * S + (t + 1) * P],
                                           va[:, t, g * HEAD:(g + 1) * HEAD], wsT[:, g, :], start=True, stop=True)
                    mm.then_inc(ph["spatial_ready"], 1)
                    pe.wait_ge(ph["bcx_ready"], 2)
                    pe.wait_ge(ph["pT_ready"], 2)
                    pe.wait_ge(ph["kv_copied"], 1)
                    pe.wait_ge(ph["qx_ready"], 1)
                    for t in range(NT):
                        for h in range(CHEADS):
                            hs = slice(h * P, (h + 1) * P)
                            mm = pe.matmul(psum[:, 2 + t, hs], pT[:, t, h, :], v[:, t, hs], start=True, stop=(t == 0))
                            if t:
                                mm = pe.matmul(psum[:, 2 + t, hs], qx[:, h, :], kv[:, hs], start=False, stop=True)
                        mm.then_inc(ph["ret_ready"], 1)
                    for t in range(NT):
                        pe.wait_ge(ph["ret_gated"], t + 1)
                        for h in range(CHEADS):
                            mm = pe.transpose(psum[:, 4 + t, h * P:(h + 1) * P], ret[:, t, h * P:(h + 1) * P], ident[:, :])
                        mm.then_inc(ph["yc_turned"], 1)
                    pe.wait_ge(ph["bcx_ready"], 3)
                    pe.wait_ge(ph["va_ready"], 1)
                    pe.wait_ge(ph["ya_ready"], 1)
                    pe.wait_ge(ph["yb_ready"], 1)
                    pe.wait_ge(ph["yc_ready"], 2)
                    w = [ring.wait(pe, 7 + i).rearrange("p (k n) -> p k n", n=D) for i in range(2)]
                    for t in range(NT):
                        for n in range(2):
                            for k in range(KT):
                                mm = pe.matmul(psum[:, 2 * t + n, :], yT[:, k, t * P:(t + 1) * P], w[k // 4][:, k % 4, n * WIDE:(n + 1) * WIDE],
                                               start=(k == 0), stop=(k == KT - 1))
                            mm.then_inc(ph["out_ready"], 1)

    def group_stats(self, ph, dve, groups, bn, mv, var, at, done):
        n = len(groups)
        for j, g in enumerate(groups):
            dve.bn_stats(bn[:, at + j, :], g).then_inc(ph[f"stats_{at}"], 1)
        for j in range(n):
            dve.wait_ge(ph[f"stats_{at}"], j + 1)
            dve.bn_aggr(mv[:, at + j, :], bn[:, at + j, :]).then_inc(ph[f"aggregated_{at}"], 1)
        dve.wait_ge(ph[f"aggregated_{at}"], n)
        dve.tensor_scalar(var[:, at:at + n], mv[:, at:at + n, 1], EPS, None, ALU.add).then_inc(done, 1)

    def finish(self, normed=True):
        x, a = self.x, self.a
        with ExitStack() as ctx:
            gain = ctx.enter_context(self.nc.sbuf_tensor([P, D], F32))
            with self.phase() as ph:
                @ph.block.sync
                def _(sp):
                    if normed:
                        sp.dma_start(gain[:, :], a["final_norm_2"].partition_broadcast(P)).then_inc(ph["gain_in"], 16)
                    for t in range(NT):
                        if normed:
                            sp.wait_ge(ph["y_ready"], t + 1)
                        sp.dma_start(self.out[0, t * P:(t + 1) * P, :], (self.xn if normed else x)[:, t, :]).then_inc(ph["stored"], 16)
                    sp.wait_ge(ph["stored"], 16 * NT)

                if not normed:
                    return

                @ph.block.gpsimd
                def _(pool):
                    self.norm_pool(ph, pool)

                @ph.block.vector
                def _(dve):
                    self.norm_dve_stats(ph, dve, x)
                    dve.wait_ge(ph["rstd_ready"], 1)
                    dve.wait_ge(ph["gain_in"], 16)
                    for t in range(NT):
                        dve.scalar_tensor_tensor(out=self.xn[:, t, :], in0=x[:, t, :], scalar=self.rstd[:, t:t + 1], in1=gain[:, :],
                                                 op0=ALU.mult, op1=ALU.mult).then_inc(ph["y_ready"], 1)

    def ffn(self, l, norm, wg, wu, wd):
        a = self.a
        psum, hT = self.psum, self.hT
        kp = "a (k p) n -> p (a k) n"
        with ExitStack() as ctx:
            hid = ctx.enter_context(self.nc.sbuf_tensor([P, FT, S], F32))
            sg = ctx.enter_context(self.nc.sbuf_tensor([P, 2, S], F32))
            with self.phase() as ph:
                ring = Ring(ph, self.ring)
                panels = FF // S
                dn = 4

                @ph.block.sync
                def _(sp):
                    for j in range(panels):
                        def parts(slot):
                            slot = slot.rearrange("p (k n) -> p k n", n=WIDE)
                            for w, o in ((wg, 0), (wu, S)):
                                yield slot[:, :, o:o + S], a[w][bass.ds(l, 1)].rearrange(kp, p=P)[:, :, j * S:(j + 1) * S]
                        ring.load(sp, parts, (ph["pair_ready"], 2 * (j - SLOTS + 1)))
                    for q, f0 in enumerate(range(0, FT, dn)):
                        n = min(dn, FT - f0)

                        def parts(slot):
                            yield (slot[:, 0:n * D].rearrange("p (k n) -> p k n", n=D),
                                   a[wd][bass.ds(l, 1)].rearrange(kp, p=P)[:, f0:f0 + n, :])
                        i = panels + q - SLOTS
                        ring.load(sp, parts, (ph["pair_ready"], 2 * (i + 1)) if i < panels else (ph["down_used"], i - panels + 1))

                @ph.block.scalar
                def _(act):
                    with self.nc.allow_non_contiguous_dma(reason="a gain vector"):
                        act.dma_start(self.gain[:, :], a[norm][bass.ds(l, 1)].rearrange("a (k p) -> p (a k)", p=P)).then_inc(ph["gain_in"], 16)
                    act.wait_ge(ph["gain_in"], 16)
                    self.norm_act(ph, act, self.gain)
                    for f in range(FT):
                        act.wait_ge(ph["pair_ready"], f + 1)
                        if f >= 2:
                            act.wait_ge(ph["hid_ready"], f - 1)
                        act.activation(sg[:, f % 2, :], psum[:, f % 4, 0:S], ACT.Silu).then_inc(ph["silu_ready"], 1)

                @ph.block.gpsimd
                def _(pool):
                    self.norm_pool(ph, pool)

                @ph.block.vector
                def _(dve):
                    self.norm_dve_stats(ph, dve, self.x)
                    self.norm_dve_scale(ph, dve, self.x)
                    dve.wait_ge(ph["gain_in"], 16)
                    self.norm_dve_turn(ph, dve, self.gain)
                    for f in range(FT):
                        dve.wait_ge(ph["silu_ready"], f + 1)
                        dve.tensor_tensor(hid[:, f, :], sg[:, f % 2, :], psum[:, f % 4, S:2 * S], ALU.mult).then_inc(ph["hid_ready"], 1)
                    for t in range(NT):
                        for n in range(2):
                            dve.wait_ge(ph["down_ready"], 2 * t + n + 1)
                            dve.scalar_tensor_tensor(out=self.x[:, t, n * WIDE:(n + 1) * WIDE], in0=psum[:, 4 + 2 * t + n, :],
                                                     scalar=0.5, in1=self.x[:, t, n * WIDE:(n + 1) * WIDE],
                                                     op0=ALU.mult, op1=ALU.add).then_inc(ph["x_ready"], 1)

                @ph.block.tensor
                def _(pe):
                    self.norm_pe(ph, pe)
                    self.norm_wait(ph, pe)
                    for j in range(panels):
                        w = ring.wait(pe, j).rearrange("p (k n) -> p k n", n=WIDE)
                        for i in range(S // P):
                            f = j * (S // P) + i
                            if f >= 4:
                                pe.wait_ge(ph["hid_ready"], f - 3)
                            for o in (0, S):
                                for k in range(KT):
                                    mm = pe.matmul(psum[:, f % 4, o:o + S], w[:, k, o + i * P:o + (i + 1) * P], hT[:, k, 0:S],
                                                   start=(k == 0), stop=(k == KT - 1))
                            mm.then_inc(ph["pair_ready"], 1)
                    for q, f0 in enumerate(range(0, FT, dn)):
                        w = ring.wait(pe, panels + q).rearrange("p (k n) -> p k n", n=D)
                        n_f = min(dn, FT - f0)
                        for i in range(n_f):
                            f = f0 + i
                            pe.wait_ge(ph["hid_ready"], f + 1)
                            for t in range(NT):
                                for n in range(2):
                                    mm = pe.matmul(psum[:, 4 + 2 * t + n, :], hid[:, f, t * P:(t + 1) * P],
                                                   w[:, i, n * WIDE:(n + 1) * WIDE], start=(f == 0), stop=(f == FT - 1))
                                    if f == FT - 1:
                                        mm.then_inc(ph["down_ready"], 1)
                        if q < (FT + dn - 1) // dn - 1:
                            mm.then_inc(ph["down_used"], 1)

    def turn_rows(self, rows, cols):
        total = sum(r.shape[0] for r in rows)
        with ExitStack() as ctx:
            sb = self.scratch(ctx)
            tiles = [sb(P) for _ in range((total + P - 1) // P)]
            with self.phase() as ph:
                @ph.block.sync
                def _(sp):
                    at = n = 0
                    for r in rows:
                        done = 0
                        while done < r.shape[0]:
                            k = min(r.shape[0] - done, P - at % P)
                            sp.dma_start(tiles[at // P][at % P:at % P + k, :], r[done:done + k, :]).then_inc(ph["rows_in"], 16)
                            done, at, n = done + k, at + k, n + 1
                    self.row_loads = n

                @ph.block.tensor
                def _(pe):
                    pe.wait_ge(ph["rows_in"], 16 * self.row_loads)
                    for i, tile in enumerate(tiles):
                        n = min(P, total - i * P)
                        pe.transpose(self.psum[:, i, 0:n], tile[0:n, :], self.ident[0:n, 0:n]).then_inc(ph["rows_turned"], 1)

                @ph.block.vector
                def _(dve):
                    for i in range(len(tiles)):
                        n = min(P, total - i * P)
                        dve.wait_ge(ph["rows_turned"], i + 1)
                        dve.tensor_copy(cols[:, i * P:i * P + n], self.psum[:, i, 0:n]).then_inc(ph["cols_ready"], 1)

    def adaln(self, l, conds):
        a, psum = self.a, self.psum
        with ExitStack() as ctx:
            sb = self.scratch(ctx)
            bias, ada = sb(3 * D), sb(3 * D)
            panels = 3 * D // WIDE
            with self.phase() as ph:
                ring = Ring(ph, self.ring)

                @ph.block.sync
                def _(sp):
                    for j in range(panels):
                        def parts(slot):
                            yield (slot.rearrange("p (k n) -> p k n", n=WIDE),
                                   a["ada_w"][l].rearrange("(k p) n -> p k n", p=P)[:, :, j * WIDE:(j + 1) * WIDE])
                        ring.load(sp, parts, (ph["ada_ready"], j - SLOTS + 1))

                @ph.block.scalar
                def _(act):
                    act.dma_start(bias[0:2, :], a["ada_b"][l].partition_broadcast(2)).then_inc(ph["bias_in"], 16)
                    act.dma_start(self.post[:, :], a["norm_post"][l].partition_broadcast(P)).then_inc(ph["post_in"], 16)
                    with self.nc.allow_non_contiguous_dma(reason="a gain vector"):
                        act.dma_start(self.gain[:, :], chan(a["norm_pre"][l])).then_inc(ph["gain_in"], 16)

                @ph.block.tensor
                def _(pe):
                    for j in range(panels):
                        w = ring.wait(pe, j).rearrange("p (k n) -> p k n", n=WIDE)
                        for k in range(KT):
                            mm = pe.matmul(psum[0:2, j, :], self.cond[:, k, :], w[:, k, :], start=(k == 0), stop=(k == KT - 1))
                        mm.then_inc(ph["ada_ready"], 1)
                    pe.wait_ge(ph["biased"], panels)
                    for k in range(2 * KT):
                        mm = pe.transpose(psum[:, 6, 2 * k:2 * k + 2], ada[0:2, k * P:(k + 1) * P], self.ident[0:2, 0:2])
                    mm.then_inc(ph["ada_turned"], 1)
                    for n in range(2):
                        mm = pe.matmul(psum[:, n, :], self.ones[0:1, :], ada[0:1, 2 * D + n * WIDE:2 * D + (n + 1) * WIDE], start=True, stop=True)
                    mm.then_inc(ph["gate_spread"], 1)

                @ph.block.vector
                def _(dve):
                    dve.wait_ge(ph["bias_in"], 16)
                    for j in range(panels):
                        dve.wait_ge(ph["ada_ready"], j + 1)
                        dve.tensor_tensor(ada[0:2, j * WIDE:(j + 1) * WIDE], psum[0:2, j, :], bias[0:2, j * WIDE:(j + 1) * WIDE], ALU.add).then_inc(ph["biased"], 1)
                    dve.wait_ge(ph["ada_turned"], 1)
                    dve.wait_ge(ph["gain_in"], 16)
                    cols = psum[:, 6, 0:4 * KT].rearrange("p (k c) -> p c k", c=2)
                    for c in range(conds):
                        dve.tensor_copy(self.shift[:, c, :], cols[:, c, 0:KT]).then_inc(ph["shift_ready"], 1)
                        dve.scalar_tensor_tensor(out=self.scale[:, c, :], in0=cols[:, c, KT:2 * KT], scalar=1.0, in1=self.gain[:, :],
                                                 op0=ALU.add, op1=ALU.mult).then_inc(ph["scale_ready"], 1)
                    dve.wait_ge(ph["gate_spread"], 1)
                    dve.wait_ge(ph["post_in"], 16)
                    for n in range(2):
                        s = slice(n * WIDE, (n + 1) * WIDE)
                        dve.tensor_tensor(self.post[:, s], self.post[:, s], psum[:, n, :], ALU.mult).then_inc(ph["post_ready"], 1)

    def norm_first(self, x, c, at):
        with self.phase() as ph:
            @ph.block.vector
            def _(dve):
                self.norm_dve_stats(ph, dve, x)
                self.norm_dve_scale(ph, dve, x)
                self.norm_dve_turn(ph, dve, self.scale[:, c, :], self.shift[:, c, :], at=at)

            @ph.block.gpsimd
            def _(pool):
                self.norm_pool(ph, pool)

            @ph.block.tensor
            def _(pe):
                self.norm_pe(ph, pe)

            @ph.block.scalar
            def _(act):
                self.norm_act(ph, act, self.scale[:, c, :], self.shift[:, c, :], at=at)

    def out_first(self, l, uT):
        a, psum = self.a, self.psum
        with self.phase() as ph:
            ring = Ring(ph, self.ring)

            @ph.block.sync
            def _(sp):
                for q in range(ET // 4):
                    def parts(slot):
                        yield (slot.rearrange("p (k n) -> p k n", n=D),
                               a["w_out"][l].rearrange("(k p) n -> p k n", p=P)[:, 4 * q:4 * q + 4, :])
                    ring.load(sp, parts, None)

            @ph.block.tensor
            def _(pe):
                for q in range(ET // 4):
                    w = ring.wait(pe, q).rearrange("p (k n) -> p k n", n=D)
                    for i in range(4):
                        e = 4 * q + i
                        for t in range(NT):
                            for n in range(2):
                                mm = pe.matmul(psum[:, 2 * t + n, :], uT[:, e, t * P:(t + 1) * P], w[:, i, n * WIDE:(n + 1) * WIDE],
                                               start=(e == 0), stop=(e == ET - 1))
                                if e == ET - 1:
                                    mm.then_inc(ph["out_ready"], 1)

            @ph.block.gpsimd
            def _(pool):
                self.norm_pool(ph, pool)

            @ph.block.vector
            def _(dve):
                o = self.hT[:, :, :].rearrange("p k s -> p (k s)")[:, 0:NT * D].rearrange("p (t d) -> p t d", t=NT)
                for t in range(NT):
                    for n in range(2):
                        dve.wait_ge(ph["out_ready"], 2 * t + n + 1)
                        dve.tensor_copy(o[:, t, n * WIDE:(n + 1) * WIDE], psum[:, 2 * t + n, :]).then_inc(ph["out_copied"], 1)
                dve.wait_ge(ph["out_copied"], 4)
                self.norm_dve_stats(ph, dve, o)
                dve.wait_ge(ph["rstd_ready"], 1)
                for t in range(NT):
                    dve.scalar_tensor_tensor(out=o[:, t, :], in0=o[:, t, :], scalar=self.rstd[:, t:t + 1], in1=self.post[:, :],
                                             op0=ALU.mult, op1=ALU.mult).then_inc(ph["out_scaled"], 1)
                for t in range(NT):
                    dve.wait_ge(ph["out_scaled"], t + 1)
                    dve.tensor_tensor(self.x[:, t, :], self.x[:, t, :], o[:, t, :], ALU.add).then_inc(ph["x_ready"], 1)

    def rwkv_mixes(self, mix, lora, cols):
        a, psum, hT = self.a, self.psum, self.hT
        groups = [(0, "r", S), (1, "k", 2 * S), (2, "v", 2 * S), (3, "g", S), (4, "w", 2 * S), (5, "a", 2 * S)]
        with ExitStack() as ctx:
            sb = self.scratch(ctx)
            xx = sb(KT, 2 * S)
            loras = {"w": sb(KT, 2 * S)}
            loras["a"] = loras["w"]
            wl = self.ring[:, 0, 0:KT * 256].rearrange("p (k n) -> p k n", n=256)
            with self.phase() as ph:
                @ph.block.sync
                def _(sp):
                    sp.dma_start(wl, a["l0_w_in"].rearrange("(k p) n -> p k n", p=P)[:, :, 4 * E:4 * E + 4 * LORA]).then_inc(ph["lora_in"], 16)

                @ph.block.vector
                def _(dve):
                    n = 0

                    def diff(dst, other, own):
                        nonlocal n
                        dve.tensor_tensor(dst, other, own, ALU.subtract).then_inc(ph["shifted"], 1)
                        n += 1

                    def edge(dst, own):
                        nonlocal n
                        dve.tensor_scalar(dst, own, -1.0, None, ALU.mult).then_inc(ph["shifted"], 1)
                        n += 1
                    for q in range(4):
                        for k in (2 * q, 2 * q + 1):
                            h, d = hT[:, k, 0:S], xx[:, k, 0:S]
                            hg, dg = (v.rearrange("p (r c) -> p r c", c=64) for v in (h, d))
                            if q == 0:
                                diff(dg[:, :, 1:], hg[:, :, 0:63], hg[:, :, 1:])
                                edge(dg[:, :, 0:1], hg[:, :, 0:1])
                            elif q == 1:
                                diff(dg[:, :, 0:63], hg[:, :, 1:], hg[:, :, 0:63])
                                edge(dg[:, :, 63:64], hg[:, :, 63:64])
                            elif q == 2:
                                diff(d[:, 64:], h[:, 0:S - 64], h[:, 64:])
                                edge(d[:, 0:64], h[:, 0:64])
                            else:
                                diff(d[:, 0:S - 64], h[:, 64:], h[:, 0:S - 64])
                                edge(d[:, S - 64:], h[:, S - 64:])
                    for k in range(KT):
                        h, d = hT[:, k, S:2 * S], xx[:, k, S:2 * S]
                        if k < KT // 2:
                            diff(d[:, 1:], h[:, 0:S - 1], h[:, 1:])
                            edge(d[:, 0:1], h[:, 0:1])
                        else:
                            diff(d[:, 0:S - 1], h[:, 1:], h[:, 0:S - 1])
                            edge(d[:, S - 1:], h[:, S - 1:])
                    dve.wait_ge(ph["shifted"], n)
                    for g, name, w in groups[4:] + groups[:4]:
                        dst = loras[name] if name in loras else mix[name]
                        if name == "a":
                            dve.wait_ge(ph["lora_ready"], 1)
                        for k in range(KT):
                            dve.scalar_tensor_tensor(out=dst[:, k, 0:w], in0=xx[:, k, 0:w], scalar=cols[:, g * KT + k:g * KT + k + 1],
                                                     in1=hT[:, k, 0:w], op0=ALU.mult, op1=ALU.add).then_inc(ph["mixed"], 1)
                    dve.wait_ge(ph["lora_ready"], 2)
                    dve.tensor_copy(lora["a"][:, :], psum[:, 1, :]).then_inc(ph["lora_a"], 1)

                @ph.block.tensor
                def _(pe):
                    pe.wait_ge(ph["lora_in"], 16)
                    for i in range(2):
                        pe.wait_ge(ph["mixed"], KT * (i + 1))
                        for k in range(KT):
                            mm = pe.matmul(psum[:, i, :], wl[:, k, i * P:(i + 1) * P], loras["w"][:, k, :], start=(k == 0), stop=(k == KT - 1))
                        mm.then_inc(ph["lora_ready"], 1)

                @ph.block.scalar
                def _(act):
                    act.wait_ge(ph["lora_ready"], 1)
                    act.activation(lora["w"][:, :], psum[:, 0, :], ACT.Tanh).then_inc(ph["lora_w"], 1)

    def rwkv_heads(self, i, mix, lora, prm, uT):
        a, psum, ident = self.a, self.psum, self.ident
        C = 2 * S // CH
        XC = S // CH
        BD = 2 * CH
        DECAY = float(np.exp(-0.5))
        LEVELS = 5
        order = [list(range(XC, C)) + list(range(XC)), list(range(C - 1, XC - 1, -1)) + list(range(XC - 1, -1, -1))]
        heads = (slice(0, CH), slice(CH, P))
        room = self.ring[:, 1:SLOTS, :].rearrange("p s n -> p (s n)")
        at = [0]

        def carve(*shape):
            n = int(np.prod(shape))
            v = room[:, at[0]:at[0] + n]
            at[0] += n
            names = "abc"[:len(shape)]
            if len(shape) > 1:
                v = v.rearrange(f"p ({' '.join(names)}) -> p {' '.join(names)}", **{c: s for c, s in zip(names, shape)})
            return v

        with ExitStack() as ctx:
            sb = self.scratch(ctx)
            w = self.ring[:, 0, :].rearrange("p (k j n) -> p k j n", j=4, n=P)
            w2, a2, cur = sb(P), sb(P), sb(10)
            vbd, Vt = carve(C, BD), carve(C, BD)
            K, KK, kn = carve(2 * S), carve(2 * S), carve(2 * S)
            R, V, G = carve(S), carve(S), carve(S)
            abd = [carve(C, BD) for _ in range(2)]
            Uv = [self.hT[:, 2 * z:2 * z + 2, :].rearrange("p k (c n) -> p (k c) n", n=BD) for z in range(2)]
            Tv = [self.hT[:, 4 + 2 * z:6 + 2 * z, :].rearrange("p k (c n) -> p (k c) n", n=BD) for z in range(2)]
            xnf = self.xn[:, :, :]
            Rv = [xnf[:, z, :].rearrange("p (c n) -> p c n", n=BD) for z in range(2)]
            assert at[0] <= 3 * KT * WIDE
            bk = self.ring[:, 0, :].rearrange("p (q c n) -> p q c n", q=4, n=BD)
            btok, ktok = [bk[:, z] for z in range(2)], [bk[:, 2 + z] for z in range(2)]
            rt = [sb(XC, CH) for _ in range(2)]
            AX_ = [sb(XC, 2 * BD) for _ in range(2)]
            AC_ = [carve(C - XC, BD) for _ in range(2)]
            bbd, kbd = sb(C, BD), sb(C, BD)
            Bv = [bbd, kbd]
            sig = [carve(2 * S) for _ in range(2)]
            al = [carve(2 * S) for _ in range(2)]
            L, E1, E3 = carve(2 * S), sb(2 * S), carve(2 * S)
            kd, E2 = carve(2 * S), carve(2 * S)
            Dt = sb(2, C)
            prod = [carve(S) for _ in range(2)]
            St, DS, Rs, Us = ([Tv[0][:, 2 * q + z, :] for z in range(2)] for q in range(4))
            y, cen = (Tv[1][:, 2 * q:2 * q + 2, :].rearrange("p c n -> p (c n)") for q in range(2))
            assert at[0] <= 3 * KT * WIDE, at

            with self.phase() as ph:
                @ph.block.sync
                def _(sp):
                    wv = a["l0_w_in"].rearrange("(k p) n -> p k n", p=P)
                    for j in (1, 0, 3, 2):
                        sp.dma_start(w[:, :, j, :], wv[:, :, bass.ds(i * P + j * E, P)]).then_inc(ph[f"w{j}_in"], 16)
                    sp.dma_start(w2[:, :], a["l0_w2"].rearrange("z r e -> (z r) e")[:, bass.ds(i * P, P)]).then_inc(ph["lora_in"], 16)
                    sp.dma_start(a2[:, :], a["l0_a2"].rearrange("z r e -> (z r) e")[:, bass.ds(i * P, P)]).then_inc(ph["lora_in"], 16)

                W0, A0, KKW, KA, RK, LNW, LNB, OMK = 0, 2, 4, 5, 6, 7, 8, 9

                def col(j):
                    return cur[:, j:j + 1]

                @ph.block.tensor
                def _(pe):
                    for j, name, bank, o, n in ((1, "k", 0, 0, 2 * S), (0, "r", 1, 0, S), (3, "g", 1, S, S), (2, "v", 2, 0, 2 * S)):
                        pe.wait_ge(ph[f"w{j}_in"], 16)
                        for k in range(KT):
                            mm = pe.matmul(psum[:, bank, o:o + n], w[:, k, j, :], mix[name][:, k, 0:n], start=(k == 0), stop=(k == KT - 1))
                        mm.then_inc(ph["proj_ready"], 1)
                    pe.wait_ge(ph["lora_in"], 32)
                    for z in range(2):
                        zs = slice(LORA * z, LORA * z + LORA)
                        pe.matmul(psum[:, 3 + 2 * z, :], w2[zs, :], lora["w"][zs, :], start=True, stop=True).then_inc(ph["lora_ready"], 1)
                        pe.matmul(psum[:, 4 + 2 * z, :], a2[zs, :], lora["a"][zs, :], start=True, stop=True).then_inc(ph["lora_ready"], 1)
                    pe.wait_ge(ph["kk_squared"], 1)
                    pe.matmul(psum[:, 7, :], self.same_head[:, :], kn[:, :], start=True, stop=True).then_inc(ph["kk_summed"], 1)
                    pe.wait_ge(ph["v_ready"], 3)
                    for c in range(C):
                        mm = pe.transpose(psum[:, c // 4, (c % 4) * BD:(c % 4 + 1) * BD], vbd[:, c, :], ident[:, :])
                        if c % 4 == 3:
                            mm.then_inc(ph["v_turned"], 1)
                    for z in range(2):
                        pe.wait_ge(ph["bd_ready"], z + 1)
                        if z == 0:
                            pe.wait_ge(ph["sig_ready"], 4)
                            pe.wait_ge(ph["kk_rooted"], 1)
                            pe.wait_ge(ph["vt_ready"], 2)
                        else:
                            pe.wait_ge(ph["tok_ready"], 4)
                        for src, b in ((bbd, 2), (kbd, 4)):
                            for c in range(C):
                                mm = pe.transpose(psum[:, b + c // 4, (c % 4) * BD:(c % 4 + 1) * BD], src[:, c, :], ident[:, :])
                                if c % 4 == 3:
                                    mm.then_inc(ph["tok_turned"], 1)
                        for c in range(C):
                            n = z * C + c
                            bank = (6, 7, 0, 1)[c % 4]
                            if n >= 4:
                                pe.wait_ge(ph["a_ready"], n - 3)
                            pe.matmul(psum[:, bank, 0:BD], bbd[:, c, :], abd[z][:, c, :], start=True, stop=True)
                            mm = pe.matmul(psum[:, bank, BD:2 * BD], kbd[:, c, :], abd[z][:, c, :], start=True, stop=True)
                            if c < XC:
                                pe.matmul(psum[:, bank, 2 * BD:2 * BD + CH], bbd[:, c, :], rt[z][:, c, :], start=True, stop=True)
                                mm = pe.matmul(psum[:, bank, 2 * BD + CH:3 * BD], kbd[:, c, :], rt[z][:, c, :], start=True, stop=True)
                            mm.then_inc(ph["a_made"], 1)
                    pe.wait_ge(ph["tok_ready"], 8)
                    pe.wait_ge(ph["a_ready"], 2 * C)
                    for z in range(2):
                        for half in range(2):
                            for c in range(4):
                                mm = pe.transpose(psum[:, 2 * z + half, c * BD:(c + 1) * BD], Rv[z][:, 4 * half + c, :], ident[:, :])
                            mm.then_inc(ph["b_turned"], 1)
                    for z in range(2):
                        for half in range(2):
                            pe.wait_ge(ph["u_level"], 2 * z + half + 1)
                            for c in range(4):
                                mm = pe.transpose(psum[:, 4 + 2 * z + half, c * BD:(c + 1) * BD], Uv[z][:, 4 * half + c, :], ident[:, :])
                            mm.then_inc(ph["t_turned"], 1)
                    for m in range(LEVELS):
                        for j in range(4):
                            z, half = j // 2, j % 2
                            pe.wait_ge(ph["b_ready"], j + 1)
                            pe.wait_ge(ph["u_level"], 4 * m + j + 1)
                            pe.wait_ge(ph["t_level"], 4 * m + j + 1)
                            for c in range(4):
                                cc = 4 * half + c
                                mm = pe.matmul(psum[:, j, c * BD:(c + 1) * BD], Bv[z][:, cc, :], Uv[z][:, cc, :], start=True, stop=True)
                            mm.then_inc(ph["r_made"], 1)
                        for j in range(4):
                            z, half = j // 2, j % 2
                            pe.wait_ge(ph["r_level"], 4 * m + j + 1)
                            for c in range(4):
                                cc = 4 * half + c
                                mm = pe.matmul(psum[:, 4 + j, c * BD:(c + 1) * BD], Tv[z][:, cc, :], Rv[z][:, cc, :], start=True, stop=True)
                            mm.then_inc(ph["u_made"], 1)
                        if m < LEVELS - 1:
                            for j in range(4):
                                z, half = j // 2, j % 2
                                pe.wait_ge(ph["u_level"], 4 * (m + 1) + j + 1)
                                for c in range(4):
                                    mm = pe.transpose(psum[:, j, c * BD:(c + 1) * BD], Uv[z][:, 4 * half + c, :], ident[:, :])
                                mm.then_inc(ph["t_turned"], 1)
                    pe.wait_ge(ph["u_level"], 4 * (LEVELS + 1))
                    for n in range(C):
                        for z in range(2):
                            c = order[z][n]
                            ak = AX_[z][:, c, 0:BD] if c < XC else AC_[z][:, c - XC, :]
                            if n:
                                pe.wait_ge(ph[f"state_{z}"], n)
                                pe.matmul(psum[:, 4 * z, 0:BD], abd[z][:, c, :], St[z], start=True, stop=False)
                            pe.matmul(psum[:, 4 * z, 0:BD], ak, Vt[:, c, :], start=(n == 0), stop=True).then_inc(ph[f"rhs_made_{z}"], 1)
                        for z in range(2):
                            c = order[z][n]
                            pe.wait_ge(ph[f"rhs_{z}"], n + 1)
                            pe.matmul(psum[:, 4 * z + 1, 0:BD], Uv[z][:, c, :], Rs[z], start=True, stop=True).then_inc(ph[f"u_made_{z}"], 1)
                        for z in range(2):
                            c = order[z][n]
                            pe.wait_ge(ph[f"u_{z}"], n + 1)
                            if n < C - 1:
                                pe.matmul(psum[:, 4 * z + 2, 0:BD], btok[z][:, c, :], Us[z], start=True, stop=False)
                                pe.matmul(psum[:, 4 * z + 2, 0:BD], ktok[z][:, c, :], Vt[:, c, :], start=False, stop=True).then_inc(ph[f"state_made_{z}"], 1)
                            if c < XC:
                                ys = psum[:, 4 * z + 3, c * CH:(c + 1) * CH]
                                pe.matmul(ys, St[z], rt[z][:, c, :], start=True, stop=False)
                                pe.matmul(ys, Us[z], AX_[z][:, c, BD:BD + CH], start=False, stop=False)
                                pe.matmul(ys, Vt[:, c, :], AX_[z][:, c, BD + CH:2 * BD], start=False, stop=True).then_inc(ph[f"y_made_{z}"], 1)
                    pe.wait_ge(ph["prod_ready"], 2)
                    for z in range(2):
                        mm = pe.matmul(psum[:, 2, 0:S], self.same_head[:, :], prod[z][:, :], start=(z == 0), stop=(z == 1))
                    mm.then_inc(ph["bonus_made"], 1)
                    pe.wait_ge(ph["y_ready"], 1)
                    pe.matmul(psum[:, 0, 0:S], self.head_mean[:, :], y, start=True, stop=True).then_inc(ph["mean_made"], 1)
                    pe.wait_ge(ph["squared"], 1)
                    pe.matmul(psum[:, 1, 0:S], self.head_mean[:, :], y, start=True, stop=True).then_inc(ph["var_made"], 1)

                @ph.block.scalar
                def _(act):
                    act.wait_ge(ph["proj_ready"], 1)
                    act.activation(K[:, :], psum[:, 0, :], ACT.Copy).then_inc(ph["k_ready"], 1)
                    act.wait_ge(ph["proj_ready"], 3)
                    act.activation(R[:, :], psum[:, 1, 0:S], ACT.Copy).then_inc(ph["r_ready"], 1)
                    act.activation(G[:, :], psum[:, 1, S:2 * S], ACT.Silu).then_inc(ph["g_ready"], 1)
                    act.wait_ge(ph["proj_ready"], 4)
                    act.wait_ge(ph["zeroed"], 1)
                    for h in range(2):
                        act.activation(vbd[heads[h], :, h * CH:(h + 1) * CH], psum[heads[h], 2, :].rearrange("p (c s) -> p c s", s=CH), ACT.Copy).then_inc(ph["v_ready"], 1)
                    act.activation(V[:, :], psum[:, 2, 0:S], ACT.Copy).then_inc(ph["v_ready"], 1)
                    act.wait_ge(ph["cur_ready"], 2)
                    for z in range(2):
                        act.wait_ge(ph["lora_ready"], 2 * z + 2)
                        act.activation(sig[z][:, :], psum[:, 3 + 2 * z, :], ACT.Sigmoid, bias=col(W0 + z)).then_inc(ph["sig_ready"], 1)
                        act.activation(al[z][:, :], psum[:, 4 + 2 * z, :], ACT.Sigmoid, bias=col(A0 + z)).then_inc(ph["sig_ready"], 1)
                    act.wait_ge(ph["kk_summed"], 1)
                    act.wait_ge(ph["kk_floored"], 1)
                    act.activation(KK[:, :], KK[:, :], ACT.Sqrt).then_inc(ph["kk_rooted"], 1)
                    for b in range(2):
                        act.wait_ge(ph["v_turned"], b + 1)
                        act.activation(Vt[:, 4 * b:4 * b + 4, :], psum[:, b, :].rearrange("p (c n) -> p c n", n=BD), ACT.Copy).then_inc(ph["vt_ready"], 1)
                    for z in range(2):
                        act.wait_ge(ph["l_ready"], z + 1)
                        if z:
                            act.wait_ge(ph["bd_ready"], 1)
                        act.activation(E1[:, :], L[:, :], ACT.Exp, scale=-DECAY).then_inc(ph["e_ready"], 1)
                        act.activation(E3[:, :], L[:, :], ACT.Exp, scale=DECAY).then_inc(ph["e_ready"], 1)
                        act.wait_ge(ph["lex_ready"], z + 1)
                        act.activation(E2[:, :], E2[:, :], ACT.Exp, scale=-DECAY).then_inc(ph["e_ready"], 1)
                        for q in range(4):
                            act.wait_ge(ph["tok_turned"], 4 * z + q + 1)
                            dst = (btok, ktok)[q // 2][z]
                            act.activation(dst[:, 4 * (q % 2):4 * (q % 2) + 4, :], psum[:, 2 + q, :].rearrange("p (c n) -> p c n", n=BD), ACT.Copy).then_inc(ph["tok_ready"], 1)
                    for j in range(4):
                        act.wait_ge(ph["b_turned"], j + 1)
                        act.activation(Bv[j // 2][:, 4 * (j % 2):4 * (j % 2) + 4, :], psum[:, j, :].rearrange("p (c n) -> p c n", n=BD), ACT.Copy).then_inc(ph["b_ready"], 1)
                    for m in range(LEVELS):
                        for j in range(4):
                            z, half = j // 2, j % 2
                            act.wait_ge(ph["t_turned"], 4 * m + j + 1)
                            if m:
                                act.wait_ge(ph["u_made"], 4 * (m - 1) + j + 1)
                            act.activation(Tv[z][:, 4 * half:4 * half + 4, :], psum[:, (4 if m == 0 else 0) + j, :].rearrange("p (c n) -> p c n", n=BD), ACT.Copy).then_inc(ph["t_level"], 1)
                    for n in range(C):
                        for z in range(2):
                            c = order[z][n]
                            act.wait_ge(ph[f"rhs_made_{z}"], n + 1)
                            if n:
                                act.wait_ge(ph[f"u_made_{z}"], n)
                            act.activation(Rs[z], psum[:, 4 * z, 0:BD], ACT.Copy).then_inc(ph[f"rhs_{z}"], 1)
                            if 0 < n < C - 1:
                                act.activation(DS[z], St[z], ACT.Copy, scale=Dt[:, z, c:c + 1]).then_inc(ph[f"ds_{z}"], 1)
                    act.wait_ge(ph["var_made"], 1)
                    act.activation(cen, psum[:, 1, 0:S], ACT.Sqrt, bias=self.gn_eps[:, 0:1]).then_inc(ph["rooted"], 1)

                @ph.block.gpsimd
                def _(pool):
                    pool.memset(vbd[:, :, :], 0.0).then_inc(ph["zeroed"], 1)
                    for t in (bbd, kbd, abd[0], abd[1]):
                        pool.memset(t[:, :, :], 0.0).then_inc(ph["zeroed"], 1)
                    pool.wait_ge(ph["kk_weighted"], 1)
                    pool.tensor_tensor(kn[:, :], E1[:, :], E1[:, :], ALU.mult).then_inc(ph["kk_squared"], 1)
                    for z in range(2):
                        pool.wait_ge(ph["l_ready"], z + 1)
                        if z:
                            pool.wait_ge(ph["bd_ready"], 1)
                        pool.tensor_tensor(E2[:, :], L[:, :], sig[z][:, :], ALU.subtract).then_inc(ph["lex_ready"], 1)
                        pool.wait_ge(ph["kd_scaled"], z + 1)
                        pool.tensor_tensor(kd[:, :], kd[:, :], K[:, :], ALU.mult).then_inc(ph["kd_ready"], 1)
                        pool.wait_ge(ph["kk_ready"], 1)
                        pool.tensor_tensor(al[z][:, :], al[z][:, :], KK[:, :], ALU.mult).then_inc(ph["b_vec"], 1)
                        pool.wait_ge(ph["kd_ready"], z + 1)
                        pool.wait_ge(ph["r_ready"], 1)
                        pool.tensor_tensor(prod[z][:, :], kd[:, 0:S], R[:, :], ALU.mult).then_inc(ph["prod_raw"], 1)
                        pool.wait_ge(ph["prod_raw"], z + 1)
                        pool.tensor_scalar(prod[z][:, :], prod[z][:, :], col(RK), None, ALU.mult).then_inc(ph["prod_ready"], 1)

                @ph.block.vector
                def _(dve):
                    dve.tensor_copy(cur[:, 0:9], prm[:, 0:9, bass.ds(i, 1)].rearrange("p j a -> p (j a)")).then_inc(ph["cur_ready"], 1)
                    dve.wait_ge(ph["cur_ready"], 1)
                    dve.tensor_scalar(cur[:, 9:10], cur[:, KA:KA + 1], -1.0, 1.0, ALU.mult, ALU.add).then_inc(ph["cur_ready"], 1)
                    dve.wait_ge(ph["cur_ready"], 2)
                    dve.wait_ge(ph["k_ready"], 1)
                    dve.tensor_scalar(E1[:, :], K[:, :], col(KKW), None, ALU.mult).then_inc(ph["kk_weighted"], 1)
                    dve.wait_ge(ph["kk_summed"], 1)
                    dve.tensor_scalar(KK[:, :], psum[:, 7, :], 1e-24, None, ALU.max).then_inc(ph["kk_floored"], 1)
                    dve.wait_ge(ph["kk_rooted"], 1)
                    dve.reciprocal(kn[:, :], KK[:, :]).then_inc(ph["kk_inverse"], 1)
                    dve.wait_ge(ph["kk_inverse"], 1)
                    dve.tensor_tensor(KK[:, :], E1[:, :], kn[:, :], ALU.mult).then_inc(ph["kk_ready"], 1)
                    dve.wait_ge(ph["zeroed"], 5)
                    dve.wait_ge(ph["kk_ready"], 1)
                    for z in range(2):
                        dve.wait_ge(ph["sig_ready"], 2 * z + 2)
                        if z:
                            dve.wait_ge(ph["halves"], 7)
                            dve.wait_ge(ph["e_ready"], 3)
                            dve.wait_ge(ph["lex_ready"], 1)
                            dve.wait_ge(ph["prod_raw"], 1)
                        lv, sv = (L[:, :], sig[z][:, :]) if z == 0 else (L[:, ::-1], sig[z][:, ::-1])
                        dve.tensor_tensor_scan(lv, self.no_start[:, :], sv, 0.0, ALU.mult, ALU.add).then_inc(ph["l_ready"], 1)
                        dve.tensor_scalar(kd[:, :], al[z][:, :], col(KA), col(OMK), ALU.mult, ALU.add).then_inc(ph["kd_scaled"], 1)
                        dve.wait_ge(ph["e_ready"], 3 * z + 3)
                        end = E1[:, :].rearrange("p (c s) -> p c s", s=CH)[:, :, CH - 1 if z == 0 else 0]
                        dve.tensor_copy(Dt[:, z, :], end).then_inc(ph["d_ready"], 1)
                        dve.wait_ge(ph["b_vec"], z + 1)
                        dve.wait_ge(ph["kd_ready"], z + 1)
                        if z:
                            dve.wait_ge(ph["a_made"], C)
                            dve.wait_ge(ph["tok_turned"], 4)

                        def chunks(v):
                            return v.rearrange("p (c s) -> p c s", s=CH)
                        for h in range(2):
                            hs, cs = heads[h], slice(h * CH, (h + 1) * CH)
                            dve.scalar_tensor_tensor(out=abd[z][hs, :, cs], in0=chunks(KK[hs, :]), scalar=-1.0, in1=chunks(E2[hs, :]),
                                                     op0=ALU.mult, op1=ALU.mult).then_inc(ph["halves"], 1)
                            dve.tensor_tensor(bbd[hs, :, cs], chunks(al[z][hs, :]), chunks(E3[hs, :]), ALU.mult).then_inc(ph["halves"], 1)
                            dve.tensor_tensor(kbd[hs, :, cs], chunks(kd[hs, :]), chunks(E3[hs, :]), ALU.mult).then_inc(ph["halves"], 1)
                        dve.tensor_tensor(rt[z][:, :, :], chunks(R[:, :]), chunks(E1[:, 0:S]), ALU.mult).then_inc(ph["halves"], 1)
                        dve.wait_ge(ph["halves"], 7 * z + 7)
                        dve.wait_ge(ph["d_ready"], z + 1)
                        dve.wait_ge(ph["d_ready"], z + 1)
                        dve.sem_inc(ph["bd_ready"], 1)
                        for c in range(C):
                            n = z * C + c
                            bank = (6, 7, 0, 1)[c % 4]
                            dve.wait_ge(ph["a_made"], n + 1)
                            dve.tensor_tensor(Rv[z][:, c, :], psum[:, bank, 0:BD], self.strict[:, z, 0:BD], ALU.mult).then_inc(ph["aab_ready"], 1)
                            if c < XC:
                                dve.tensor_tensor(AX_[z][:, c, :], psum[:, bank, BD:3 * BD], self.strict[:, z, BD:3 * BD], ALU.mult).then_inc(ph["a_ready"], 1)
                            else:
                                dve.tensor_tensor(AC_[z][:, c - XC, :], psum[:, bank, BD:2 * BD], self.strict[:, z, BD:2 * BD], ALU.mult).then_inc(ph["a_ready"], 1)
                    dve.wait_ge(ph["aab_ready"], 2 * C)
                    for j in range(4):
                        z, half = j // 2, j % 2
                        us, rs = Uv[z][:, 4 * half:4 * half + 4, :], Rv[z][:, 4 * half:4 * half + 4, :]
                        dve.tensor_tensor(us, rs, self.level[:, z, 0, :].unsqueeze(1).to_broadcast([P, 4, BD]), ALU.mult).then_inc(ph["first_pairs"], 1)
                        dve.wait_ge(ph["first_pairs"], j + 1)
                        dve.tensor_tensor(us, us, ident[:, :].unsqueeze(1).to_broadcast([P, 4, BD]), ALU.add).then_inc(ph["u_level"], 1)
                    for m in range(LEVELS):
                        for j in range(4):
                            z, half = j // 2, j % 2
                            dve.wait_ge(ph["r_made"], 4 * m + j + 1)
                            dve.wait_ge(ph["b_turned"], 4)
                            dve.tensor_tensor(Rv[z][:, 4 * half:4 * half + 4, :], psum[:, j, :].rearrange("p (c n) -> p c n", n=BD),
                                              self.level[:, z, m + 1, :].unsqueeze(1).to_broadcast([P, 4, BD]), ALU.mult).then_inc(ph["r_level"], 1)
                        for j in range(4):
                            z, half = j // 2, j % 2
                            dve.wait_ge(ph["u_made"], 4 * m + j + 1)
                            us = Uv[z][:, 4 * half:4 * half + 4, :]
                            dve.tensor_tensor(us, psum[:, 4 + j, :].rearrange("p (c n) -> p c n", n=BD), us, ALU.add).then_inc(ph["u_level"], 1)
                    for n in range(C):
                        for z in range(2):
                            dve.wait_ge(ph[f"u_made_{z}"], n + 1)
                            if n:
                                dve.wait_ge(ph[f"state_made_{z}"], n)
                                if order[z][n - 1] < XC:
                                    dve.wait_ge(ph[f"y_made_{z}"], n - XC)
                            dve.tensor_copy(Us[z], psum[:, 4 * z + 1, 0:BD]).then_inc(ph[f"u_{z}"], 1)
                        for z in range(2):
                            if n == C - 1:
                                continue
                            c = order[z][n]
                            dve.wait_ge(ph[f"state_made_{z}"], n + 1)
                            if c < XC:
                                dve.wait_ge(ph[f"y_made_{z}"], n - XC + 1)
                            if n == 0:
                                dve.tensor_scalar(St[z], psum[:, 4 * z + 2, 0:BD], Dt[:, z, c:c + 1], None, ALU.mult).then_inc(ph[f"state_{z}"], 1)
                            else:
                                dve.wait_ge(ph[f"ds_{z}"], n)
                                dve.scalar_tensor_tensor(out=St[z], in0=psum[:, 4 * z + 2, 0:BD], scalar=Dt[:, z, c:c + 1], in1=DS[z],
                                                         op0=ALU.mult, op1=ALU.add).then_inc(ph[f"state_{z}"], 1)
                    for z in range(2):
                        dve.wait_ge(ph[f"y_made_{z}"], XC)
                    dve.tensor_copy(cen, psum[:, 3, 0:S]).then_inc(ph["y_half"], 1)
                    dve.wait_ge(ph["y_half"], 1)
                    dve.tensor_tensor(y, psum[:, 7, 0:S], cen, ALU.add).then_inc(ph["y_ready"], 1)
                    dve.wait_ge(ph["mean_made"], 1)
                    dve.wait_ge(ph["y_ready"], 1)
                    yn = E3[:, 0:S]
                    dve.tensor_tensor(yn, y, psum[:, 0, 0:S], ALU.subtract).then_inc(ph["centred"], 1)
                    dve.wait_ge(ph["centred"], 1)
                    dve.tensor_tensor(y, yn, yn, ALU.mult).then_inc(ph["squared"], 1)
                    dve.wait_ge(ph["rooted"], 1)
                    dve.reciprocal(y, cen).then_inc(ph["gn_inverse"], 1)
                    dve.wait_ge(ph["gn_inverse"], 1)
                    dve.tensor_tensor(yn, yn, y, ALU.mult).then_inc(ph["gn_scaled"], 1)
                    dve.wait_ge(ph["bonus_made"], 1)
                    dve.tensor_tensor(cen, psum[:, 2, 0:S], V[:, :], ALU.mult).then_inc(ph["bonus_ready"], 1)
                    dve.wait_ge(ph["gn_scaled"], 1)
                    dve.tensor_scalar(yn, yn, col(LNW), col(LNB), ALU.mult, ALU.add).then_inc(ph["gn_scaled"], 1)
                    dve.wait_ge(ph["gn_scaled"], 2)
                    dve.wait_ge(ph["bonus_ready"], 1)
                    dve.tensor_tensor(yn, yn, cen, ALU.add).then_inc(ph["gn_scaled"], 1)
                    dve.wait_ge(ph["gn_scaled"], 3)
                    dve.tensor_tensor(uT[:, bass.ds(i, 1), :].rearrange("p a s -> p (a s)"), yn, G[:, :], ALU.mult).then_inc(ph["u_out"], 1)

    def rwkv_layer(self):
        a = self.a
        self.adaln(0, 2)
        with ExitStack() as ctx:
            sb = self.scratch(ctx)
            uT = sb(ET, S)
            with ExitStack() as inner:
                sb = self.scratch(inner)
                mu, prm = sb(6 * KT), sb(9 * ET)
                mix = {"r": sb(KT, S), "k": sb(KT, 2 * S), "v": sb(KT, 2 * S), "g": sb(KT, S)}
                lora = {"w": sb(2 * S), "a": sb(2 * S)}

                def rows(name):
                    v = a[name]
                    if len(v.shape) == 2:
                        v = v.rearrange("a b -> (a b)")
                    return v.rearrange("(n p) -> n p", p=P)
                self.turn_rows([rows("l0_mu")], mu)
                self.turn_rows([rows("l0_" + n) for n in ("w0", "a0", "k_k", "k_a", "r_k", "ln_w", "ln_b")], prm)
                with ExitStack() as early:
                    ctx_x = self.scratch(early)(NT, D)
                    with self.phase() as ph:
                        @ph.block.sync
                        def _(sp):
                            sp.dma_start(ctx_x[:, :, :], a["ctx"][0].rearrange("(t p) d -> p t d", p=P)).then_inc(ph["ctx_in"], 16)
                            sp.wait_ge(ph["ctx_in"], 16)
                    self.norm_first(self.x, 0, 0)
                    self.norm_first(ctx_x, 1, S)
                self.rwkv_mixes(mix, lora, mu)
                with ExitStack() as cst:
                    sb = self.scratch(cst)
                    self.strict, self.level, self.no_start = sb(2, 3 * P), sb(2, 6, P), sb(2 * S)
                    self.same_head, self.head_mean, self.gn_eps = sb(P), sb(P), sb(1)
                    with self.phase() as ph:
                        @ph.block.sync
                        def _(sp):
                            for dst, name in ((self.strict[:, :, :], "k_strict"), (self.level[:, :, :, :], "k_level"), (self.no_start[:, :], "k_no_start"),
                                              (self.same_head[:, :], "k_same_head"), (self.head_mean[:, :], "k_head_mean")):
                                sp.dma_start(dst, a[name]).then_inc(ph["constants_in"], 16)
                            sp.wait_ge(ph["constants_in"], 80)

                        @ph.block.vector
                        def _(dve):
                            dve.memset(self.gn_eps[:, :], GN_EPS).then_inc(ph["eps_set"], 1)
                            dve.wait_ge(ph["eps_set"], 1)
                    prm3 = prm[:, :].rearrange("p (j e) -> p j e", e=ET)
                    with self.nc.Fori(0, ET) as i:
                        self.rwkv_heads(i, mix, lora, prm3, uT)
            self.out_first(0, uT)

    def hyena_hidden(self, hdn):
        a, psum = self.a, self.psum
        W = HW
        TWO_PI, ROUND = float(2 * np.pi), 1.5 * 2.0 ** 23
        LIMIT = 3.1415925
        with ExitStack() as ctx:
            sb = self.scratch(ctx)
            z, w1, w23 = sb(S), sb(W), sb(2, W)
            b, turns = sb(4), sb(S)
            with self.phase() as ph:
                @ph.block.sync
                def _(sp):
                    sp.dma_start(z[0:EMB, :], a["k_pos"]).then_inc(ph["hidden_in"], 16)
                    sp.dma_start(w1[0:EMB, :], a["l1_f_w1"]).then_inc(ph["hidden_in"], 16)
                    for j, name in enumerate(("l1_f_w2", "l1_f_w3")):
                        sp.dma_start(w23[0:W, j, :], a[name]).then_inc(ph["hidden_in"], 16)
                    with self.nc.allow_non_contiguous_dma(reason="64-element vectors"):
                        for j, name in enumerate(("l1_f_b1", "l1_f_b2", "l1_f_b3", "l1_sin_freq")):
                            sp.dma_start(b[0:W, j:j + 1], a[name].rearrange("(p a) -> p a", a=1)).then_inc(ph["hidden_in"], 16)

                @ph.block.tensor
                def _(pe):
                    pe.wait_ge(ph["hidden_in"], 16 * 8)
                    pe.matmul(psum[0:W, 0, 0:S], w1[0:EMB, :], z[0:EMB, :], start=True, stop=True).then_inc(ph["layer_made"], 1)
                    for j in range(2):
                        pe.wait_ge(ph["layer_ready"], j + 1)
                        pe.matmul(psum[0:W, j + 1, 0:S], w23[0:W, j, :], hdn[0:W, :], start=True, stop=True).then_inc(ph["layer_made"], 1)

                @ph.block.vector
                def _(dve):
                    dve.wait_ge(ph["hidden_in"], 16 * 8)
                    h, t = hdn[0:W, :], turns[0:W, :]
                    n = 0

                    def chained(ins):
                        nonlocal n
                        n += 1
                        ins.then_inc(ph["reduced"], 1)
                        dve.wait_ge(ph["reduced"], n)
                    for j in range(3):
                        dve.wait_ge(ph["layer_made"], j + 1)
                        chained(dve.tensor_scalar(h, psum[0:W, j, 0:S], b[0:W, j:j + 1], b[0:W, 3:4], ALU.add, ALU.mult))
                        chained(dve.tensor_scalar(t, h, 1.0 / TWO_PI, ROUND, ALU.mult, ALU.add))
                        chained(dve.tensor_scalar(t, t, -ROUND, -TWO_PI, ALU.add, ALU.mult))
                        chained(dve.tensor_tensor(h, h, t, ALU.add))
                        dve.tensor_scalar(h, h, LIMIT, -LIMIT, ALU.min, ALU.max).then_inc(ph["angle_ready"], 1)
                        dve.wait_ge(ph["layer_ready"], j + 1)

                @ph.block.scalar
                def _(act):
                    for j in range(3):
                        act.wait_ge(ph["angle_ready"], j + 1)
                        act.activation(hdn[0:W, :], hdn[0:W, :], ACT.Sin).then_inc(ph["layer_ready"], 1)

    def hyena_tiles(self, i, U, hdn, prm, dft, idft, uT):
        a, psum, hT, ident = self.a, self.psum, self.hT, self.ident
        with ExitStack() as ctx:
            sb = self.scratch(ctx)
            cur = sb(U, 13)
            fw, win = [sb(2, P) for _ in range(2)], [sb(NT, P) for _ in range(2)]
            pad = [sb(3, S + 2) for _ in range(2)]
            gate, conv = [sb(S) for _ in range(2)], [sb(3, S) for _ in range(2)]
            ut = [sb(NT, P) for _ in range(2)]
            hw, fsum, fdif = sb(NT, 2, P), sb(NT, P), sb(NT, P)
            AB, m1, m2, Y, Yf = sb(2, S), sb(2, S), sb(2, S), sb(2, S), sb(4, P)
            long = sb(S)
            w = self.ring[:, :, :].rearrange("p s (k j n) -> p s k j n", j=4, n=P)
            COL = (2, 1, 0, 3)
            assert U <= SLOTS
            with self.phase() as ph:
                @ph.block.sync
                def _(sp):
                    wv = a["l1_w_in"].rearrange("(k p) n -> p k n", p=P)
                    for u in range(U):
                        ct = i * U + u
                        for j in range(4):
                            sp.dma_start(w[:, u, :, j, :], wv[:, :, bass.ds(ct * P + COL[j] * E, P)]).then_inc(ph[f"w_in_{u}_{j // 2}"], 16)
                        if u >= 2:
                            sp.wait_ge(ph["filter_made"], u - 1)
                            sp.wait_ge(ph["windowed"], u - 1)
                        sp.dma_start(fw[u % 2][0:HW, :, :], a["l1_f_w4"].rearrange("p (b n) -> p b n", b=2)[:, :, bass.ds(ct * P, P)]).then_inc(ph[f"filter_in_{u}"], 16)
                        sp.dma_start(win[u % 2][:, :, :], a["k_window"].rearrange("(t p) n -> p t n", p=P)[:, :, bass.ds(ct * P, P)]).then_inc(ph[f"filter_in_{u}"], 16)

                @ph.block.tensor
                def _(pe):
                    def piece(u, j):
                        if u >= U:
                            return
                        bank = 2 * (u % 2) + j // 2
                        pe.wait_ge(ph[f"w_in_{u}_{j // 2}"], 32)
                        if u >= 2 and j % 2 == 0:
                            pe.wait_ge(ph["copied"], 3 * (u - 2) + (1, 3)[j // 2])
                        for k in range(KT):
                            mm = pe.matmul(psum[:, bank, (j % 2) * S:(j % 2 + 1) * S], w[:, u, k, j, :], hT[:, k, 0:S], start=(k == 0), stop=(k == KT - 1))
                        mm.then_inc(ph["proj_ready"], 1)
                    for j in range(4):
                        piece(0, j)
                    for u in range(U):
                        pe.wait_ge(ph[f"filter_in_{u}"], 32)
                        if u:
                            pe.wait_ge(ph["yf_ready"], u)
                        for t in range(NT):
                            mm = pe.matmul(psum[:, 4, t * S:(t + 1) * S], hdn[0:HW, t * P:(t + 1) * P], fw[u % 2][0:HW, :, :].rearrange("p b n -> p (b n)"),
                                           start=True, stop=True)
                        mm.then_inc(ph["filter_made"], 1)
                        piece(u + 1, 0)
                        pe.wait_ge(ph["product_ready"], u + 1)
                        if u:
                            pe.wait_ge(ph["long_read"], u)
                        for t in range(NT):
                            mm = pe.transpose(psum[:, 5, t * P:(t + 1) * P], conv[u % 2][:, 0, t * P:(t + 1) * P], ident[:, :])
                        mm.then_inc(ph["ut_made"], 1)
                        piece(u + 1, 1)
                        pe.wait_ge(ph["fsum_ready"], u + 1)
                        pe.wait_ge(ph["fdif_ready"], u + 1)
                        pe.wait_ge(ph["ut_ready"], u + 1)
                        if u:
                            pe.wait_ge(ph["cd_read"], 2 * u)
                        for src, o in ((fsum, 0), (fdif, S)):
                            for t in range(NT):
                                mm = pe.matmul(psum[:, 7, o:o + S], src[:, t, :], dft[:, t, o:o + S], start=(t == 0), stop=(t == NT - 1))
                        mm.then_inc(ph["cd_made"], 1)
                        for t in range(NT):
                            mm = pe.matmul(psum[:, 6, :], ut[u % 2][:, t, :], dft[:, t, :], start=(t == 0), stop=(t == NT - 1))
                        mm.then_inc(ph["ab_made"], 1)
                        piece(u + 1, 2)
                        pe.wait_ge(ph["spectrum_ready"], 2 * u + 2)
                        for q in range(4):
                            mm = pe.transpose(psum[:, 4, q * P:(q + 1) * P], Y[:, q // 2, (q % 2) * P:(q % 2 + 1) * P], ident[:, :])
                        mm.then_inc(ph["yf_made"], 1)
                        piece(u + 1, 3)
                        pe.wait_ge(ph["yf_ready"], u + 1)
                        for q in range(4):
                            mm = pe.matmul(psum[:, 5, S:2 * S], Yf[:, q, :], idft[:, q, :], start=(q == 0), stop=(q == 3))
                        mm.then_inc(ph["long_made"], 1)

                @ph.block.scalar
                def _(act):
                    def load(u):
                        if u >= U:
                            return
                        b, d = 2 * (u % 2), u % 2
                        act.wait_ge(ph["edges"], 2)
                        act.wait_ge(ph["proj_ready"], 4 * u + 2)
                        if u >= 2:
                            act.wait_ge(ph["tile_done"], u - 1)
                        act.activation(pad[d][:, 0:2, 1:S + 1], psum[:, b, :].rearrange("p (j s) -> p j s", j=2), ACT.Copy).then_inc(ph["copied"], 1)
                        act.wait_ge(ph["proj_ready"], 4 * u + 4)
                        act.activation(pad[d][:, 2, 1:S + 1], psum[:, b + 1, 0:S], ACT.Copy).then_inc(ph["copied"], 1)
                        act.activation(gate[d][:, :], psum[:, b + 1, S:2 * S], ACT.Silu).then_inc(ph["copied"], 1)
                    load(0)
                    for u in range(U):
                        act.wait_ge(ph["ut_made"], u + 1)
                        act.activation(ut[u % 2][:, :, :], psum[:, 5, 0:S].rearrange("p (t n) -> p t n", t=NT), ACT.Copy).then_inc(ph["ut_ready"], 1)
                        act.wait_ge(ph["ab_made"], u + 1)
                        if u:
                            act.wait_ge(ph["cd_read"], 2 * u)
                        act.activation(AB[:, :, :], psum[:, 6, :].rearrange("p (q s) -> p q s", q=2), ACT.Copy).then_inc(ph["ab_ready"], 1)
                        act.wait_ge(ph["yf_made"], u + 1)
                        if u:
                            act.wait_ge(ph["long_made"], u)
                        act.activation(Yf[:, :, :], psum[:, 4, :].rearrange("p (q n) -> p q n", q=4), ACT.Copy).then_inc(ph["yf_ready"], 1)
                        load(u + 1)

                @ph.block.gpsimd
                def _(pool):
                    for d in range(2):
                        pool.memset(pad[d][:, :, 0:S + 2:S + 1], 0.0).then_inc(ph["edges"], 1)

                @ph.block.vector
                def _(dve):
                    for u in range(U):
                        dve.tensor_copy(cur[:, u, :], prm[:, :, bass.ds(i * U + u, 1)].rearrange("p j a -> p (j a)")).then_inc(ph["cur_ready"], 1)
                    dve.wait_ge(ph["cur_ready"], U)
                    for u in range(U):
                        d = u % 2
                        dve.wait_ge(ph["filter_made"], u + 1)
                        dve.wait_ge(ph[f"filter_in_{u}"], 32)
                        dve.tensor_tensor(hw[:, :, :, :], psum[:, 4, :].rearrange("p (t b n) -> p t b n", t=NT, b=2),
                                          win[d][:, :, :].unsqueeze(2).to_broadcast([P, NT, 2, P]), ALU.mult).then_inc(ph["windowed"], 1)
                        dve.wait_ge(ph["windowed"], u + 1)
                        if u:
                            dve.wait_ge(ph["cd_made"], u)
                        dve.tensor_tensor(fsum[:, :, :], hw[:, :, 0, :], hw[:, :, 1, :], ALU.add).then_inc(ph["fsum_ready"], 1)
                        dve.tensor_tensor(fdif[:, :, :], hw[:, :, 1, :], hw[:, :, 0, :], ALU.subtract).then_inc(ph["fdif_ready"], 1)
                        for j in range(3):
                            if j < 2:
                                dve.wait_ge(ph["copied"], 3 * u + 1)
                            else:
                                dve.wait_ge(ph["copied"], 3 * u + 2)
                            tap = [cur[:, u, 3 * q + COL[j]:3 * q + COL[j] + 1] for q in range(4)]
                            dve.tensor_scalar(conv[d][:, j, :], pad[d][:, j, 1:S + 1], tap[1], tap[3], ALU.mult, ALU.add).then_inc(ph["taps"], 1)
                        for q, o in ((0, 0), (2, 2)):
                            for j in range(3):
                                dve.wait_ge(ph["taps"], 9 * u + (3 if q else 0) + j + 1)
                                tap = cur[:, u, 3 * q + COL[j]:3 * q + COL[j] + 1]
                                dve.scalar_tensor_tensor(out=conv[d][:, j, :], in0=pad[d][:, j, o:o + S], scalar=tap, in1=conv[d][:, j, :],
                                                         op0=ALU.mult, op1=ALU.add).then_inc(ph["taps"], 1)
                        dve.wait_ge(ph["taps"], 9 * u + 8)
                        dve.tensor_tensor(conv[d][:, 0, :], conv[d][:, 0, :], conv[d][:, 1, :], ALU.mult).then_inc(ph["product_ready"], 1)
                        dve.wait_ge(ph["ab_ready"], u + 1)
                        dve.wait_ge(ph["cd_made"], u + 1)
                        if u:
                            dve.wait_ge(ph["spectrum_ready"], 2 * u)
                        for m, o in ((m1, 0), (m2, S)):
                            dve.tensor_tensor(m[:, :, :], AB[:, :, :], psum[:, 7, o:o + S].unsqueeze(1).to_broadcast([P, 2, S]), ALU.mult).then_inc(ph["cd_read"], 1)
                        dve.wait_ge(ph["cd_read"], 2 * u + 2)
                        if u:
                            dve.wait_ge(ph["yf_made"], u)
                        dve.tensor_tensor(Y[:, 0, :], m1[:, 0, :], m2[:, 1, :], ALU.add).then_inc(ph["spectrum_ready"], 1)
                        dve.tensor_tensor(Y[:, 1, :], m2[:, 0, :], m1[:, 1, :], ALU.subtract).then_inc(ph["spectrum_ready"], 1)
                        dve.wait_ge(ph["product_ready"], u + 1)
                        dve.wait_ge(ph["long_made"], u + 1)
                        dve.scalar_tensor_tensor(out=long[:, :], in0=conv[d][:, 0, :], scalar=cur[:, u, 12:13], in1=psum[:, 5, S:2 * S],
                                                 op0=ALU.mult, op1=ALU.add).then_inc(ph["long_read"], 1)
                        dve.wait_ge(ph["long_read"], u + 1)
                        dve.wait_ge(ph["taps"], 9 * u + 9)
                        dve.tensor_tensor(long[:, :], long[:, :], conv[d][:, 2, :], ALU.mult).then_inc(ph["long_gated"], 1)
                        dve.wait_ge(ph["long_gated"], u + 1)
                        dve.wait_ge(ph["copied"], 3 * u + 3)
                        dve.tensor_tensor(uT[:, bass.ds(i * U + u, 1), :].rearrange("p a s -> p (a s)"), long[:, :], gate[d][:, :], ALU.mult).then_inc(ph["tile_done"], 1)
                        dve.wait_ge(ph["tile_done"], u + 1)

    def hyena_layer(self):
        a = self.a
        U = 4
        self.adaln(1, 1)
        self.norm_first(self.x, 0, 0)
        with ExitStack() as ctx:
            sb = self.scratch(ctx)
            uT = sb(ET, S)
            with ExitStack() as inner:
                sb = self.scratch(inner)
                prm, hdn = sb(13 * ET), sb(S)
                dft, idft = sb(NT, 2 * S), sb(4, S)

                def rows(name):
                    v = a[name]
                    if len(v.shape) == 2:
                        v = v.rearrange("a b -> (a b)")
                    return v.rearrange("(n p) -> n p", p=P)
                self.turn_rows([rows("l1_" + n) for n in ("conv_w", "conv_b", "filter_bias")], prm)
                self.hyena_hidden(hdn)
                with self.phase() as ph:
                    @ph.block.sync
                    def _(sp):
                        sp.dma_start(dft[:, :, :], a["k_dft"]).then_inc(ph["dft_in"], 16)
                        sp.dma_start(idft[:, :, :], a["k_idft"]).then_inc(ph["dft_in"], 16)
                        sp.wait_ge(ph["dft_in"], 32)
                prm3 = prm[:, :].rearrange("p (j e) -> p j e", e=ET)
                with self.nc.Fori(0, ET // U) as i:
                    self.hyena_tiles(i, U, hdn, prm3, dft, idft, uT)
            self.out_first(1, uT)


def build(nc, a, out, parts=("first", "second")):
    with ExitStack() as ctx:
        prog = Program(nc, ctx, a, out)
        prog.load_start()
        if "rwkv" in parts or "first" in parts:
            prog.rwkv_layer()
        if "hyena" in parts or "first" in parts:
            prog.hyena_layer()
        if "second" in parts or "ffn" in parts or "mixer" in parts:
            with nc.Fori(0, 2 if "second" in parts else 1) as l:
                if "mixer" not in parts:
                    prog.ffn(l, "ffn1_norm_2", "ffn1_w_gate_2", "ffn1_w_up_2", "ffn1_w_down_2")
                if "ffn" not in parts:
                    prog.mixer(l)
                if "second" in parts:
                    prog.ffn(l, "ffn2_norm_2", "ffn2_w_gate_2", "ffn2_w_up_2", "ffn2_w_down_2")
        prog.finish("second" in parts)


def constants():
    f = np.float32
    pos = np.arange(S, dtype=f)
    half = P // 2
    inv = (f(10000.0) ** (-np.arange(half, dtype=f) / f(half))).astype(f)
    ang = pos[:, None] * inv[None, :]
    cos = np.concatenate([np.cos(ang)] * 2, 1)
    sin = np.concatenate([-np.sin(ang), np.sin(ang)], 1)
    rope = np.stack([np.stack([cos, sin]), np.stack([cos, sin]) * P ** -0.5])
    log_g = np.log1p(-np.exp2(-5.0 - np.arange(CHEADS, dtype=np.float64)))
    idx = np.arange(P)
    diff = idx[None, :] - idx[:, None]
    decay = np.where(diff[:, None, :] >= 0, np.exp(log_g[None, :, None] * np.maximum(diff, 0)[:, None, :]), 0.0)
    t = np.arange(P)
    j, h = t % CH, t // CH
    same = h[:, None] == h[None, :]
    before = np.stack([j[:, None] < j[None, :], j[:, None] > j[None, :]])
    upto = np.stack([j[:, None] <= j[None, :CH], j[:, None] >= j[None, :CH]])
    strict = np.concatenate([before & same, before & same, upto, upto], 2)
    level = np.stack([np.stack([b & same & (j[:, None] // m // 2 == j[None, :] // m // 2) & (j[:, None] // m != j[None, :] // m)
                                for m in (1, 2, 4, 8, 16, 32)]) for b in before])
    no_start = np.broadcast_to(np.arange(2 * S) % CH != 0, (P, 2 * S))
    tt = np.linspace(0.0, 1.0, S)
    bands = (EMB - 1) // 2
    turn = (2.0 * np.pi / S) * np.arange(S)[:, None] * np.linspace(1e-4, bands - 1, bands)[None, :]
    pos_features = np.concatenate([tt[:, None], np.cos(turn), -np.sin(turn)], 1)
    deltas = np.abs(np.linspace(np.log(1e-2) / 1.5, np.log(1e-2) / 0.3, E))
    omega = np.pi / S * np.arange(S)[:, None] * (np.arange(S) + 0.5)[None, :]
    dft = np.concatenate([np.cos(omega), np.sin(omega)], 1)
    idft = np.concatenate([np.cos(omega), -np.sin(omega)], 1).T / S
    return {
        "k_pos": np.ascontiguousarray(pos_features.T).astype(f),
        "k_window": np.exp(-tt[:, None] * deltas[None, :]).astype(f),
        "k_dft": np.ascontiguousarray(dft.reshape(NT, P, 2 * S).transpose(1, 0, 2)).astype(f),
        "k_idft": np.ascontiguousarray(idft.reshape(4, P, S).transpose(1, 0, 2)).astype(f),
        "k_strict": strict.transpose(1, 0, 2).astype(f),
        "k_level": level.transpose(2, 0, 1, 3).astype(f),
        "k_no_start": no_start.astype(f),
        "k_same_head": same.astype(f),
        "k_head_mean": (same / CH).astype(f),
        "k_ident": np.eye(P, dtype=f),
        "k_rope": np.ascontiguousarray(rope.reshape(2, 2, NT, P, P).transpose(3, 0, 1, 2, 4)).astype(f),
        "k_decay": decay.astype(f),
        "k_xi": np.broadcast_to(np.exp(log_g[:, None] * (idx + 1.0)), (P, CHEADS, P)).astype(f),
        "k_zeta": np.exp(log_g[None, :] * (P - 1 - idx)[:, None]).astype(f),
        "k_causal": (diff >= 0).astype(f),
    }


_INS = ["x", "c", "ctx", "c_ctx", "ada_w", "ada_b", "norm_pre", "norm_post", "w_out",
        "l0_w_in", "l0_mu", "l0_w0", "l0_w2", "l0_a0", "l0_a2", "l0_k_k", "l0_k_a", "l0_r_k", "l0_ln_w", "l0_ln_b",
        "l1_w_in", "l1_conv_w", "l1_conv_b", "l1_f_w1", "l1_f_b1", "l1_f_w2", "l1_f_b2", "l1_f_w3", "l1_f_b3", "l1_f_w4",
        "l1_sin_freq", "l1_filter_bias", "ffn1_norm_2", "ffn1_w_gate_2", "ffn1_w_up_2", "ffn1_w_down_2", "mix_norm_2",
        "w_in_2", "gmlp_v_norm_2", "gmlp_w_s_2", "gmlp_b_s_2", "conv_w_2", "ret_gn_2", "w_out_2", "ffn2_norm_2",
        "ffn2_w_gate_2", "ffn2_w_up_2", "ffn2_w_down_2", "final_norm_2"]


def kernel(**inputs):
    import concourse.bacc as bacc
    from concourse.bass_utils import run_bass_kernel_spmd

    nc = bacc.Bacc("TRN2", target_bir_lowering=False, num_devices=1)
    arrays, a = {}, {}
    given = {n: np.ascontiguousarray(inputs[n]) for n in _INS}
    for name, v in {**given, **constants()}.items():
        arrays[f"in_{name}"] = v
        a[name] = nc.dram_tensor(f"in_{name}", v.shape, mybir.dt.from_np(v.dtype), kind="ExternalInput").ap()
    out = nc.dram_tensor("out_0", (1, S, D), F32, kind="ExternalOutput").ap()
    build(nc, a, out)
    r = run_bass_kernel_spmd(nc, [arrays], core_ids=[0])
    return r.results[0]["out_0"]
```

```python
from contextlib import ExitStack

import numpy as np

import concourse.bass as bass
from concourse import mybir

ALU = mybir.AluOpType
ACT = mybir.ActivationFunctionType
AX = mybir.AxisListType
F32 = mybir.dt.float32
F32R = mybir.dt.float32r

P = 128
D = 1024
KT = D // P
S = 256
NT = S // P
E = 2 * D
ET = E // P
HEAD = 64
LORA = 64
FF = 2816
FT = FF // P
WIDE = 512
EPS = 1e-6
GN_EPS = 64e-5
CH = 64
AW = 256
CW = 512
CHEADS = 4
PROJ = 2 * AW + 3 * AW + 4 * CW
EMB, HW = 33, 64
SLOTS = 4
SMALL = 16 * 14


class Phase:

    def __init__(self, nc, pool):
        self.nc, self.pool, self.used = nc, pool, {}
        self.stack = ExitStack()

    def __enter__(self):
        self.block = self.stack.enter_context(self.nc.Block())
        return self

    def __getitem__(self, name):
        if name not in self.used:
            self.used[name] = self.pool[len(self.used)]
        return self.used[name]

    def __exit__(self, *exc):
        self.stack.__exit__(*exc)
        if exc[0] is None:
            if self.used:
                self.nc.sync.sem_clear(range(self.pool[0].num, self.pool[len(self.used) - 1].num + 1))
            self.nc.all_engine_barrier()
        return False


class Ring:

    def __init__(self, ph, buf):
        self.ph, self.buf, self.pieces = ph, buf, []
        self.counts = [0] * SLOTS

    def load(self, sp, parts, free):
        i = len(self.pieces)
        slot = i % SLOTS
        if i >= SLOTS:
            sp.wait_ge(*free)
        for dst, src in parts(self.buf[:, slot, :]):
            sp.dma_start(dst, src).then_inc(self.ph[f"panel_landed_{slot}"], 16)
            self.counts[slot] += 16
        self.pieces.append(self.counts[slot])

    def wait(self, pe, i):
        pe.wait_ge(self.ph[f"panel_landed_{i % SLOTS}"], self.pieces[i])
        return self.buf[:, i % SLOTS, :]


def chan(v):
    return v.rearrange("(k p) -> p k", p=P)


class Program:
    def __init__(self, nc, ctx, a, out):
        self.nc, self.a, self.out, self.n = nc, a, out, 0

        def sb(name, *shape):
            return ctx.enter_context(nc.sbuf_tensor(name, [P, *shape], F32))

        self.sems = [ctx.enter_context(nc.semaphore(f"s{i}")) for i in range(90)]
        self.psum = ctx.enter_context(nc.psum_tensor("psum", [P, 8, WIDE], F32))
        self.ring = sb("ring", SLOTS, KT * WIDE)
        self.x = sb("x", NT, D)
        self.xn = sb("xn", NT, D)
        self.hT = sb("hT", KT, 2 * S)
        self.ident = sb("ident", P)
        self.half = sb("half", 16)
        self.ss = sb("ss", 8)
        self.ms = sb("ms", 8)
        self.rstd = sb("rstd", 8)
        self.gain = sb("gain", KT)
        self.cond = sb("cond", KT, 2)
        self.shift, self.scale = sb("shift", 2, KT), sb("scale", 2, KT)
        self.post = sb("post", D)
        self.ones = sb("ones", P)

    def phase(self):
        return Phase(self.nc, self.sems)

    def scratch(self, ctx):
        def sb(*shape):
            self.n += 1
            return ctx.enter_context(self.nc.sbuf_tensor(f"scratch{self.n}", [P, *shape], F32))
        return sb

    def split_pair(self, ctx, *shape):
        self.n += 1
        return [ctx.enter_context(self.nc.sbuf_tensor(f"part{self.n}{c}", [P, *shape], F32R)) for c in "hl"]

    def load_start(self):
        nc = self.nc
        with self.phase() as ph:
            @ph.block.sync
            def _(sp):
                sp.dma_start(self.x[:, :, :], self.a["x"][0].rearrange("(t p) d -> p t d", p=P)).then_inc(ph["start"], 16)
                sp.dma_start(self.ident[:, :], self.a["k_ident"]).then_inc(ph["start"], 16)
                sp.wait_ge(ph["start"], 32)

            @ph.block.vector
            def _(dve):
                dve.memset(self.half[:, :], -0.5).then_inc(ph["constants_set"], 1)
                dve.memset(self.ones[:, :], 1.0).then_inc(ph["constants_set"], 1)
                dve.wait_ge(ph["constants_set"], 2)

            @ph.block.scalar
            def _(act):
                with nc.allow_non_contiguous_dma(reason="the two condition vectors, once"):
                    act.dma_start(self.cond[:, :, 0], chan(self.a["c"][0])).then_inc(ph["cond_in"], 16)
                    act.dma_start(self.cond[:, :, 1], chan(self.a["c_ctx"])).then_inc(ph["cond_in"], 16)
                act.wait_ge(ph["cond_in"], 32)
                act.activation(self.cond[:, :, :], self.cond[:, :, :], ACT.Silu).then_inc(ph["cond_ready"], 1)

    def norm_dve_stats(self, ph, dve, x, n=NT):
        for t in range(n):
            dve.tensor_tensor_reduce(out=self.xn[:, t, :], in0=x[:, t, :], in1=x[:, t, :], scale=1.0, scalar=0.0,
                                     op0=ALU.mult, op1=ALU.add, accum_out=self.ss[:, t:t + 1]).then_inc(ph["squares"], 1)
        dve.wait_ge(ph["squares"], n)
        dve.tensor_scalar(self.ms[:, 0:n], self.ss[:, 0:n], 1.0 / D, EPS, ALU.mult, ALU.add).then_inc(ph["mean_square"], 1)

    def norm_pool(self, ph, pool, n=NT):
        pool.wait_ge(ph["mean_square"], 1)
        pool.tensor_tensor(self.rstd[:, 0:n], self.ms[:, 0:n], self.half[:, 0:n], ALU.pow).then_inc(ph["rstd_ready"], 1)

    def norm_dve_scale(self, ph, dve, x, n=NT):
        dve.wait_ge(ph["rstd_ready"], 1)
        for t in range(n):
            dve.tensor_scalar(self.xn[:, t, :], x[:, t, :], self.rstd[:, t:t + 1], None, ALU.mult).then_inc(ph["xn_ready"], 1)

    def norm_pe(self, ph, pe, bank=4):
        pe.wait_ge(ph["xn_ready"], NT)
        for k in range(KT):
            for t in range(NT):
                mm = pe.transpose(self.psum[:, bank + k // 2, (k % 2) * S + t * P:(k % 2) * S + (t + 1) * P],
                                  self.xn[:, t, k * P:(k + 1) * P], self.ident[:, :])
            mm.then_inc(ph["turned"], 1)

    def norm_act(self, ph, act, scale, bias=None, bank=4, at=0):
        for k in range(KT):
            if k // 2 % 2 == 0:
                act.wait_ge(ph["turned"], (k // 2 + 1) * 2)
                act.activation(self.hT[:, k, at:at + S], self.psum[:, bank + k // 2, k % 2 * S:(k % 2 + 1) * S], ACT.Identity,
                               scale=scale[:, k:k + 1], bias=bias[:, k:k + 1] if bias is not None else 0.0).then_inc(ph["h_even"], 1)

    def norm_dve_turn(self, ph, dve, scale, bias=None, bank=4, at=0):
        for k in range(KT):
            if k // 2 % 2 == 1:
                dve.wait_ge(ph["turned"], (k // 2 + 1) * 2)
                src = self.psum[:, bank + k // 2, k % 2 * S:(k % 2 + 1) * S]
                if bias is None:
                    ins = dve.tensor_scalar(self.hT[:, k, at:at + S], src, scale[:, k:k + 1], None, ALU.mult)
                else:
                    ins = dve.tensor_scalar(self.hT[:, k, at:at + S], src, scale[:, k:k + 1], bias[:, k:k + 1], ALU.mult, ALU.add)
                ins.then_inc(ph["h_odd"], 1)

    def norm_wait(self, ph, eng):
        eng.wait_ge(ph["h_even"], KT // 2)
        eng.wait_ge(ph["h_odd"], KT // 2)

    def mixer(self, l):
        a, psum, hT, ident = self.a, self.psum, self.hT, self.ident
        kp = "a (k p) n -> p (a k) n"
        order = [1280, 1792, 2304, 2816, 0, 512, 1024]
        width = [WIDE] * 6 + [AW]
        with ExitStack() as ctx:
            sb = self.scratch(ctx)
            rope = sb(2, 2, NT, P)
            gain_c, gain_a = sb(CW), sb(AW)
            decay, xi, zeta = sb(CHEADS, P), sb(CHEADS, P), sb(CHEADS)
            causal, w_s, wsT, b_s = sb(P), sb(4, P), sb(4, P), sb(2, P)
            conv = sb(2, 3)
            m1, m2 = self.post[:, 0:CW], self.post[:, CW:2 * CW]
            qk = sb(2, NT, CW)
            qkT = hT[:, :, S:2 * S].rearrange("p (i h) s -> p i h s", i=2)
            qx = sb(CHEADS, P)
            kz, kv = sb(CW), sb(CW)
            v, sg = sb(NT, CW), sb(NT, CW)
            pT = self.xn[:, :, 0:CW].rearrange("p t (h s) -> p t h s", h=CHEADS)
            bn, mv = sb(16, 6), sb(16, 2)
            var, rs = sb(16), sb(16)
            ret = self.xn[:, :, CW:2 * CW]
            uT, va = sb(2, S), sb(NT, AW)
            bcx = sb(6, S)
            z, yb = sb(2, S + 2), sb(2, S)
            yT = qk[:, 0, :, :].rearrange("p t (k s) -> p (t k) s", s=S)
            BUFS = 4
            w_hi, w_lo = self.split_pair(ctx, BUFS, D)
            h_hi, h_lo = self.split_pair(ctx, KT, S)
            y_hi, y_lo = h_hi, h_lo
            IN = 24
            banks_out = (0, 1, 6, 7)

            def source(g):
                if g < 16:
                    i, at = g // 4, slice(g % 4 * 2, g % 4 * 2 + 2)
                    return i, lambda slot: slot.rearrange("p (k n) -> p k n", n=WIDE)[:, at, :]
                if g < IN:
                    i, c = [(4, 0), (4, 1), (5, 0), (5, 1), (5, 2), (5, 3), (6, 0), (6, 1)][g - 16]
                    return i, lambda slot: slot.rearrange("p (k n) -> p k n", n=WIDE)[:, :, c * P:(c + 1) * P]
                return 7 + (g - IN) // 4, lambda slot: slot.rearrange("p (k n) -> p k n", n=D)[:, (g - IN) % 4, :]

            def part(w, g):
                v = w[:, g % BUFS, :]
                return v.rearrange("p (k n) -> p k n", n=WIDE) if g < 16 else v.rearrange("p (k n) -> p k n", n=P) if g < IN else v
            with self.phase() as ph:
                ring = Ring(ph, self.ring)

                @ph.block.sync
                def _(sp):
                    for i, (c, w) in enumerate(zip(order, width)):
                        def parts(slot):
                            yield (slot.rearrange("p (k n) -> p k n", n=WIDE)[:, :, 0:w],
                                   a["w_in_2"][bass.ds(l, 1)].rearrange(kp, p=P)[:, :, c:c + w])
                        ring.load(sp, parts, (ph["w_split"], 4 * (i - SLOTS + 1)))
                    for i in range(2):
                        def parts(slot):
                            yield (slot.rearrange("p (k n) -> p k n", n=D),
                                   a["w_out_2"][bass.ds(l, 1)].rearrange(kp, p=P)[:, 4 * i:4 * i + 4, :])
                        ring.load(sp, parts, [(ph["w_split"], 16), (ph["va_made"], 1)][i])

                @ph.block.scalar
                def _(act):
                    with self.nc.allow_non_contiguous_dma(reason="small vectors"):
                        act.dma_start(self.gain[:, :], a["mix_norm_2"][bass.ds(l, 1)].rearrange("a (k p) -> p (a k)", p=P)).then_inc(ph["gain_in"], 16)
                        loads = [(conv[:, c, :], a["conv_w_2"][bass.ds(l, 1), :, c * P:(c + 1) * P].rearrange("a i p -> p (a i)")) for c in range(2)]
                        loads += [
                            (rope[:, :, :, :, :], a["k_rope"]),
                            (decay[:, :, :], a["k_decay"]), (xi[:, :, :], a["k_xi"]), (zeta[:, :], a["k_zeta"]), (causal[:, :], a["k_causal"]),
                            (w_s[:, :, :], a["gmlp_w_s_2"][bass.ds(l, 1)].rearrange("a g t s -> t (a g) s")),
                            (gain_c[:, :], a["ret_gn_2"][bass.ds(l, 1)].partition_broadcast(P).rearrange("p a n -> p (a n)")),
                            (gain_a[:, :], a["gmlp_v_norm_2"][bass.ds(l, 1)].partition_broadcast(P).rearrange("p a n -> p (a n)"))]
                        for g in range(4):
                            loads.append((b_s[HEAD * (g % 2):HEAD * (g % 2) + HEAD, g // 2, :],
                                          a["gmlp_b_s_2"][bass.ds(l, 1), g, :].partition_broadcast(HEAD).rearrange("p a n -> p (a n)")))
                        for dst, src in loads:
                            act.dma_start(dst, src).then_inc(ph["small_in"], 16)
                    small = 16 * len(loads)
                    assert small == SMALL

                    def round_weights(g):
                        i, view = source(g)
                        w = view(ring.wait(act, i))
                        if g >= BUFS:
                            act.wait_ge(ph["w_used"], g - BUFS + 1)
                        act.activation(part(w_hi, g), w, ACT.Copy).then_inc(ph["w_rounded"], 1)
                    round_weights(0)
                    act.wait_ge(ph["gain_in"], 16)
                    for k in range(KT):
                        act.wait_ge(ph["turned"], (k // 2 + 1) * 2)
                        act.activation(h_hi[:, k, :], psum[:, 4 + k // 2, k % 2 * S:(k % 2 + 1) * S], ACT.Copy, scale=self.gain[:, k:k + 1]).then_inc(ph["h_rounded"], 1)
                    for g in range(1, 16):
                        round_weights(g)
                    for t in range(NT):
                        act.wait_ge(ph["w_used"], 12)
                        act.activation(v[:, t, :], psum[:, t, :], ACT.Copy).then_inc(ph["v_ready"], 1)
                    for g in range(16, 20):
                        round_weights(g)
                    for t in range(NT):
                        act.wait_ge(ph["w_used"], 16)
                        act.activation(sg[:, t, :], psum[:, 2 + t, :], ACT.Silu).then_inc(ph["gate_ready"], 1)
                    for g in range(20, 22):
                        round_weights(g)
                    act.wait_ge(ph["w_used"], 18)
                    act.activation(uT[:, :, :], psum[:, 0, :].rearrange("p (c s) -> p c s", c=2), ACT.Gelu_apprx_tanh).then_inc(ph["u_ready"], 1)
                    round_weights(22)
                    act.wait_ge(ph["va_made"], 1)
                    act.activation(va[:, :, :], psum[:, 1, :].rearrange("p (t n) -> p t n", t=NT), ACT.Gelu_apprx_tanh).then_inc(ph["va_ready"], 1)
                    for i in range(3):
                        for g in ([23], [24, 25], [26, 27])[i]:
                            round_weights(g)
                        act.wait_ge(ph["w_used"], 20 + 2 * i)
                        act.activation(bcx[:, 2 * i:2 * i + 2, :], psum[:, [2, 3, 0][i], :].rearrange("p (c s) -> p c s", c=2), ACT.Copy).then_inc(ph["bcx_ready"], 1)
                    act.wait_ge(ph["ya_ready"], 1)
                    act.activation(y_hi[:, 0:2, :], yT[:, 0:2, :], ACT.Copy).then_inc(ph["y_rounded"], 1)
                    act.wait_ge(ph["yb_ready"], 1)
                    act.activation(y_hi[:, 2:4, :], yT[:, 2:4, :], ACT.Copy).then_inc(ph["y_rounded"], 1)
                    for g in range(28, 32):
                        round_weights(g)
                    for t in range(NT):
                        act.wait_ge(ph["yc_turned"], t + 1)
                        act.activation(y_hi[:, 4:8, t * P:(t + 1) * P], psum[:, 4 + t, :].rearrange("p (h s) -> p h s", h=CHEADS), ACT.Copy).then_inc(ph["y_rounded"], 1)

                @ph.block.gpsimd
                def _(pool):
                    self.norm_pool(ph, pool)
                    pool.memset(z[:, :, 0:2], 0.0).then_inc(ph["z_edge"], 1)
                    pool.wait_ge(ph["small_in"], SMALL)
                    for n, (var_in, out_sem, cnt) in enumerate(((ph["var_a"], ph["rs_a"], 8), (ph["var_c"], ph["rs_c"], 8))):
                        pool.wait_ge(var_in, 1)
                        pool.tensor_tensor(rs[:, 8 * n:8 * n + 8], var[:, 8 * n:8 * n + 8], self.half[:, 0:8], ALU.pow).then_inc(out_sem, 1)

                @ph.block.vector
                def _(dve):
                    self.norm_dve_stats(ph, dve, self.x)
                    self.norm_dve_scale(ph, dve, self.x)

                    def rest_of_weights(*granules):
                        for g in granules:
                            i, view = source(g)
                            dve.wait_ge(ph["w_rounded"], g + 1)
                            dve.tensor_tensor(part(w_lo, g), view(self.ring[:, i % SLOTS, :]), part(w_hi, g), ALU.subtract).then_inc(ph["w_split"], 1)
                    rest_of_weights(0)
                    dve.wait_ge(ph["gain_in"], 16)
                    for k in range(KT):
                        dve.wait_ge(ph["h_rounded"], (k // 2 + 1) * 2)
                        dve.scalar_tensor_tensor(out=h_lo[:, k, :], in0=psum[:, 4 + k // 2, k % 2 * S:(k % 2 + 1) * S], scalar=self.gain[:, k:k + 1],
                                                 in1=h_hi[:, k, :], op0=ALU.mult, op1=ALU.subtract).then_inc(ph["h_split"], 1)
                    rest_of_weights(1, 2, 3)
                    for k in range(KT):
                        dve.tensor_scalar(hT[:, k, 0:S], psum[:, 4 + k // 2, k % 2 * S:(k % 2 + 1) * S], self.gain[:, k:k + 1], None, ALU.mult).then_inc(ph["h_whole"], 1)
                    rest_of_weights(4, 5, 6, 7)
                    dve.wait_ge(ph["small_in"], SMALL)
                    dve.wait_ge(ph["ws_turned"], 1)
                    dve.tensor_tensor(wsT[:, :, :], psum[:, 7, :].rearrange("p (g t) -> p g t", g=4),
                                      causal[:, :].unsqueeze(1).to_broadcast([P, 4, P]), ALU.mult).then_inc(ph["ws_ready"], 1)
                    for i in range(2):
                        for t in range(NT):
                            n = 2 * i + t
                            dve.wait_ge(ph["w_used"], 4 * (i + 1))
                            src = psum[:, n, :].rearrange("p (h d) -> p h d", h=CHEADS)
                            m1v, m2v = (m[:, :].rearrange("p (h d) -> p h d", h=CHEADS) for m in (m1, m2))
                            if n:
                                dve.wait_ge(ph["rotated"], n)
                            dve.tensor_tensor(m1v, src, rope[:, i, 0, t, :].unsqueeze(1).to_broadcast([P, CHEADS, P]), ALU.mult).then_inc(ph["rope_parts"], 1)
                            for o in (0, HEAD):
                                dve.tensor_tensor(m2v[:, :, o:o + HEAD], src[:, :, HEAD - o:P - o],
                                                  rope[:, i, 1, t, o:o + HEAD].unsqueeze(1).to_broadcast([P, CHEADS, HEAD]), ALU.mult).then_inc(ph["rope_parts"], 1)
                            dve.wait_ge(ph["rope_parts"], 3 * (n + 1))
                            dve.tensor_tensor(qk[:, i, t, :], m1[:, :], m2[:, :], ALU.add).then_inc(ph["rotated"], 1)
                        rest_of_weights(*range(8 + 4 * i, 12 + 4 * i))
                    dve.wait_ge(ph["rotated"], 4)
                    dve.tensor_tensor(kz[:, :].rearrange("p (h d) -> p h d", h=CHEADS), qk[:, 1, 0, :].rearrange("p (h d) -> p h d", h=CHEADS),
                                      zeta[:, :].unsqueeze(2).to_broadcast([P, CHEADS, P]), ALU.mult).then_inc(ph["kz_ready"], 1)
                    rest_of_weights(16, 17, 18, 19)
                    for i in range(2):
                        for t in range(NT):
                            n = 2 * i + t
                            dve.wait_ge(ph["qk_turned"], n + 1)
                            dve.tensor_copy(qkT[:, i, :, t * P:(t + 1) * P], psum[:, 4 + n, :].rearrange("p (h s) -> p h s", h=CHEADS)).then_inc(ph["qkT_ready"], 1)
                    dve.wait_ge(ph["qkT_ready"], 4)
                    dve.tensor_tensor(qx[:, :, :], qkT[:, 0, :, P:S], xi[:, :, :], ALU.mult).then_inc(ph["qx_ready"], 1)
                    rest_of_weights(20, 21, 22, 23)
                    dve.wait_ge(ph["va_ready"], 1)
                    vg = va[:, :, :].rearrange("p t (g d) -> p (t g) d", g=4)
                    self.group_stats(ph, dve, [vg[:, j, :] for j in range(8)], bn, mv, var, 0, ph["var_a"])
                    dve.wait_ge(ph["rs_a"], 1)
                    for j in range(8):
                        dve.tensor_scalar(vg[:, j, :], vg[:, j, :], mv[:, j, 0:1], rs[:, j:j + 1], ALU.subtract, ALU.mult).then_inc(ph["va_scaled"], 1)
                    dve.wait_ge(ph["va_scaled"], 8)
                    dve.tensor_tensor(va[:, :, :], va[:, :, :], gain_a[:, :].unsqueeze(1).to_broadcast([P, NT, AW]), ALU.mult).then_inc(ph["va_normed"], 1)
                    rest_of_weights(24, 25, 26, 27)
                    for t in range(NT):
                        dve.wait_ge(ph["scores_ready"], t + 1)
                        dve.tensor_tensor(pT[:, t, :, :], psum[:, 4 + t, :].rearrange("p (h s) -> p h s", h=CHEADS), decay[:, :, :], ALU.mult).then_inc(ph["pT_ready"], 1)
                    dve.wait_ge(ph["kv_ready"], 1)
                    dve.tensor_copy(kv[:, :], psum[:, 6, :]).then_inc(ph["kv_copied"], 1)
                    dve.wait_ge(ph["spatial_ready"], 1)
                    sv = psum[:, 7, :].rearrange("p (c s) -> p c s", c=2)
                    for t in range(NT):
                        dve.tensor_tensor(yT[:, 0:2, t * P:(t + 1) * P], sv[:, :, t * P:(t + 1) * P], b_s[:, :, :], ALU.add).then_inc(ph["sv_ready"], 1)
                    dve.wait_ge(ph["sv_ready"], 2)
                    dve.wait_ge(ph["u_ready"], 1)
                    dve.tensor_tensor(yT[:, 0:2, :], yT[:, 0:2, :], uT[:, :, :], ALU.mult).then_inc(ph["ya_ready"], 1)
                    dve.wait_ge(ph["bcx_ready"], 3)
                    dve.wait_ge(ph["z_edge"], 1)
                    dve.tensor_tensor(z[:, :, 2:S + 2], bcx[:, 2:4, :], bcx[:, 4:6, :], ALU.mult).then_inc(ph["z_ready"], 1)
                    dve.wait_ge(ph["z_ready"], 1)
                    for c in range(2):
                        dve.tensor_scalar(yb[:, c, :], z[:, c, 0:S], conv[:, c, 0:1], None, ALU.mult).then_inc(ph["taps"], 1)
                    for i in range(1, 3):
                        for c in range(2):
                            dve.wait_ge(ph["taps"], 2 * i + c - 1)
                            dve.scalar_tensor_tensor(out=yb[:, c, :], in0=z[:, c, i:i + S], scalar=conv[:, c, i:i + 1], in1=yb[:, c, :],
                                                     op0=ALU.mult, op1=ALU.add).then_inc(ph["taps"], 1)
                    dve.wait_ge(ph["taps"], 6)
                    dve.tensor_tensor(yT[:, 2:4, :], yb[:, :, :], bcx[:, 0:2, :], ALU.mult).then_inc(ph["yb_ready"], 1)
                    for i in range(2):
                        dve.wait_ge(ph["y_rounded"], i + 1)
                        dve.tensor_tensor(y_lo[:, 2 * i:2 * i + 2, :], yT[:, 2 * i:2 * i + 2, :], y_hi[:, 2 * i:2 * i + 2, :], ALU.subtract).then_inc(ph["y_split"], 1)
                    for t in range(NT):
                        dve.wait_ge(ph["ret_ready"], t + 1)
                    rg = [psum[:, 2 + t, h * P:(h + 1) * P] for t in range(NT) for h in range(CHEADS)]
                    self.group_stats(ph, dve, rg, bn, mv, var, 8, ph["var_c"])
                    dve.wait_ge(ph["rs_c"], 1)
                    for j in range(8):
                        dve.tensor_scalar(ret[:, j // 4, (j % 4) * P:(j % 4 + 1) * P], rg[j], mv[:, 8 + j, 0:1], rs[:, 8 + j:9 + j],
                                          ALU.subtract, ALU.mult).then_inc(ph["ret_scaled"], 1)
                    dve.wait_ge(ph["gate_ready"], 2)
                    for t in range(NT):
                        dve.wait_ge(ph["ret_scaled"], 4 * t + 4)
                        dve.tensor_tensor(ret[:, t, :], ret[:, t, :], gain_c[:, :], ALU.mult).then_inc(ph["ret_gained"], 1)
                        dve.wait_ge(ph["ret_gained"], t + 1)
                        dve.tensor_tensor(ret[:, t, :], ret[:, t, :], sg[:, t, :], ALU.mult).then_inc(ph["ret_gated"], 1)
                    rest_of_weights(28, 29, 30, 31)
                    for t in range(NT):
                        dve.wait_ge(ph["y_rounded"], 3 + t)
                        dve.tensor_tensor(y_lo[:, 4:8, t * P:(t + 1) * P], psum[:, 4 + t, :].rearrange("p (h s) -> p h s", h=CHEADS),
                                          y_hi[:, 4:8, t * P:(t + 1) * P], ALU.subtract).then_inc(ph["y_split"], 1)
                    for t in range(NT):
                        for n in range(2):
                            dve.wait_ge(ph["out_ready"], 2 * t + n + 1)
                            xs = self.x[:, t, n * WIDE:(n + 1) * WIDE]
                            dve.tensor_tensor(xs, psum[:, banks_out[2 * t + n], :], xs, ALU.add).then_inc(ph["x_ready"], 1)

                @ph.block.tensor
                def _(pe):
                    self.norm_pe(ph, pe)

                    def passes(dst, left, right, first, last):
                        for n, (a, b) in enumerate(((0, 0), (0, 1), (1, 0))):
                            mm = pe.matmul(dst, left[a], right[b], start=first and n == 0, stop=last and n == 2)
                        return mm

                    def by_token(i, bank):
                        for g in range(4 * i, 4 * i + 4):
                            pe.wait_ge(ph["w_split"], g + 1)
                            for kk in range(2):
                                k = g % 4 * 2 + kk
                                if i == 0:
                                    pe.wait_ge(ph["h_split"], k + 1)
                                for t in range(NT):
                                    mm = passes(psum[:, bank + t, :], [h[:, k, t * P:(t + 1) * P] for h in (h_hi, h_lo)],
                                                [part(w, g)[:, kk, :] for w in (w_hi, w_lo)], k == 0, k == KT - 1)
                            mm.then_inc(ph["w_used"], 1)

                    def by_channel(g, bank):
                        for c in range(2):
                            pe.wait_ge(ph["w_split"], g + c + 1)
                            for k in range(KT):
                                mm = passes(psum[:, bank, c * S:(c + 1) * S], [part(w, g + c)[:, k, :] for w in (w_hi, w_lo)],
                                            [h[:, k, :] for h in (h_hi, h_lo)], k == 0, k == KT - 1)
                            mm.then_inc(ph["w_used"], 1)

                    by_token(0, 0)
                    pe.wait_ge(ph["small_in"], SMALL)
                    pe.wait_ge(ph["h_whole"], KT)
                    for g in range(4):
                        mm = pe.transpose(psum[:, 7, g * P:(g + 1) * P], w_s[:, g, :], ident[:, :])
                    mm.then_inc(ph["ws_turned"], 1)
                    by_token(1, 2)
                    pe.wait_ge(ph["rotated"], 2)
                    by_token(2, 0)
                    pe.wait_ge(ph["rotated"], 4)
                    by_token(3, 2)
                    pe.wait_ge(ph["ws_ready"], 1)
                    for i in range(2):
                        for t in range(NT):
                            for h in range(CHEADS):
                                mm = pe.transpose(psum[:, 4 + 2 * i + t, h * P:(h + 1) * P], qk[:, i, t, h * P:(h + 1) * P], ident[:, :])
                            mm.then_inc(ph["qk_turned"], 1)
                    pe.wait_ge(ph["v_ready"], 2)
                    by_channel(16, 0)
                    w = ring.wait(pe, 4).rearrange("p (k n) -> p k n", n=WIDE)
                    for t in range(NT):
                        for k in range(KT):
                            mm = pe.matmul(psum[:, 1, t * AW:(t + 1) * AW], hT[:, k, t * P:(t + 1) * P], w[:, k, AW:2 * AW], start=(k == 0), stop=(k == KT - 1))
                    mm.then_inc(ph["va_made"], 1)
                    pe.wait_ge(ph["gate_ready"], 2)
                    by_channel(18, 2)
                    by_channel(20, 3)
                    pe.wait_ge(ph["u_ready"], 1)
                    by_channel(22, 0)
                    pe.wait_ge(ph["qkT_ready"], 4)
                    for t in range(NT):
                        for h in range(CHEADS):
                            mm = pe.matmul(psum[:, 4 + t, h * P:(h + 1) * P], qkT[:, 1, h, t * P:(t + 1) * P], qkT[:, 0, h, t * P:(t + 1) * P],
                                           start=True, stop=True)
                        mm.then_inc(ph["scores_ready"], 1)
                    pe.wait_ge(ph["kz_ready"], 1)
                    for h in range(CHEADS):
                        mm = pe.matmul(psum[:, 6, h * P:(h + 1) * P], kz[:, h * P:(h + 1) * P], v[:, 0, h * P:(h + 1) * P], start=True, stop=True)
                    mm.then_inc(ph["kv_ready"], 1)
                    pe.wait_ge(ph["va_normed"], 1)
                    for t in range(NT):
                        for g in range(4):
                            o = HEAD * (g % 2)
                            mm = pe.matmul(psum[o:o + HEAD, 7, (g // 2) * S + t * P:(g // 2) * S + (t + 1) * P],
                                           va[:, t, g * HEAD:(g + 1) * HEAD], wsT[:, g, :], start=True, stop=True)
                    mm.then_inc(ph["spatial_ready"], 1)
                    pe.wait_ge(ph["bcx_ready"], 2)
                    pe.wait_ge(ph["pT_ready"], 2)
                    pe.wait_ge(ph["kv_copied"], 1)
                    pe.wait_ge(ph["qx_ready"], 1)
                    for t in range(NT):
                        for h in range(CHEADS):
                            hs = slice(h * P, (h + 1) * P)
                            mm = pe.matmul(psum[:, 2 + t, hs], pT[:, t, h, :], v[:, t, hs], start=True, stop=(t == 0))
                            if t:
                                mm = pe.matmul(psum[:, 2 + t, hs], qx[:, h, :], kv[:, hs], start=False, stop=True)
                        mm.then_inc(ph["ret_ready"], 1)
                    def out_rows(k):
                        g = IN + k
                        pe.wait_ge(ph["w_split"], g + 1)
                        for t in range(NT):
                            for n in range(2):
                                mm = passes(psum[:, banks_out[2 * t + n], :], [y[:, k, t * P:(t + 1) * P] for y in (y_hi, y_lo)],
                                            [part(w, g)[:, n * WIDE:(n + 1) * WIDE] for w in (w_hi, w_lo)], k == 0, k == KT - 1)
                                if k == KT - 1:
                                    mm.then_inc(ph["out_ready"], 1)
                        if k < KT - 1:
                            mm.then_inc(ph["w_used"], 1)
                    pe.wait_ge(ph["bcx_ready"], 3)
                    pe.wait_ge(ph["va_ready"], 1)
                    pe.wait_ge(ph["sv_ready"], 2)
                    for k in range(4):
                        pe.wait_ge(ph["y_split"], k // 2 + 1)
                        out_rows(k)
                    for t in range(NT):
                        pe.wait_ge(ph["ret_gated"], t + 1)
                        for h in range(CHEADS):
                            mm = pe.transpose(psum[:, 4 + t, h * P:(h + 1) * P], ret[:, t, h * P:(h + 1) * P], ident[:, :])
                        mm.then_inc(ph["yc_turned"], 1)
                    pe.wait_ge(ph["y_split"], 4)
                    for k in range(4, KT):
                        out_rows(k)

    def group_stats(self, ph, dve, groups, bn, mv, var, at, done):
        n = len(groups)
        for j, g in enumerate(groups):
            dve.bn_stats(bn[:, at + j, :], g).then_inc(ph[f"stats_{at}"], 1)
        for j in range(n):
            dve.wait_ge(ph[f"stats_{at}"], j + 1)
            dve.bn_aggr(mv[:, at + j, :], bn[:, at + j, :]).then_inc(ph[f"aggregated_{at}"], 1)
        dve.wait_ge(ph[f"aggregated_{at}"], n)
        dve.tensor_scalar(var[:, at:at + n], mv[:, at:at + n, 1], EPS, None, ALU.add).then_inc(done, 1)

    def finish(self, normed=True):
        x, a = self.x, self.a
        with ExitStack() as ctx:
            gain = ctx.enter_context(self.nc.sbuf_tensor([P, D], F32))
            with self.phase() as ph:
                @ph.block.sync
                def _(sp):
                    if normed:
                        sp.dma_start(gain[:, :], a["final_norm_2"].partition_broadcast(P)).then_inc(ph["gain_in"], 16)
                    for t in range(NT):
                        if normed:
                            sp.wait_ge(ph["y_ready"], t + 1)
                        sp.dma_start(self.out[0, t * P:(t + 1) * P, :], (self.xn if normed else x)[:, t, :]).then_inc(ph["stored"], 16)
                    sp.wait_ge(ph["stored"], 16 * NT)

                if not normed:
                    return

                @ph.block.gpsimd
                def _(pool):
                    self.norm_pool(ph, pool)

                @ph.block.vector
                def _(dve):
                    self.norm_dve_stats(ph, dve, x)
                    dve.wait_ge(ph["rstd_ready"], 1)
                    dve.wait_ge(ph["gain_in"], 16)
                    for t in range(NT):
                        dve.scalar_tensor_tensor(out=self.xn[:, t, :], in0=x[:, t, :], scalar=self.rstd[:, t:t + 1], in1=gain[:, :],
                                                 op0=ALU.mult, op1=ALU.mult).then_inc(ph["y_ready"], 1)

    def ffn(self, l, norm, wg, wu, wd):
        a, psum = self.a, self.psum
        kp = "a (k p) n -> p (a k) n"
        GRAN, BUFS = D, 4
        panels, per = FF // S, KT * WIDE // GRAN
        granules = panels * per + FT
        with ExitStack() as ctx:
            w_hi, w_lo = self.split_pair(ctx, BUFS, GRAN)
            h_hi, h_lo = self.split_pair(ctx, KT, S)
            hid_hi, hid_lo = self.split_pair(ctx, FT, S)
            sb = self.scratch(ctx)
            sg, hid = sb(2, S), sb(2, S)
            with self.phase() as ph:
                ring = Ring(ph, self.ring)

                @ph.block.sync
                def _(sp):
                    for j in range(panels):
                        def parts(slot):
                            slot = slot.rearrange("p (k n) -> p k n", n=WIDE)
                            for w, o in ((wg, 0), (wu, S)):
                                yield slot[:, :, o:o + S], a[w][bass.ds(l, 1)].rearrange(kp, p=P)[:, :, j * S:(j + 1) * S]
                        ring.load(sp, parts, (ph["w_split"], per * (j - SLOTS + 1)))
                    for q, f0 in enumerate(range(0, FT, per)):
                        n = min(per, FT - f0)

                        def parts(slot):
                            yield (slot[:, 0:n * D].rearrange("p (k n) -> p k n", n=D),
                                   a[wd][bass.ds(l, 1)].rearrange(kp, p=P)[:, f0:f0 + n, :])
                        ring.load(sp, parts, (ph["w_split"], per * (panels + q - SLOTS + 1)))

                @ph.block.scalar
                def _(act):
                    with self.nc.allow_non_contiguous_dma(reason="a gain vector"):
                        act.dma_start(self.gain[:, :], a[norm][bass.ds(l, 1)].rearrange("a (k p) -> p (a k)", p=P)).then_inc(ph["gain_in"], 16)

                    def round_weights(g):
                        w = ring.wait(act, g // per)
                        if g >= BUFS:
                            act.wait_ge(ph["w_used"], g - BUFS + 1)
                        act.activation(w_hi[:, g % BUFS, :], w[:, g % per * GRAN:(g % per + 1) * GRAN], ACT.Copy).then_inc(ph["w_rounded"], 1)
                    round_weights(0)
                    act.wait_ge(ph["gain_in"], 16)
                    for k in range(KT):
                        act.wait_ge(ph["turned"], (k // 2 + 1) * 2)
                        act.activation(h_hi[:, k, :], psum[:, 4 + k // 2, k % 2 * S:(k % 2 + 1) * S], ACT.Copy, scale=self.gain[:, k:k + 1]).then_inc(ph["h_rounded"], 1)
                    for g in range(1, granules):
                        j = g // per - 2
                        if g % per == per - 1 and 0 <= j < panels:
                            act.wait_ge(ph["w_used"], per * (j + 1))
                            if j:
                                act.wait_ge(ph["hid_made"], 2 * j)
                            for i in range(2):
                                act.activation(sg[:, i, :], psum[:, j % 2 * 4 + 2 * i, 0:S], ACT.Silu).then_inc(ph["silu_ready"], 1)
                        round_weights(g)

                @ph.block.gpsimd
                def _(pool):
                    self.norm_pool(ph, pool)

                @ph.block.vector
                def _(dve):
                    def rest_of_weights(g):
                        dve.wait_ge(ph["w_rounded"], g + 1)
                        w = self.ring[:, g // per % SLOTS, g % per * GRAN:(g % per + 1) * GRAN]
                        dve.tensor_tensor(w_lo[:, g % BUFS, :], w, w_hi[:, g % BUFS, :], ALU.subtract).then_inc(ph["w_split"], 1)
                    self.norm_dve_stats(ph, dve, self.x)
                    self.norm_dve_scale(ph, dve, self.x)
                    rest_of_weights(0)
                    dve.wait_ge(ph["gain_in"], 16)
                    for k in range(KT):
                        dve.wait_ge(ph["h_rounded"], (k // 2 + 1) * 2)
                        dve.scalar_tensor_tensor(out=h_lo[:, k, :], in0=psum[:, 4 + k // 2, k % 2 * S:(k % 2 + 1) * S], scalar=self.gain[:, k:k + 1],
                                                 in1=h_hi[:, k, :], op0=ALU.mult, op1=ALU.subtract).then_inc(ph["h_split"], 1)
                    for g in range(1, granules):
                        j = g // per - 2
                        if g % per == per - 1 and 0 <= j < panels:
                            for i in range(2):
                                f = 2 * j + i
                                dve.wait_ge(ph["silu_ready"], f + 1)
                                if j:
                                    dve.wait_ge(ph["hid_split"], f - 1)
                                dve.tensor_tensor(hid[:, i, :], sg[:, i, :], psum[:, j % 2 * 4 + 2 * i + 1, 0:S], ALU.mult).then_inc(ph["hid_made"], 1)
                            for i in range(2):
                                f = 2 * j + i
                                dve.wait_ge(ph["hid_made"], f + 1)
                                dve.tensor_copy(hid_hi[:, f, :], hid[:, i, :]).then_inc(ph["hid_rounded"], 1)
                            for i in range(2):
                                f = 2 * j + i
                                dve.wait_ge(ph["hid_rounded"], f + 1)
                                dve.tensor_tensor(hid_lo[:, f, :], hid[:, i, :], hid_hi[:, f, :], ALU.subtract).then_inc(ph["hid_split"], 1)
                        rest_of_weights(g)
                    for t in range(NT):
                        for n in range(2):
                            dve.wait_ge(ph["down_ready"], 2 * t + n + 1)
                            dve.scalar_tensor_tensor(out=self.x[:, t, n * WIDE:(n + 1) * WIDE], in0=psum[:, 4 + 2 * t + n, :],
                                                     scalar=0.5, in1=self.x[:, t, n * WIDE:(n + 1) * WIDE],
                                                     op0=ALU.mult, op1=ALU.add).then_inc(ph["x_ready"], 1)

                @ph.block.tensor
                def _(pe):
                    self.norm_pe(ph, pe)
                    for j in range(panels):
                        for q in range(per):
                            g = j * per + q
                            hi, lo = (w[:, g % BUFS, :].rearrange("p (k n) -> p k n", n=WIDE) for w in (w_hi, w_lo))
                            pe.wait_ge(ph["w_split"], g + 1)
                            if q == 0 and j >= 2:
                                pe.wait_ge(ph["hid_made"], 2 * (j - 1))
                            for kk in range(2):
                                k = 2 * q + kk
                                if j == 0:
                                    pe.wait_ge(ph["h_split"], k + 1)
                                for i in range(2):
                                    for o in (0, S):
                                        at = slice(o + i * P, o + (i + 1) * P)
                                        for n, (w, h) in enumerate(((hi, h_hi), (hi, h_lo), (lo, h_hi))):
                                            mm = pe.matmul(psum[:, j % 2 * 4 + 2 * i + o // S, 0:S], w[:, kk, at], h[:, k, :],
                                                           start=(k == 0 and n == 0), stop=(k == KT - 1 and n == 2))
                            mm.then_inc(ph["w_used"], 1)
                    for f in range(FT):
                        g = panels * per + f
                        pe.wait_ge(ph["w_split"], g + 1)
                        pe.wait_ge(ph["hid_split"], f + 1)
                        if f == 0:
                            pe.wait_ge(ph["hid_made"], FT - 2)
                        for t in range(NT):
                            for n in range(2):
                                ws = slice(n * WIDE, (n + 1) * WIDE)
                                for m, (h, w) in enumerate(((hid_hi, w_hi), (hid_hi, w_lo), (hid_lo, w_hi))):
                                    mm = pe.matmul(psum[:, 4 + 2 * t + n, :], h[:, f, t * P:(t + 1) * P], w[:, g % BUFS, ws],
                                                   start=(f == 0 and m == 0), stop=(f == FT - 1 and m == 2))
                                if f == FT - 1:
                                    mm.then_inc(ph["down_ready"], 1)
                        if f < FT - 1:
                            mm.then_inc(ph["w_used"], 1)

    def turn_rows(self, rows, cols):
        total = sum(r.shape[0] for r in rows)
        with ExitStack() as ctx:
            sb = self.scratch(ctx)
            tiles = [sb(P) for _ in range((total + P - 1) // P)]
            with self.phase() as ph:
                @ph.block.sync
                def _(sp):
                    at = n = 0
                    for r in rows:
                        done = 0
                        while done < r.shape[0]:
                            k = min(r.shape[0] - done, P - at % P)
                            sp.dma_start(tiles[at // P][at % P:at % P + k, :], r[done:done + k, :]).then_inc(ph["rows_in"], 16)
                            done, at, n = done + k, at + k, n + 1
                    self.row_loads = n

                @ph.block.tensor
                def _(pe):
                    pe.wait_ge(ph["rows_in"], 16 * self.row_loads)
                    for i, tile in enumerate(tiles):
                        n = min(P, total - i * P)
                        pe.transpose(self.psum[:, i, 0:n], tile[0:n, :], self.ident[0:n, 0:n]).then_inc(ph["rows_turned"], 1)

                @ph.block.vector
                def _(dve):
                    for i in range(len(tiles)):
                        n = min(P, total - i * P)
                        dve.wait_ge(ph["rows_turned"], i + 1)
                        dve.tensor_copy(cols[:, i * P:i * P + n], self.psum[:, i, 0:n]).then_inc(ph["cols_ready"], 1)

    def adaln(self, l, conds):
        a, psum = self.a, self.psum
        with ExitStack() as ctx:
            sb = self.scratch(ctx)
            bias, ada = sb(3 * D), sb(3 * D)
            panels = 3 * D // WIDE
            with self.phase() as ph:
                ring = Ring(ph, self.ring)

                @ph.block.sync
                def _(sp):
                    for j in range(panels):
                        def parts(slot):
                            yield (slot.rearrange("p (k n) -> p k n", n=WIDE),
                                   a["ada_w"][l].rearrange("(k p) n -> p k n", p=P)[:, :, j * WIDE:(j + 1) * WIDE])
                        ring.load(sp, parts, (ph["ada_ready"], j - SLOTS + 1))

                @ph.block.scalar
                def _(act):
                    act.dma_start(bias[0:2, :], a["ada_b"][l].partition_broadcast(2)).then_inc(ph["bias_in"], 16)
                    act.dma_start(self.post[:, :], a["norm_post"][l].partition_broadcast(P)).then_inc(ph["post_in"], 16)
                    with self.nc.allow_non_contiguous_dma(reason="a gain vector"):
                        act.dma_start(self.gain[:, :], chan(a["norm_pre"][l])).then_inc(ph["gain_in"], 16)

                @ph.block.tensor
                def _(pe):
                    for j in range(panels):
                        w = ring.wait(pe, j).rearrange("p (k n) -> p k n", n=WIDE)
                        for k in range(KT):
                            mm = pe.matmul(psum[0:2, j, :], self.cond[:, k, :], w[:, k, :], start=(k == 0), stop=(k == KT - 1))
                        mm.then_inc(ph["ada_ready"], 1)
                    pe.wait_ge(ph["biased"], panels)
                    for k in range(2 * KT):
                        mm = pe.transpose(psum[:, 6, 2 * k:2 * k + 2], ada[0:2, k * P:(k + 1) * P], self.ident[0:2, 0:2])
                    mm.then_inc(ph["ada_turned"], 1)
                    for n in range(2):
                        mm = pe.matmul(psum[:, n, :], self.ones[0:1, :], ada[0:1, 2 * D + n * WIDE:2 * D + (n + 1) * WIDE], start=True, stop=True)
                    mm.then_inc(ph["gate_spread"], 1)

                @ph.block.vector
                def _(dve):
                    dve.wait_ge(ph["bias_in"], 16)
                    for j in range(panels):
                        dve.wait_ge(ph["ada_ready"], j + 1)
                        dve.tensor_tensor(ada[0:2, j * WIDE:(j + 1) * WIDE], psum[0:2, j, :], bias[0:2, j * WIDE:(j + 1) * WIDE], ALU.add).then_inc(ph["biased"], 1)
                    dve.wait_ge(ph["ada_turned"], 1)
                    dve.wait_ge(ph["gain_in"], 16)
                    cols = psum[:, 6, 0:4 * KT].rearrange("p (k c) -> p c k", c=2)
                    for c in range(conds):
                        dve.tensor_copy(self.shift[:, c, :], cols[:, c, 0:KT]).then_inc(ph["shift_ready"], 1)
                        dve.scalar_tensor_tensor(out=self.scale[:, c, :], in0=cols[:, c, KT:2 * KT], scalar=1.0, in1=self.gain[:, :],
                                                 op0=ALU.add, op1=ALU.mult).then_inc(ph["scale_ready"], 1)
                    dve.wait_ge(ph["gate_spread"], 1)
                    dve.wait_ge(ph["post_in"], 16)
                    for n in range(2):
                        s = slice(n * WIDE, (n + 1) * WIDE)
                        dve.tensor_tensor(self.post[:, s], self.post[:, s], psum[:, n, :], ALU.mult).then_inc(ph["post_ready"], 1)

    def norm_first(self, x, c, at):
        with self.phase() as ph:
            @ph.block.vector
            def _(dve):
                self.norm_dve_stats(ph, dve, x)
                self.norm_dve_scale(ph, dve, x)
                self.norm_dve_turn(ph, dve, self.scale[:, c, :], self.shift[:, c, :], at=at)

            @ph.block.gpsimd
            def _(pool):
                self.norm_pool(ph, pool)

            @ph.block.tensor
            def _(pe):
                self.norm_pe(ph, pe)

            @ph.block.scalar
            def _(act):
                self.norm_act(ph, act, self.scale[:, c, :], self.shift[:, c, :], at=at)

    def out_first(self, l, uT):
        a, psum = self.a, self.psum
        BUFS = 4
        with ExitStack() as ctx, self.phase() as ph:
            w_hi, w_lo = self.split_pair(ctx, BUFS, D)
            u_hi, u_lo = self.split_pair(ctx, ET, S)
            o = self.scratch(ctx)(NT, D)
            ring = Ring(ph, self.ring)

            @ph.block.sync
            def _(sp):
                for q in range(ET // 4):
                    def parts(slot):
                        yield (slot.rearrange("p (k n) -> p k n", n=D),
                               a["w_out"][l].rearrange("(k p) n -> p k n", p=P)[:, 4 * q:4 * q + 4, :])
                    ring.load(sp, parts, None)

            @ph.block.scalar
            def _(act):
                for e in range(ET):
                    act.activation(u_hi[:, e, :], uT[:, e, :], ACT.Copy).then_inc(ph["u_rounded"], 1)
                    if e % 4 == 0:
                        w = ring.wait(act, e // 4)
                    if e >= BUFS:
                        act.wait_ge(ph["w_used"], e - BUFS + 1)
                    act.activation(w_hi[:, e % BUFS, :], w[:, e % 4 * D:(e % 4 + 1) * D], ACT.Copy).then_inc(ph["w_rounded"], 1)

            @ph.block.tensor
            def _(pe):
                for e in range(ET):
                    pe.wait_ge(ph["u_split"], e + 1)
                    pe.wait_ge(ph["w_split"], e + 1)
                    for t in range(NT):
                        for n in range(2):
                            for m, (u, w) in enumerate(((u_hi, w_hi), (u_hi, w_lo), (u_lo, w_hi))):
                                mm = pe.matmul(psum[:, 2 * t + n, :], u[:, e, t * P:(t + 1) * P], w[:, e % BUFS, n * WIDE:(n + 1) * WIDE],
                                               start=(e == 0 and m == 0), stop=(e == ET - 1 and m == 2))
                            if e == ET - 1:
                                mm.then_inc(ph["out_ready"], 1)
                    if e < ET - 1:
                        mm.then_inc(ph["w_used"], 1)

            @ph.block.gpsimd
            def _(pool):
                self.norm_pool(ph, pool)

            @ph.block.vector
            def _(dve):
                for e in range(ET):
                    dve.wait_ge(ph["u_rounded"], e + 1)
                    dve.tensor_tensor(u_lo[:, e, :], uT[:, e, :], u_hi[:, e, :], ALU.subtract).then_inc(ph["u_split"], 1)
                    dve.wait_ge(ph["w_rounded"], e + 1)
                    dve.tensor_tensor(w_lo[:, e % BUFS, :], self.ring[:, e // 4, e % 4 * D:(e % 4 + 1) * D], w_hi[:, e % BUFS, :], ALU.subtract).then_inc(ph["w_split"], 1)
                for t in range(NT):
                    for n in range(2):
                        dve.wait_ge(ph["out_ready"], 2 * t + n + 1)
                        dve.tensor_copy(o[:, t, n * WIDE:(n + 1) * WIDE], psum[:, 2 * t + n, :]).then_inc(ph["out_copied"], 1)
                dve.wait_ge(ph["out_copied"], 4)
                self.norm_dve_stats(ph, dve, o)
                dve.wait_ge(ph["rstd_ready"], 1)
                for t in range(NT):
                    dve.scalar_tensor_tensor(out=o[:, t, :], in0=o[:, t, :], scalar=self.rstd[:, t:t + 1], in1=self.post[:, :],
                                             op0=ALU.mult, op1=ALU.mult).then_inc(ph["out_scaled"], 1)
                for t in range(NT):
                    dve.wait_ge(ph["out_scaled"], t + 1)
                    dve.tensor_tensor(self.x[:, t, :], self.x[:, t, :], o[:, t, :], ALU.add).then_inc(ph["x_ready"], 1)

    def rwkv_mixes(self, mix, lora, cols):
        a, psum, hT = self.a, self.psum, self.hT
        groups = [(0, "r", S), (1, "k", 2 * S), (2, "v", 2 * S), (3, "g", S), (4, "w", 2 * S), (5, "a", 2 * S)]
        with ExitStack() as ctx:
            sb = self.scratch(ctx)
            xx = sb(KT, 2 * S)
            loras = {"w": sb(KT, 2 * S)}
            loras["a"] = loras["w"]
            wl = self.ring[:, 0, 0:KT * 256].rearrange("p (k n) -> p k n", n=256)
            with self.phase() as ph:
                @ph.block.sync
                def _(sp):
                    sp.dma_start(wl, a["l0_w_in"].rearrange("(k p) n -> p k n", p=P)[:, :, 4 * E:4 * E + 4 * LORA]).then_inc(ph["lora_in"], 16)

                @ph.block.vector
                def _(dve):
                    n = 0

                    def diff(dst, other, own):
                        nonlocal n
                        dve.tensor_tensor(dst, other, own, ALU.subtract).then_inc(ph["shifted"], 1)
                        n += 1

                    def edge(dst, own):
                        nonlocal n
                        dve.tensor_scalar(dst, own, -1.0, None, ALU.mult).then_inc(ph["shifted"], 1)
                        n += 1
                    for q in range(4):
                        for k in (2 * q, 2 * q + 1):
                            h, d = hT[:, k, 0:S], xx[:, k, 0:S]
                            hg, dg = (v.rearrange("p (r c) -> p r c", c=64) for v in (h, d))
                            if q == 0:
                                diff(dg[:, :, 1:], hg[:, :, 0:63], hg[:, :, 1:])
                                edge(dg[:, :, 0:1], hg[:, :, 0:1])
                            elif q == 1:
                                diff(dg[:, :, 0:63], hg[:, :, 1:], hg[:, :, 0:63])
                                edge(dg[:, :, 63:64], hg[:, :, 63:64])
                            elif q == 2:
                                diff(d[:, 64:], h[:, 0:S - 64], h[:, 64:])
                                edge(d[:, 0:64], h[:, 0:64])
                            else:
                                diff(d[:, 0:S - 64], h[:, 64:], h[:, 0:S - 64])
                                edge(d[:, S - 64:], h[:, S - 64:])
                    for k in range(KT):
                        h, d = hT[:, k, S:2 * S], xx[:, k, S:2 * S]
                        if k < KT // 2:
                            diff(d[:, 1:], h[:, 0:S - 1], h[:, 1:])
                            edge(d[:, 0:1], h[:, 0:1])
                        else:
                            diff(d[:, 0:S - 1], h[:, 1:], h[:, 0:S - 1])
                            edge(d[:, S - 1:], h[:, S - 1:])
                    dve.wait_ge(ph["shifted"], n)
                    for g, name, w in groups[4:] + groups[:4]:
                        dst = loras[name] if name in loras else mix[name]
                        if name == "a":
                            dve.wait_ge(ph["lora_ready"], 1)
                        for k in range(KT):
                            dve.scalar_tensor_tensor(out=dst[:, k, 0:w], in0=xx[:, k, 0:w], scalar=cols[:, g * KT + k:g * KT + k + 1],
                                                     in1=hT[:, k, 0:w], op0=ALU.mult, op1=ALU.add).then_inc(ph["mixed"], 1)
                    dve.wait_ge(ph["lora_ready"], 2)
                    dve.tensor_copy(lora["a"][:, :], psum[:, 1, :]).then_inc(ph["lora_a"], 1)

                @ph.block.tensor
                def _(pe):
                    pe.wait_ge(ph["lora_in"], 16)
                    for i in range(2):
                        pe.wait_ge(ph["mixed"], KT * (i + 1))
                        for k in range(KT):
                            mm = pe.matmul(psum[:, i, :], wl[:, k, i * P:(i + 1) * P], loras["w"][:, k, :], start=(k == 0), stop=(k == KT - 1))
                        mm.then_inc(ph["lora_ready"], 1)

                @ph.block.scalar
                def _(act):
                    act.wait_ge(ph["lora_ready"], 1)
                    act.activation(lora["w"][:, :], psum[:, 0, :], ACT.Tanh).then_inc(ph["lora_w"], 1)

    def rwkv_room(self, sb):
        C, XC, BD = self.C, self.XC, self.BD
        room = [self.ring[:, 2:SLOTS, :].rearrange("p s n -> p (s n)"), self.x[:, :, :].rearrange("p t d -> p (t d)")]
        left = [2 * KT * WIDE, NT * D]
        at = [0, 0]

        def carve(*shape):
            n = int(np.prod(shape))
            q = 0 if at[0] + n <= left[0] else 1
            if at[q] + n > left[q]:
                return sb(*shape)[(slice(None),) * (1 + len(shape))]
            v = room[q][:, at[q]:at[q] + n]
            at[q] += n
            names = "abc"[:len(shape)]
            if len(shape) > 1:
                v = v.rearrange(f"p ({' '.join(names)}) -> p {' '.join(names)}", **{c: n for c, n in zip(names, shape)})
            return v

        class Room:
            pass
        r = Room()
        r.w = self.ring[:, 1, :].rearrange("p (k j n) -> p k j n", j=4, n=P)
        bk = self.ring[:, 0, :].rearrange("p (q c n) -> p q c n", q=4, n=BD)
        r.btok, r.ktok = [bk[:, z] for z in range(2)], [bk[:, 2 + z] for z in range(2)]
        r.U = [self.hT[:, 2 * z:2 * z + 2, :].rearrange("p k (c n) -> p (k c) n", n=BD) for z in range(2)]
        r.T = [self.hT[:, 4 + 2 * z:6 + 2 * z, :].rearrange("p k (c n) -> p (k c) n", n=BD) for z in range(2)]
        r.R = [self.xn[:, z, :].rearrange("p (c n) -> p c n", n=BD) for z in range(2)]
        r.ar = [carve(XC, 2, BD) for _ in range(2)]
        r.ac = [carve(C - XC, BD) for _ in range(2)]
        r.ax = [carve(XC, 3, BD) for _ in range(2)]
        r.akc = [carve(C - XC, BD) for _ in range(2)]
        r.bbd, r.kbd = [carve(C, BD) for _ in range(2)], [carve(C, BD) for _ in range(2)]
        r.B = r.bbd
        r.Vt = carve(C, BD)
        r.vbd = r.kbd[0]
        r.K, r.KK = carve(2 * S), carve(2 * S)
        r.L, r.sig, r.al, r.kd, r.E3 = ([carve(2 * S) for _ in range(2)] for _ in range(5))
        r.E1, r.E2 = r.L, r.sig
        r.kw, r.kn = self.xn[:, 1, 0:2 * S], self.xn[:, 1, 2 * S:4 * S]
        r.Rr, r.V, r.G, r.Gs, r.Gh, r.BV = (carve(S) for _ in range(6))
        r.prod = [carve(S) for _ in range(2)]
        r.cur, r.ln, r.D = sb(10), sb(2), sb(2, C)
        r.St, r.DS, r.Rs, r.Us = ([r.T[0][:, 2 * q + z, :] for z in range(2)] for q in range(4))
        r.y, r.cen, r.yn = (r.T[1][:, 2 * q:2 * q + 2, :].rearrange("p c n -> p (c n)") for q in range(3))
        r.w2, r.a2 = r.T[1][:, 6, :], r.T[1][:, 7, :]
        r.uo = r.cen
        return r

    def rwkv_step(self, r, head, tail, mix, lora, prm, uT):
        a, psum, ident = self.a, self.psum, self.ident
        C, XC, BD = self.C, self.XC, self.BD
        DECAY = float(np.exp(-0.5))
        LEVELS = 5
        order = [list(range(XC, C)) + list(range(XC)), list(range(C - 1, XC - 1, -1)) + list(range(XC - 1, -1, -1))]
        heads = (slice(0, CH), slice(CH, P))
        doing_head, doing_tail = head is not None, tail is not None
        W0, A0, KKW, KA, RK, LNW, OMK = 0, 2, 4, 5, 6, 7, 9

        def col(j):
            return r.cur[:, j:j + 1]

        def a_of(z, c):
            return r.ar[z][:, c, 0, :] if c < XC else r.ac[z][:, c - XC, :]

        def four(v, half):
            return v[:, 4 * half:4 * half + 4, :]

        def bank(b):
            return psum[:, b, :].rearrange("p (c n) -> p c n", n=BD)

        def chunks(v):
            return v.rearrange("p (c s) -> p c s", s=CH)

        with self.phase() as ph:
            def load_weights(sp):
                wv = a["l0_w_in"].rearrange("(k p) n -> p k n", p=P)
                for j in (1, 0, 3, 2):
                    sp.dma_start(r.w[:, :, j, :], wv[:, :, bass.ds(tail * P + j * E, P)]).then_inc(ph[f"w{j}_in"], 16)
                    if j == 2:
                        if doing_head:
                            sp.wait_ge(ph["u_made"], 4 * LEVELS)
                        sp.dma_start(r.w2, a["l0_w2"].rearrange("z r e -> (z r) e")[:, bass.ds(tail * P, P)]).then_inc(ph["lora_in"], 16)
                        sp.dma_start(r.a2, a["l0_a2"].rearrange("z r e -> (z r) e")[:, bass.ds(tail * P, P)]).then_inc(ph["lora_in"], 16)

            @ph.block.sync
            def _(sp):
                if doing_tail:
                    load_weights(sp)
                if doing_head:
                    sp.wait_ge(ph["u_out"], 1)
                    sp.dma_start(uT[:, bass.ds(head, 1), :].rearrange("p a s -> p (a s)"), r.uo).then_inc(ph["u_stored"], 16)
                    sp.wait_ge(ph["u_stored"], 16)

            @ph.block.tensor
            def _(pe):
                def project():
                    def whole(j, name, b, o, n):
                        for k in range(KT):
                            if k == 0:
                                pe.wait_ge(ph[f"w{j}_in"], 16)
                            mm = pe.matmul(psum[:, b, o:o + n], r.w[:, k, j, :], mix[name][:, k, 0:n], start=(k == 0), stop=(k == KT - 1))
                            if k == KT - 1:
                                mm.then_inc(ph["proj_ready"], 1)
                            if n == 2 * S or k % 2:
                                yield
                    def rank(what, z, b):
                        zs = slice(LORA * z, LORA * z + LORA)
                        pe.matmul(psum[:, b, :], {"w": r.w2, "a": r.a2}[what][zs, :], lora[what][zs, :], start=True, stop=True).then_inc(ph["lora_ready"], 1)

                    yield from whole(1, "k", 4, 0, 2 * S)
                    pe.wait_ge(ph["lora_in"], 32)
                    rank("w", 0, 7)
                    yield
                    yield from whole(0, "r", 5, 0, S)
                    gate = whole(3, "g", 5, S, S)
                    yield from gate
                    pe.wait_ge(ph["k_ready"], 1)
                    pe.wait_ge(ph["kk_squared"], 1)
                    pe.matmul(psum[:, 4, :], self.same_head[:, :], r.kn, start=True, stop=True).then_inc(ph["kk_summed"], 1)
                    yield
                    pe.wait_ge(ph["sig_ready"], 1)
                    rank("a", 0, 7)
                    yield
                    value = whole(2, "v", 6, 0, 2 * S)
                    for _ in range(2):
                        next(value)
                        yield
                    pe.wait_ge(ph["kk_floored"], 1)
                    rank("w", 1, 4)
                    yield
                    for _ in range(2):
                        next(value)
                        yield
                    pe.wait_ge(ph["sig_ready"], 2)
                    rank("a", 1, 7)
                    yield
                    yield from value

                work = project() if doing_tail else iter(())
                if doing_head:
                    for z in range(2):
                        mm = pe.matmul(psum[:, 7, 0:S], self.same_head[:, :], r.prod[z], start=(z == 0), stop=(z == 1))
                    mm.then_inc(ph["bonus_made"], 1)
                    for j in range(4):
                        z, half = j // 2, j % 2
                        for c in range(4):
                            mm = pe.transpose(psum[:, j, c * BD:(c + 1) * BD], r.R[z][:, 4 * half + c, :], ident[:, :])
                        mm.then_inc(ph["b_turned"], 1)
                    for j in range(4):
                        z, half = j // 2, j % 2
                        if j >= 2:
                            pe.wait_ge(ph["u_level"], j - 1)
                        if j == 3:
                            pe.wait_ge(ph["bonus_read"], 1)
                        for c in range(4):
                            mm = pe.transpose(psum[:, 4 + j, c * BD:(c + 1) * BD], r.U[z][:, 4 * half + c, :], ident[:, :])
                        mm.then_inc(ph["t_turned"], 1)
                    for m in range(LEVELS):
                        for j in range(4):
                            z, half = j // 2, j % 2
                            pe.wait_ge(ph["b_ready"], j + 1)
                            if m or j >= 2:
                                pe.wait_ge(ph["u_level"], 4 * m + j - 1)
                            pe.wait_ge(ph["t_level"], 4 * m + j + 1)
                            for c in range(4):
                                cc = 4 * half + c
                                mm = pe.matmul(psum[:, j, c * BD:(c + 1) * BD], r.B[z][:, cc, :], r.U[z][:, cc, :], start=True, stop=True)
                            mm.then_inc(ph["r_made"], 1)
                        for j in range(4):
                            z, half = j // 2, j % 2
                            pe.wait_ge(ph["r_level"], 4 * m + j + 1)
                            for c in range(4):
                                cc = 4 * half + c
                                mm = pe.matmul(psum[:, 4 + j, c * BD:(c + 1) * BD], r.T[z][:, cc, :], r.R[z][:, cc, :], start=True, stop=True)
                            mm.then_inc(ph["u_made"], 1)
                        if m < LEVELS - 1:
                            for j in range(4):
                                z, half = j // 2, j % 2
                                pe.wait_ge(ph["u_level"], 4 * (m + 1) + j - 1)
                                for c in range(4):
                                    mm = pe.transpose(psum[:, j, c * BD:(c + 1) * BD], r.U[z][:, 4 * half + c, :], ident[:, :])
                                mm.then_inc(ph["t_turned"], 1)
                    pe.wait_ge(ph["r_level"], 4 * LEVELS)
                    for n in range(C):
                        for z in range(2):
                            c = order[z][n]
                            ak = r.ax[z][:, c, 1, :] if c < XC else r.akc[z][:, c - XC, :]
                            if n:
                                pe.wait_ge(ph[f"state_{z}"], n)
                                pe.matmul(psum[:, z, 0:BD], a_of(z, c), r.St[z], start=True, stop=False)
                            pe.matmul(psum[:, z, 0:BD], ak, r.Vt[:, c, :], start=(n == 0), stop=True).then_inc(ph[f"rhs_made_{z}"], 1)
                        if n == 0:
                            pe.wait_ge(ph["u_level"], 4 * LEVELS + 2)
                        next(work, None)
                        for z in range(2):
                            c = order[z][n]
                            pe.wait_ge(ph[f"rhs_{z}"], n + 1)
                            pe.matmul(psum[:, z, BD:2 * BD], r.U[z][:, c, :], r.Rs[z], start=True, stop=True).then_inc(ph[f"u_made_{z}"], 1)
                        next(work, None)
                        next(work, None)
                        for z in range(2):
                            c = order[z][n]
                            pe.wait_ge(ph[f"u_{z}"], n + 1)
                            if n < C - 1:
                                pe.matmul(psum[:, z, 2 * BD:3 * BD], r.btok[z][:, c, :], r.Us[z], start=True, stop=False)
                                pe.matmul(psum[:, z, 2 * BD:3 * BD], r.ktok[z][:, c, :], r.Vt[:, c, :], start=False, stop=True).then_inc(ph[f"state_made_{z}"], 1)
                        for z in range(2):
                            c = order[z][n]
                            if c < XC:
                                ys = psum[:, 2 + z, c * BD:(c + 1) * BD]
                                pe.matmul(ys, r.St[z], r.ar[z][:, c, 1, :], start=True, stop=False)
                                pe.matmul(ys, r.Us[z], r.ax[z][:, c, 0, :], start=False, stop=False)
                                pe.matmul(ys, r.Vt[:, c, :], r.ax[z][:, c, 2, :], start=False, stop=True).then_inc(ph[f"y_made_{z}"], 1)
                        if n < 5:
                            next(work, None)
                for _ in work:
                    pass
                if doing_head:
                    pe.wait_ge(ph["y_ready"], 2)
                    pe.matmul(psum[:, 0, 0:S], self.head_mean[:, :], r.y, start=True, stop=True).then_inc(ph["mean_made"], 1)
                if doing_tail:
                    pe.wait_ge(ph["sig_ready"], 3)
                    pe.wait_ge(ph["g_ready"], 1)
                    pe.wait_ge(ph["v_ready"], 2)
                    for c in range(C):
                        mm = pe.transpose(psum[:, 4 + c // 4, (c % 4) * BD:(c % 4 + 1) * BD], r.vbd[:, c, :], ident[:, :])
                        if c % 4 == 3:
                            mm.then_inc(ph["v_turned"], 1)
                if doing_head:
                    pe.wait_ge(ph["squared"], 1)
                    pe.matmul(psum[:, 1, 0:S], self.head_mean[:, :], r.y, start=True, stop=True).then_inc(ph["var_made"], 1)
                if doing_tail:
                    for z in range(2):
                        if z == 0:
                            pe.wait_ge(ph["sig_ready"], 4)
                        else:
                            pe.wait_ge(ph["tok_ready"], 4)
                        for q, src in enumerate((r.bbd[z], r.kbd[z])):
                            pe.wait_ge(ph["bk"[q] + "_laid"], 2 * z + 2)
                            if z == 0 and q == 1:
                                pe.wait_ge(ph["vt_ready"], 2)
                            for c in range(C):
                                b = (7, 2, 4, 5)[2 * q + c // 4]
                                mm = pe.transpose(psum[:, b, (c % 4) * BD:(c % 4 + 1) * BD], src[:, c, :], ident[:, :])
                                if c % 4 == 3:
                                    mm.then_inc(ph["tok_turned"], 1)
                        pe.wait_ge(ph["ar_laid"], 7 * z + 7)
                        for c in range(C):
                            n = z * C + c
                            b = (0, 1, 6)[n % 3]
                            if n >= 3:
                                pe.wait_ge(ph["a_ready"], n - 2)
                            elif n == 0:
                                pe.wait_ge(ph["v_ready"], 3)
                                if doing_head:
                                    pe.wait_ge(ph["rooted"], 1)
                                    pe.wait_ge(ph["centred"], 1)
                            if c < XC:
                                ar = r.ar[z][:, c, :, :].rearrange("p q n -> p (q n)")
                                pe.matmul(psum[:, b, 0:2 * BD], r.bbd[z][:, c, :], ar, start=True, stop=True)
                                mm = pe.matmul(psum[:, b, 2 * BD:4 * BD], r.kbd[z][:, c, :], ar, start=True, stop=True)
                            else:
                                pe.matmul(psum[:, b, 0:BD], r.bbd[z][:, c, :], a_of(z, c), start=True, stop=True)
                                mm = pe.matmul(psum[:, b, 2 * BD:3 * BD], r.kbd[z][:, c, :], a_of(z, c), start=True, stop=True)
                            mm.then_inc(ph["a_made"], 1)

            @ph.block.scalar
            def _(act):
                def take():
                    act.wait_ge(ph["proj_ready"], 1)
                    act.activation(r.K, psum[:, 4, :], ACT.Copy).then_inc(ph["k_ready"], 1)
                    yield
                    act.wait_ge(ph["lora_ready"], 1)
                    act.wait_ge(ph["cur_ready"], 2)
                    act.activation(r.sig[0], psum[:, 7, :], ACT.Sigmoid, bias=col(W0)).then_inc(ph["sig_ready"], 1)
                    yield
                    act.wait_ge(ph["proj_ready"], 3)
                    if doing_head:
                        act.wait_ge(ph["gate_kept"], 1)
                    act.activation(r.Rr, psum[:, 5, 0:S], ACT.Copy).then_inc(ph["r_ready"], 1)
                    act.activation(r.G, psum[:, 5, S:2 * S], ACT.Copy).then_inc(ph["graw_ready"], 1)
                    act.activation(r.Gs, psum[:, 5, S:2 * S], ACT.Sigmoid).then_inc(ph["g_ready"], 1)
                    act.wait_ge(ph["lora_ready"], 2)
                    act.activation(r.al[0], psum[:, 7, :], ACT.Sigmoid, bias=col(A0)).then_inc(ph["sig_ready"], 1)
                    yield
                    act.wait_ge(ph["lora_ready"], 3)
                    act.activation(r.sig[1], psum[:, 4, :], ACT.Sigmoid, bias=col(W0 + 1)).then_inc(ph["sig_ready"], 1)
                    act.wait_ge(ph["kk_floored"], 1)
                    act.activation(r.KK, r.KK, ACT.Sqrt).then_inc(ph["kk_rooted"], 1)
                    yield
                    act.wait_ge(ph["lora_ready"], 4)
                    act.activation(r.al[1], psum[:, 7, :], ACT.Sigmoid, bias=col(A0 + 1)).then_inc(ph["sig_ready"], 1)
                    yield

                work = take() if doing_tail else iter(())
                if doing_head:
                    for j in range(4):
                        act.wait_ge(ph["b_turned"], j + 1)
                        act.activation(four(r.B[j // 2], j % 2), bank(j), ACT.Copy).then_inc(ph["b_ready"], 1)
                    for m in range(LEVELS):
                        for j in range(4):
                            z, half = j // 2, j % 2
                            act.wait_ge(ph["t_turned"], 4 * m + j + 1)
                            if m:
                                act.wait_ge(ph["u_made"], 4 * (m - 1) + j + 1)
                            act.activation(four(r.T[z], half), bank((4 if m == 0 else 0) + j), ACT.Copy).then_inc(ph["t_level"], 1)
                    for n in range(C):
                        for z in range(2):
                            c = order[z][n]
                            act.wait_ge(ph[f"rhs_made_{z}"], n + 1)
                            if n:
                                act.wait_ge(ph[f"u_made_{z}"], n)
                            act.activation(r.Rs[z], psum[:, z, 0:BD], ACT.Copy).then_inc(ph[f"rhs_{z}"], 1)
                        for z in range(2):
                            c = order[z][n]
                            if 0 < n < C - 1:
                                act.activation(r.DS[z], r.St[z], ACT.Copy, scale=r.D[:, z, c:c + 1]).then_inc(ph[f"ds_{z}"], 1)
                        if n in (2, 3, 5, 6, 7):
                            next(work, None)
                for _ in work:
                    pass
                if doing_tail:
                    act.wait_ge(ph["proj_ready"], 4)
                    act.wait_ge(ph["zeroed"], 1)
                    for h in range(2):
                        act.activation(r.vbd[heads[h], :, h * CH:(h + 1) * CH], chunks(psum[heads[h], 6, :]), ACT.Copy).then_inc(ph["v_ready"], 1)
                    if doing_head:
                        act.wait_ge(ph["bonus_read"], 1)
                    act.activation(r.V, psum[:, 6, 0:S], ACT.Copy).then_inc(ph["v_ready"], 1)
                    for z in range(2):
                        act.wait_ge(ph["l_ready"], 2 * z + 2)
                        act.activation(r.E3[z], r.L[z], ACT.Exp, scale=DECAY).then_inc(ph["e_ready"], 1)
                        act.wait_ge(ph["lex_ready"], z + 1)
                        act.activation(r.E1[z], r.L[z], ACT.Exp, scale=-DECAY).then_inc(ph["e_ready"], 1)
                        act.activation(r.E2[z], r.E2[z], ACT.Exp, scale=-DECAY).then_inc(ph["e_ready"], 1)
                    for q in range(2):
                        act.wait_ge(ph["v_turned"], q + 1)
                        act.activation(four(r.Vt, q), bank(4 + q), ACT.Copy).then_inc(ph["vt_ready"], 1)
                if doing_head:
                    act.wait_ge(ph["var_made"], 1)
                    act.activation(r.cen, psum[:, 1, 0:S], ACT.Sqrt, bias=self.gn_eps[:, 0:1]).then_inc(ph["rooted"], 1)
                if doing_tail:
                    for z in range(2):
                        for q in range(4):
                            act.wait_ge(ph["tok_turned"], 4 * z + q + 1)
                            act.activation(four((r.btok, r.ktok)[q // 2][z], q % 2), bank((7, 2, 4, 5)[q]), ACT.Copy).then_inc(ph["tok_ready"], 1)

            @ph.block.gpsimd
            def _(pool):
                if doing_head:
                    pool.tensor_tensor(r.Gh, r.G, r.Gs, ALU.mult).then_inc(ph["gate_kept"], 1)
                if not doing_tail:
                    return
                if doing_head:
                    pool.wait_ge(ph["r_made"], 4 * LEVELS)
                for t in r.bbd:
                    pool.memset(t[:, :, :], 0.0).then_inc(ph["zeroed"], 1)
                if not doing_head:
                    for t in (*r.kbd, r.ac[0], r.ac[1]):
                        pool.memset(t[:, :, :], 0.0).then_inc(ph["zeroed"], 1)
                    for t in (r.ar[0], r.ar[1]):
                        pool.memset(t[:, :, :, :], 0.0).then_inc(ph["zeroed"], 1)
                pool.wait_ge(ph["kk_weighted"], 1)
                pool.tensor_tensor(r.kn, r.kw, r.kw, ALU.mult).then_inc(ph["kk_squared"], 1)
                for z in range(2):
                    pool.wait_ge(ph["l_ready"], 2 * z + 2)
                    pool.tensor_tensor(r.E2[z], r.L[z], r.sig[z], ALU.subtract).then_inc(ph["lex_ready"], 1)
                    pool.wait_ge(ph["kd_scaled"], z + 1)
                    pool.tensor_tensor(r.kd[z], r.kd[z], r.K, ALU.mult).then_inc(ph["kd_ready"], 1)
                for z in range(2):
                    pool.wait_ge(ph["e_ready"], 3 * z + 1)
                    pool.wait_ge(ph["kd_ready"], z + 1)
                    if z == 0:
                        pool.wait_ge(ph["v_turned"], 2)
                        pool.wait_ge(ph["zeroed"], 2 if doing_head else 8)
                    for h in range(2):
                        hs, cs = heads[h], slice(h * CH, (h + 1) * CH)
                        if z or h:
                            pool.wait_ge(ph["k_laid"], 2 * z + h)
                        pool.tensor_tensor(r.kbd[z][hs, :, cs], chunks(r.kd[z][hs, :]), chunks(r.E3[z][hs, :]), ALU.mult).then_inc(ph["k_laid"], 1)
                pool.wait_ge(ph["k_laid"], 4)
                for z in range(2):
                    pool.wait_ge(ph["r_ready"], 1)
                    if doing_head:
                        pool.wait_ge(ph["bonus_made"], 1)
                    pool.tensor_tensor(r.prod[z], r.kd[z][:, 0:S], r.Rr, ALU.mult).then_inc(ph["prod_raw"], 1)
                for z in range(2):
                    pool.wait_ge(ph["prod_raw"], z + 1)
                    pool.tensor_scalar(r.prod[z], r.prod[z], col(RK), None, ALU.mult).then_inc(ph["prod_ready"], 1)
                pool.wait_ge(ph["aab_ready"], C)
                for j in (0, 1):
                    self.first_pair(ph, pool, r, j, "first_pairs")
                for j in (0, 1):
                    pool.wait_ge(ph["first_pairs"], j + 1)
                    self.add_identity(pool, r, j).then_inc(ph["u_begun"], 1)

            @ph.block.vector
            def _(dve):
                def prepare():
                    dve.tensor_copy(r.cur[:, 0:9], prm[:, 0:9, bass.ds(tail, 1)].rearrange("p j a -> p (j a)")).then_inc(ph["cur_ready"], 1)
                    dve.wait_ge(ph["cur_ready"], 1)
                    dve.tensor_scalar(r.cur[:, OMK:OMK + 1], r.cur[:, KA:KA + 1], -1.0, 1.0, ALU.mult, ALU.add).then_inc(ph["cur_ready"], 1)
                    dve.wait_ge(ph["cur_ready"], 2)
                    yield
                    dve.wait_ge(ph["k_ready"], 1)
                    dve.tensor_scalar(r.kw, r.K, col(KKW), None, ALU.mult).then_inc(ph["kk_weighted"], 1)
                    yield
                    dve.wait_ge(ph["kk_summed"], 1)
                    dve.tensor_scalar(r.KK, psum[:, 4, :], 1e-24, None, ALU.max).then_inc(ph["kk_floored"], 1)
                    yield
                    dve.wait_ge(ph["sig_ready"], 1)
                    self.decay_sums(ph, dve, r, 0)
                    yield
                    dve.wait_ge(ph["sig_ready"], 2)
                    dve.tensor_scalar(r.kd[0], r.al[0], col(KA), col(OMK), ALU.mult, ALU.add).then_inc(ph["kd_scaled"], 1)
                    dve.wait_ge(ph["kk_rooted"], 1)
                    dve.reciprocal(r.kn, r.KK).then_inc(ph["kk_inverse"], 1)
                    yield
                    dve.wait_ge(ph["kk_inverse"], 1)
                    dve.tensor_tensor(r.KK, r.kw, r.kn, ALU.mult).then_inc(ph["kk_ready"], 1)
                    dve.wait_ge(ph["sig_ready"], 3)
                    self.decay_sums(ph, dve, r, 1)
                    yield
                    dve.wait_ge(ph["sig_ready"], 4)
                    dve.tensor_scalar(r.kd[1], r.al[1], col(KA), col(OMK), ALU.mult, ALU.add).then_inc(ph["kd_scaled"], 1)
                    yield

                work = prepare() if doing_tail else iter(())
                if doing_head:
                    dve.tensor_copy(r.ln[:, :], prm[:, LNW:LNW + 2, bass.ds(head, 1)].rearrange("p j a -> p (j a)")).then_inc(ph["ln_ready"], 1)
                    for j in (2, 3):
                        self.first_pair(ph, dve, r, j)
                    for j in (2, 3):
                        dve.wait_ge(ph["pairs"], j - 1)
                        self.add_identity(dve, r, j).then_inc(ph["u_level"], 1)
                    dve.wait_ge(ph["bonus_made"], 1)
                    dve.tensor_tensor(r.BV, psum[:, 7, 0:S], r.V, ALU.mult).then_inc(ph["bonus_read"], 1)
                    for m in range(LEVELS):
                        for j in range(4):
                            z, half = j // 2, j % 2
                            dve.wait_ge(ph["r_made"], 4 * m + j + 1)
                            dve.tensor_tensor(four(r.R[z], half), bank(j), self.level[:, z, m + 1, :].unsqueeze(1).to_broadcast([P, 4, BD]),
                                              ALU.mult).then_inc(ph["r_level"], 1)
                        for j in range(4):
                            z, half = j // 2, j % 2
                            dve.wait_ge(ph["u_made"], 4 * m + j + 1)
                            dve.tensor_tensor(four(r.U[z], half), bank(4 + j), four(r.U[z], half), ALU.add).then_inc(ph["u_level"], 1)
                    next(work, None)
                    for n in range(C):
                        for z in range(2):
                            dve.wait_ge(ph[f"u_made_{z}"], n + 1)
                            if n:
                                dve.wait_ge(ph[f"state_made_{z}"], n)
                                if order[z][n - 1] < XC:
                                    dve.wait_ge(ph[f"y_made_{z}"], n - XC)
                            dve.tensor_copy(r.Us[z], psum[:, z, BD:2 * BD]).then_inc(ph[f"u_{z}"], 1)
                        for z in range(2):
                            if n == C - 1:
                                continue
                            c = order[z][n]
                            dve.wait_ge(ph[f"state_made_{z}"], n + 1)
                            if c < XC:
                                dve.wait_ge(ph[f"y_made_{z}"], n - XC + 1)
                            if n == 0:
                                dve.tensor_scalar(r.St[z], psum[:, z, 2 * BD:3 * BD], r.D[:, z, c:c + 1], None, ALU.mult).then_inc(ph[f"state_{z}"], 1)
                            else:
                                dve.wait_ge(ph[f"ds_{z}"], n)
                                dve.scalar_tensor_tensor(out=r.St[z], in0=psum[:, z, 2 * BD:3 * BD], scalar=r.D[:, z, c:c + 1], in1=r.DS[z],
                                                         op0=ALU.mult, op1=ALU.add).then_inc(ph[f"state_{z}"], 1)
                        if n >= 3:
                            next(work, None)
                    for z in range(2):
                        dve.wait_ge(ph[f"y_made_{z}"], XC)
                    for h in range(2):
                        dve.tensor_copy(chunks(r.cen[heads[h], :]), bank(2)[heads[h], :, h * CH:(h + 1) * CH]).then_inc(ph["y_half"], 1)
                    for h in range(2):
                        dve.wait_ge(ph["y_half"], h + 1)
                        dve.tensor_tensor(chunks(r.y[heads[h], :]), bank(3)[heads[h], :, h * CH:(h + 1) * CH], chunks(r.cen[heads[h], :]), ALU.add).then_inc(ph["y_ready"], 1)
                for _ in work:
                    pass
                if doing_head:
                    dve.wait_ge(ph["mean_made"], 1)
                    dve.wait_ge(ph["y_ready"], 2)
                    dve.tensor_tensor(r.yn, r.y, psum[:, 0, 0:S], ALU.subtract).then_inc(ph["centred"], 1)
                    dve.wait_ge(ph["centred"], 1)
                    dve.tensor_tensor(r.y, r.yn, r.yn, ALU.mult).then_inc(ph["squared"], 1)
                if doing_tail:
                    dve.wait_ge(ph["kk_ready"], 1)
                    dve.wait_ge(ph["zeroed"], 2 if doing_head else 8)
                    for z in range(2):
                        dve.tensor_tensor(r.al[z], r.al[z], r.KK, ALU.mult).then_inc(ph["b_vec"], 1)
                    for z in range(2):
                        dve.wait_ge(ph["e_ready"], 3 * z + 1)
                        dve.wait_ge(ph["b_vec"], z + 1)
                        for h in range(2):
                            hs, cs = heads[h], slice(h * CH, (h + 1) * CH)
                            dve.tensor_tensor(r.bbd[z][hs, :, cs], chunks(r.al[z][hs, :]), chunks(r.E3[z][hs, :]), ALU.mult).then_inc(ph["b_laid"], 1)
                        dve.wait_ge(ph["e_ready"], 3 * z + 3)
                        for h in range(2):
                            hs, cs = heads[h], slice(h * CH, (h + 1) * CH)
                            for dst, o in ((r.ar[z][hs, :, 0, cs], 0), (r.ac[z][hs, :, cs], S)):
                                dve.scalar_tensor_tensor(out=dst, in0=chunks(r.KK[hs, o:o + S]), scalar=-1.0, in1=chunks(r.E2[z][hs, o:o + S]),
                                                         op0=ALU.mult, op1=ALU.mult).then_inc(ph["ar_laid"], 1)
                            dve.tensor_tensor(r.ar[z][hs, :, 1, cs], chunks(r.Rr[hs, :]), chunks(r.E1[z][hs, 0:S]), ALU.mult).then_inc(ph["ar_laid"], 1)
                        dve.tensor_copy(r.D[:, z, :], chunks(r.E1[z])[:, :, CH - 1 if z == 0 else 0]).then_inc(ph["ar_laid"], 1)
                    for z in range(2):
                        for c in range(C):
                            n = z * C + c
                            b = (0, 1, 6)[n % 3]
                            dve.wait_ge(ph["a_made"], n + 1)
                            dve.tensor_tensor(r.R[z][:, c, :], psum[:, b, 0:BD], self.strict[:, z, 1, :], ALU.mult).then_inc(ph["aab_ready"], 1)
                            if c < XC:
                                dve.tensor_tensor(r.ax[z][:, c, :, :], psum[:, b, BD:4 * BD].rearrange("p (q n) -> p q n", q=3), self.strict[:, z, :, :],
                                                  ALU.mult).then_inc(ph["a_ready"], 1)
                            else:
                                dve.tensor_tensor(r.akc[z][:, c - XC, :], psum[:, b, 2 * BD:3 * BD], self.strict[:, z, 1, :], ALU.mult).then_inc(ph["a_ready"], 1)
                        if z == 0 and doing_head:
                            self.rwkv_gate(ph, dve, r, head, uT)
                elif doing_head:
                    self.rwkv_gate(ph, dve, r, head, uT)

    def first_pair(self, ph, eng, r, j, done="pairs"):
        z, four = j // 2, slice(4 * (j % 2), 4 * (j % 2) + 4)
        eng.tensor_tensor(r.U[z][:, four, :], r.R[z][:, four, :], self.level[:, z, 0, :].unsqueeze(1).to_broadcast([P, 4, self.BD]),
                          ALU.mult).then_inc(ph[done], 1)

    def add_identity(self, eng, r, j):
        us = r.U[j // 2][:, 4 * (j % 2):4 * (j % 2) + 4, :]
        return eng.tensor_tensor(us, us, self.ident[:, :].unsqueeze(1).to_broadcast([P, 4, self.BD]), ALU.add)

    def decay_sums(self, ph, dve, r, z):
        for o in (0, S):
            out, sig = r.L[z][:, o:o + S], r.sig[z][:, o:o + S]
            if z:
                out, sig = out[:, ::-1], sig[:, ::-1]
            dve.tensor_tensor_scan(out, self.no_start[:, :], sig, 0.0, ALU.mult, ALU.add).then_inc(ph["l_ready"], 1)

    def rwkv_gate(self, ph, dve, r, head, uT):
        yn = r.yn
        dve.wait_ge(ph["rooted"], 1)
        dve.reciprocal(r.y, r.cen).then_inc(ph["gn_inverse"], 1)
        dve.wait_ge(ph["gn_inverse"], 1)
        dve.tensor_tensor(yn, yn, r.y, ALU.mult).then_inc(ph["gn_scaled"], 1)
        dve.wait_ge(ph["gn_scaled"], 1)
        dve.wait_ge(ph["ln_ready"], 1)
        dve.tensor_scalar(yn, yn, r.ln[:, 0:1], r.ln[:, 1:2], ALU.mult, ALU.add).then_inc(ph["gn_scaled"], 1)
        dve.wait_ge(ph["gn_scaled"], 2)
        dve.wait_ge(ph["bonus_read"], 1)
        dve.tensor_tensor(yn, yn, r.BV, ALU.add).then_inc(ph["gn_scaled"], 1)
        dve.wait_ge(ph["gn_scaled"], 3)
        dve.wait_ge(ph["gate_kept"], 1)
        dve.tensor_tensor(r.uo, yn, r.Gh, ALU.mult).then_inc(ph["u_out"], 1)

    def rwkv_layer(self):
        a = self.a
        self.C, self.XC, self.BD = 2 * S // CH, S // CH, 2 * CH
        self.adaln(0, 2)
        with ExitStack() as ctx:
            u_dram = self.nc.dram_tensor("u_scratch", [P, ET, S], F32, kind="Internal").ap()
            with ExitStack() as inner:
                sb = self.scratch(inner)
                mu, prm = sb(6 * KT), sb(9 * ET)
                mix = {"r": sb(KT, S), "k": sb(KT, 2 * S), "v": sb(KT, 2 * S), "g": sb(KT, S)}
                lora = {"w": sb(2 * S), "a": sb(2 * S)}

                def rows(name):
                    v = a[name]
                    if len(v.shape) == 2:
                        v = v.rearrange("a b -> (a b)")
                    return v.rearrange("(n p) -> n p", p=P)
                self.turn_rows([rows("l0_mu")], mu)
                self.turn_rows([rows("l0_" + n) for n in ("w0", "a0", "k_k", "k_a", "r_k", "ln_w", "ln_b")], prm)
                with ExitStack() as early:
                    ctx_x = self.scratch(early)(NT, D)
                    with self.phase() as ph:
                        @ph.block.sync
                        def _(sp):
                            sp.dma_start(ctx_x[:, :, :], a["ctx"][0].rearrange("(t p) d -> p t d", p=P)).then_inc(ph["ctx_in"], 16)
                            sp.wait_ge(ph["ctx_in"], 16)
                    self.norm_first(self.x, 0, 0)
                    self.norm_first(ctx_x, 1, S)
                self.rwkv_mixes(mix, lora, mu)
                with ExitStack() as cst:
                    sb = self.scratch(cst)
                    self.strict, self.level, self.no_start = sb(2, 3, P), sb(2, 6, P), sb(S)
                    self.same_head, self.head_mean, self.gn_eps = sb(P), sb(P), sb(1)
                    room = self.rwkv_room(sb)
                    with self.phase() as ph:
                        @ph.block.sync
                        def _(sp):
                            for dst, name in ((self.strict[:, :, :, :], "k_strict"), (self.level[:, :, :, :], "k_level"), (self.no_start[:, :], "k_no_start"),
                                              (self.same_head[:, :], "k_same_head"), (self.head_mean[:, :], "k_head_mean")):
                                sp.dma_start(dst, a[name]).then_inc(ph["constants_in"], 16)
                            sp.wait_ge(ph["constants_in"], 80)

                        @ph.block.vector
                        def _(dve):
                            dve.memset(self.gn_eps[:, :], GN_EPS).then_inc(ph["eps_set"], 1)
                            dve.wait_ge(ph["eps_set"], 1)
                    prm3 = prm[:, :].rearrange("p (j e) -> p j e", e=ET)
                    self.rwkv_step(room, None, 0, mix, lora, prm3, u_dram)
                    with self.nc.Fori(0, ET - 1) as i:
                        self.rwkv_step(room, i, i + 1, mix, lora, prm3, u_dram)
                    self.rwkv_step(room, ET - 1, None, mix, lora, prm3, u_dram)
            uT = self.scratch(ctx)(ET, S)
            with self.phase() as ph:
                @ph.block.sync
                def _(sp):
                    sp.dma_start(self.x[:, :, :], a["x"][0].rearrange("(t p) d -> p t d", p=P)).then_inc(ph["x_in"], 16)
                    sp.dma_start(uT[:, :, :], u_dram).then_inc(ph["x_in"], 16)
                    sp.wait_ge(ph["x_in"], 32)
            self.out_first(0, uT)


    def hyena_hidden(self, hdn):
        a, psum = self.a, self.psum
        W = HW
        TWO_PI, ROUND = float(2 * np.pi), 1.5 * 2.0 ** 23
        LIMIT = 3.1415925
        with ExitStack() as ctx:
            sb = self.scratch(ctx)
            z, w1, w23 = sb(S), sb(W), sb(2, W)
            b, turns = sb(4), sb(S)
            with self.phase() as ph:
                @ph.block.sync
                def _(sp):
                    sp.dma_start(z[0:EMB, :], a["k_pos"]).then_inc(ph["hidden_in"], 16)
                    sp.dma_start(w1[0:EMB, :], a["l1_f_w1"]).then_inc(ph["hidden_in"], 16)
                    for j, name in enumerate(("l1_f_w2", "l1_f_w3")):
                        sp.dma_start(w23[0:W, j, :], a[name]).then_inc(ph["hidden_in"], 16)
                    with self.nc.allow_non_contiguous_dma(reason="64-element vectors"):
                        for j, name in enumerate(("l1_f_b1", "l1_f_b2", "l1_f_b3", "l1_sin_freq")):
                            sp.dma_start(b[0:W, j:j + 1], a[name].rearrange("(p a) -> p a", a=1)).then_inc(ph["hidden_in"], 16)

                @ph.block.tensor
                def _(pe):
                    pe.wait_ge(ph["hidden_in"], 16 * 8)
                    pe.matmul(psum[0:W, 0, 0:S], w1[0:EMB, :], z[0:EMB, :], start=True, stop=True).then_inc(ph["layer_made"], 1)
                    for j in range(2):
                        pe.wait_ge(ph["layer_ready"], j + 1)
                        pe.matmul(psum[0:W, j + 1, 0:S], w23[0:W, j, :], hdn[0:W, :], start=True, stop=True).then_inc(ph["layer_made"], 1)

                @ph.block.vector
                def _(dve):
                    dve.wait_ge(ph["hidden_in"], 16 * 8)
                    h, t = hdn[0:W, :], turns[0:W, :]
                    n = 0

                    def chained(ins):
                        nonlocal n
                        n += 1
                        ins.then_inc(ph["reduced"], 1)
                        dve.wait_ge(ph["reduced"], n)
                    for j in range(3):
                        dve.wait_ge(ph["layer_made"], j + 1)
                        chained(dve.tensor_scalar(h, psum[0:W, j, 0:S], b[0:W, j:j + 1], b[0:W, 3:4], ALU.add, ALU.mult))
                        chained(dve.tensor_scalar(t, h, 1.0 / TWO_PI, ROUND, ALU.mult, ALU.add))
                        chained(dve.tensor_scalar(t, t, -ROUND, -TWO_PI, ALU.add, ALU.mult))
                        chained(dve.tensor_tensor(h, h, t, ALU.add))
                        dve.tensor_scalar(h, h, LIMIT, -LIMIT, ALU.min, ALU.max).then_inc(ph["angle_ready"], 1)
                        dve.wait_ge(ph["layer_ready"], j + 1)

                @ph.block.scalar
                def _(act):
                    for j in range(3):
                        act.wait_ge(ph["angle_ready"], j + 1)
                        act.activation(hdn[0:W, :], hdn[0:W, :], ACT.Sin).then_inc(ph["layer_ready"], 1)

    def hyena_tiles(self, i, U, h_hi, h_lo, hdn, prm, dft, idft, uT):
        a, psum, ident = self.a, self.psum, self.ident
        BUFS = 4
        with ExitStack() as ctx:
            sb = self.scratch(ctx)
            w_hi, w_lo = self.split_pair(ctx, BUFS, KT, P)
            cur = sb(U, 13)
            fw, win = [sb(2, P) for _ in range(2)], [sb(NT, P) for _ in range(2)]
            pad = [sb(3, S + 2) for _ in range(2)]
            gate, conv = [sb(S) for _ in range(2)], [sb(3, S) for _ in range(2)]
            ut = [sb(NT, P) for _ in range(2)]
            hw, fsum, fdif = sb(NT, 2, P), sb(NT, P), sb(NT, P)
            AB, m1, m2, Y, Yf = sb(2, S), sb(2, S), sb(2, S), sb(2, S), sb(4, P)
            long = sb(S)
            w = self.ring[:, :, :].rearrange("p s (k j n) -> p s k j n", j=4, n=P)
            COL = (2, 1, 0, 3)
            with self.phase() as ph:
                @ph.block.sync
                def _(sp):
                    wv = a["l1_w_in"].rearrange("(k p) n -> p k n", p=P)
                    for u in range(U):
                        ct = i * U + u
                        for j in range(4):
                            if u >= SLOTS:
                                sp.wait_ge(ph["w_split"], 4 * (u - SLOTS) + j + 1)
                            sp.dma_start(w[:, u % SLOTS, :, j, :], wv[:, :, bass.ds(ct * P + COL[j] * E, P)]).then_inc(ph[f"w_in_{u % SLOTS}_{j}"], 16)
                        if u >= 2:
                            sp.wait_ge(ph["filter_made"], u - 1)
                            sp.wait_ge(ph["windowed"], u - 1)
                        sp.dma_start(fw[u % 2][0:HW, :, :], a["l1_f_w4"].rearrange("p (b n) -> p b n", b=2)[:, :, bass.ds(ct * P, P)]).then_inc(ph[f"filter_in_{u % 2}"], 16)
                        sp.dma_start(win[u % 2][:, :, :], a["k_window"].rearrange("(t p) n -> p t n", p=P)[:, :, bass.ds(ct * P, P)]).then_inc(ph[f"filter_in_{u % 2}"], 16)

                @ph.block.tensor
                def _(pe):
                    def piece(u, j):
                        if u >= U:
                            return
                        bank = 2 * (u % 2) + j // 2
                        pe.wait_ge(ph["w_split"], 4 * u + j + 1)
                        if u >= 2 and j % 2 == 0:
                            pe.wait_ge(ph["copied"], 3 * (u - 2) + (1, 3)[j // 2])
                        for k in range(KT):
                            for n, (wp, h) in enumerate(((w_hi, h_hi), (w_hi, h_lo), (w_lo, h_hi))):
                                mm = pe.matmul(psum[:, bank, (j % 2) * S:(j % 2 + 1) * S], wp[:, j, k, :], h[:, k, :],
                                               start=(k == 0 and n == 0), stop=(k == KT - 1 and n == 2))
                        mm.then_inc(ph["proj_ready"], 1)
                    for j in range(4):
                        piece(0, j)
                    for u in range(U):
                        pe.wait_ge(ph[f"filter_in_{u % 2}"], 32 * (u // 2 + 1))
                        if u:
                            pe.wait_ge(ph["yf_ready"], u)
                        for t in range(NT):
                            mm = pe.matmul(psum[:, 4, t * S:(t + 1) * S], hdn[0:HW, t * P:(t + 1) * P], fw[u % 2][0:HW, :, :].rearrange("p b n -> p (b n)"),
                                           start=True, stop=True)
                        mm.then_inc(ph["filter_made"], 1)
                        piece(u + 1, 0)
                        pe.wait_ge(ph["product_ready"], u + 1)
                        if u:
                            pe.wait_ge(ph["long_read"], u)
                        for t in range(NT):
                            mm = pe.transpose(psum[:, 5, t * P:(t + 1) * P], conv[u % 2][:, 0, t * P:(t + 1) * P], ident[:, :])
                        mm.then_inc(ph["ut_made"], 1)
                        piece(u + 1, 1)
                        pe.wait_ge(ph["fsum_ready"], u + 1)
                        pe.wait_ge(ph["fdif_ready"], u + 1)
                        pe.wait_ge(ph["ut_ready"], u + 1)
                        if u:
                            pe.wait_ge(ph["cd_read"], 2 * u)
                        for src, o in ((fsum, 0), (fdif, S)):
                            for t in range(NT):
                                mm = pe.matmul(psum[:, 7, o:o + S], src[:, t, :], dft[:, t, o:o + S], start=(t == 0), stop=(t == NT - 1))
                        mm.then_inc(ph["cd_made"], 1)
                        for t in range(NT):
                            mm = pe.matmul(psum[:, 6, :], ut[u % 2][:, t, :], dft[:, t, :], start=(t == 0), stop=(t == NT - 1))
                        mm.then_inc(ph["ab_made"], 1)
                        piece(u + 1, 2)
                        pe.wait_ge(ph["spectrum_ready"], 2 * u + 2)
                        for q in range(4):
                            mm = pe.transpose(psum[:, 4, q * P:(q + 1) * P], Y[:, q // 2, (q % 2) * P:(q % 2 + 1) * P], ident[:, :])
                        mm.then_inc(ph["yf_made"], 1)
                        piece(u + 1, 3)
                        pe.wait_ge(ph["yf_ready"], u + 1)
                        for q in range(4):
                            mm = pe.matmul(psum[:, 5, S:2 * S], Yf[:, q, :], idft[:, q, :], start=(q == 0), stop=(q == 3))
                        mm.then_inc(ph["long_made"], 1)

                @ph.block.scalar
                def _(act):
                    def load(u):
                        if u >= U:
                            return
                        b, d = 2 * (u % 2), u % 2
                        act.wait_ge(ph["edges"], 2)
                        act.wait_ge(ph["proj_ready"], 4 * u + 2)
                        if u >= 2:
                            act.wait_ge(ph["tile_done"], u - 1)
                        act.activation(pad[d][:, 0:2, 1:S + 1], psum[:, b, :].rearrange("p (j s) -> p j s", j=2), ACT.Copy).then_inc(ph["copied"], 1)
                        act.wait_ge(ph["proj_ready"], 4 * u + 4)
                        act.activation(pad[d][:, 2, 1:S + 1], psum[:, b + 1, 0:S], ACT.Copy).then_inc(ph["copied"], 1)
                        act.activation(gate[d][:, :], psum[:, b + 1, S:2 * S], ACT.Silu).then_inc(ph["copied"], 1)

                    def round_piece(u, j):
                        if u >= U:
                            return
                        act.wait_ge(ph[f"w_in_{u % SLOTS}_{j}"], 16 * (u // SLOTS + 1))
                        if u:
                            act.wait_ge(ph["proj_ready"], 4 * (u - 1) + j + 1)
                        act.activation(w_hi[:, j, :, :], w[:, u % SLOTS, :, j, :], ACT.Copy).then_inc(ph["w_rounded"], 1)
                    for j in range(4):
                        round_piece(0, j)
                    for j in range(2):
                        round_piece(1, j)
                    load(0)
                    for j in range(2, 4):
                        round_piece(1, j)
                    for u in range(U):
                        act.wait_ge(ph["ut_made"], u + 1)
                        act.activation(ut[u % 2][:, :, :], psum[:, 5, 0:S].rearrange("p (t n) -> p t n", t=NT), ACT.Copy).then_inc(ph["ut_ready"], 1)
                        round_piece(u + 2, 0)
                        act.wait_ge(ph["ab_made"], u + 1)
                        if u:
                            act.wait_ge(ph["cd_read"], 2 * u)
                        act.activation(AB[:, :, :], psum[:, 6, :].rearrange("p (q s) -> p q s", q=2), ACT.Copy).then_inc(ph["ab_ready"], 1)
                        round_piece(u + 2, 1)
                        act.wait_ge(ph["yf_made"], u + 1)
                        if u:
                            act.wait_ge(ph["long_made"], u)
                        act.activation(Yf[:, :, :], psum[:, 4, :].rearrange("p (q n) -> p q n", q=4), ACT.Copy).then_inc(ph["yf_ready"], 1)
                        round_piece(u + 2, 2)
                        load(u + 1)
                        round_piece(u + 2, 3)

                @ph.block.gpsimd
                def _(pool):
                    for d in range(2):
                        pool.memset(pad[d][:, :, 0:S + 2:S + 1], 0.0).then_inc(ph["edges"], 1)

                @ph.block.vector
                def _(dve):
                    for u in range(U):
                        dve.tensor_copy(cur[:, u, :], prm[:, :, bass.ds(i * U + u, 1)].rearrange("p j a -> p (j a)")).then_inc(ph["cur_ready"], 1)

                    def rest_of_piece(u, j):
                        if u >= U:
                            return
                        dve.wait_ge(ph["w_rounded"], 4 * u + j + 1)
                        dve.tensor_tensor(w_lo[:, j, :, :], w[:, u % SLOTS, :, j, :], w_hi[:, j, :, :], ALU.subtract).then_inc(ph["w_split"], 1)
                    def convolve(u):
                        if u >= U:
                            return
                        d = u % 2
                        for j in range(3):
                            if j < 2:
                                dve.wait_ge(ph["copied"], 3 * u + 1)
                            else:
                                dve.wait_ge(ph["copied"], 3 * u + 2)
                            tap = [cur[:, u, 3 * q + COL[j]:3 * q + COL[j] + 1] for q in range(4)]
                            dve.tensor_scalar(conv[d][:, j, :], pad[d][:, j, 1:S + 1], tap[1], tap[3], ALU.mult, ALU.add).then_inc(ph["taps"], 1)
                        for q, o in ((0, 0), (2, 2)):
                            for j in range(3):
                                dve.wait_ge(ph["taps"], 9 * u + (3 if q else 0) + j + 1)
                                tap = cur[:, u, 3 * q + COL[j]:3 * q + COL[j] + 1]
                                dve.scalar_tensor_tensor(out=conv[d][:, j, :], in0=pad[d][:, j, o:o + S], scalar=tap, in1=conv[d][:, j, :],
                                                         op0=ALU.mult, op1=ALU.add).then_inc(ph["taps"], 1)
                        dve.wait_ge(ph["taps"], 9 * u + 8)
                        dve.tensor_tensor(conv[d][:, 0, :], conv[d][:, 0, :], conv[d][:, 1, :], ALU.mult).then_inc(ph["product_ready"], 1)
                    for u in range(2):
                        for j in range(4 if u == 0 else 2):
                            rest_of_piece(u, j)
                    dve.wait_ge(ph["cur_ready"], U)
                    for u in range(U):
                        d = u % 2
                        dve.wait_ge(ph["filter_made"], u + 1)
                        dve.wait_ge(ph[f"filter_in_{u % 2}"], 32 * (u // 2 + 1))
                        dve.tensor_tensor(hw[:, :, :, :], psum[:, 4, :].rearrange("p (t b n) -> p t b n", t=NT, b=2),
                                          win[d][:, :, :].unsqueeze(2).to_broadcast([P, NT, 2, P]), ALU.mult).then_inc(ph["windowed"], 1)
                        dve.wait_ge(ph["windowed"], u + 1)
                        if u:
                            dve.wait_ge(ph["cd_made"], u)
                        dve.tensor_tensor(fsum[:, :, :], hw[:, :, 0, :], hw[:, :, 1, :], ALU.add).then_inc(ph["fsum_ready"], 1)
                        dve.tensor_tensor(fdif[:, :, :], hw[:, :, 1, :], hw[:, :, 0, :], ALU.subtract).then_inc(ph["fdif_ready"], 1)
                        if u == 0:
                            for j in range(2, 4):
                                rest_of_piece(1, j)
                            convolve(0)
                        rest_of_piece(u + 2, 0)
                        dve.wait_ge(ph["ab_ready"], u + 1)
                        dve.wait_ge(ph["cd_made"], u + 1)
                        if u:
                            dve.wait_ge(ph["spectrum_ready"], 2 * u)
                        for m, o in ((m1, 0), (m2, S)):
                            dve.tensor_tensor(m[:, :, :], AB[:, :, :], psum[:, 7, o:o + S].unsqueeze(1).to_broadcast([P, 2, S]), ALU.mult).then_inc(ph["cd_read"], 1)
                        dve.wait_ge(ph["cd_read"], 2 * u + 2)
                        if u:
                            dve.wait_ge(ph["yf_made"], u)
                        dve.tensor_tensor(Y[:, 0, :], m1[:, 0, :], m2[:, 1, :], ALU.add).then_inc(ph["spectrum_ready"], 1)
                        dve.tensor_tensor(Y[:, 1, :], m2[:, 0, :], m1[:, 1, :], ALU.subtract).then_inc(ph["spectrum_ready"], 1)
                        rest_of_piece(u + 2, 1)
                        rest_of_piece(u + 2, 2)
                        convolve(u + 1)
                        dve.wait_ge(ph["product_ready"], u + 1)
                        dve.wait_ge(ph["long_made"], u + 1)
                        dve.scalar_tensor_tensor(out=long[:, :], in0=conv[d][:, 0, :], scalar=cur[:, u, 12:13], in1=psum[:, 5, S:2 * S],
                                                 op0=ALU.mult, op1=ALU.add).then_inc(ph["long_read"], 1)
                        dve.wait_ge(ph["long_read"], u + 1)
                        dve.wait_ge(ph["taps"], 9 * u + 9)
                        dve.tensor_tensor(long[:, :], long[:, :], conv[d][:, 2, :], ALU.mult).then_inc(ph["long_gated"], 1)
                        dve.wait_ge(ph["long_gated"], u + 1)
                        dve.wait_ge(ph["copied"], 3 * u + 3)
                        dve.tensor_tensor(uT[:, bass.ds(i * U + u, 1), :].rearrange("p a s -> p (a s)"), long[:, :], gate[d][:, :], ALU.mult).then_inc(ph["tile_done"], 1)
                        rest_of_piece(u + 2, 3)
                    dve.wait_ge(ph["tile_done"], U)

    def hyena_layer(self):
        a = self.a
        U = 8
        self.adaln(1, 1)
        self.norm_first(self.x, 0, 0)
        uT = self.hT[:, :, :].rearrange("p k (a s) -> p (k a) s", s=S)
        if True:
            with ExitStack() as inner:
                sb = self.scratch(inner)
                prm, hdn = sb(13 * ET), sb(S)
                dft, idft = sb(NT, 2 * S), sb(4, S)
                h_hi, h_lo = self.split_pair(inner, KT, S)

                def rows(name):
                    v = a[name]
                    if len(v.shape) == 2:
                        v = v.rearrange("a b -> (a b)")
                    return v.rearrange("(n p) -> n p", p=P)
                self.turn_rows([rows("l1_" + n) for n in ("conv_w", "conv_b", "filter_bias")], prm)
                self.hyena_hidden(hdn)
                with self.phase() as ph:
                    @ph.block.sync
                    def _(sp):
                        sp.dma_start(dft[:, :, :], a["k_dft"]).then_inc(ph["dft_in"], 16)
                        sp.dma_start(idft[:, :, :], a["k_idft"]).then_inc(ph["dft_in"], 16)
                        sp.wait_ge(ph["dft_in"], 32)

                    @ph.block.scalar
                    def _(act):
                        for k in range(0, KT, 2):
                            act.activation(h_hi[:, k:k + 2, :], self.hT[:, k:k + 2, 0:S], ACT.Copy).then_inc(ph["h_rounded"], 1)

                    @ph.block.vector
                    def _(dve):
                        for k in range(0, KT, 2):
                            dve.wait_ge(ph["h_rounded"], k // 2 + 1)
                            dve.tensor_tensor(h_lo[:, k:k + 2, :], self.hT[:, k:k + 2, 0:S], h_hi[:, k:k + 2, :], ALU.subtract).then_inc(ph["h_split"], 1)
                prm3 = prm[:, :].rearrange("p (j e) -> p j e", e=ET)
                with self.nc.Fori(0, ET // U) as i:
                    self.hyena_tiles(i, U, h_hi, h_lo, hdn, prm3, dft, idft, uT)
            self.out_first(1, uT)


def build(nc, a, out, parts=("first", "second")):
    with ExitStack() as ctx:
        prog = Program(nc, ctx, a, out)
        prog.load_start()
        if "rwkv" in parts or "first" in parts:
            prog.rwkv_layer()
        if "hyena" in parts or "first" in parts:
            prog.hyena_layer()
        if "second" in parts or "ffn" in parts or "mixer" in parts:
            with nc.Fori(0, 2 if "second" in parts else 1) as l:
                if "mixer" not in parts:
                    prog.ffn(l, "ffn1_norm_2", "ffn1_w_gate_2", "ffn1_w_up_2", "ffn1_w_down_2")
                if "ffn" not in parts:
                    prog.mixer(l)
                if "second" in parts:
                    prog.ffn(l, "ffn2_norm_2", "ffn2_w_gate_2", "ffn2_w_up_2", "ffn2_w_down_2")
        prog.finish("second" in parts)


def constants():
    f = np.float32
    pos = np.arange(S, dtype=f)
    half = P // 2
    inv = (f(10000.0) ** (-np.arange(half, dtype=f) / f(half))).astype(f)
    ang = pos[:, None] * inv[None, :]
    cos = np.concatenate([np.cos(ang)] * 2, 1)
    sin = np.concatenate([-np.sin(ang), np.sin(ang)], 1)
    rope = np.stack([np.stack([cos, sin]), np.stack([cos, sin]) * P ** -0.5])
    log_g = np.log1p(-np.exp2(-5.0 - np.arange(CHEADS, dtype=np.float64)))
    idx = np.arange(P)
    diff = idx[None, :] - idx[:, None]
    decay = np.where(diff[:, None, :] >= 0, np.exp(log_g[None, :, None] * np.maximum(diff, 0)[:, None, :]), 0.0)
    t = np.arange(P)
    j, h = t % CH, t // CH
    same = h[:, None] == h[None, :]
    before = np.stack([j[:, None] < j[None, :], j[:, None] > j[None, :]])
    upto = np.stack([j[:, None] <= j[None, :], j[:, None] >= j[None, :]])
    strict = np.stack([upto & same, before & same, upto & same], 2)
    level = np.stack([np.stack([b & same & (j[:, None] // m // 2 == j[None, :] // m // 2) & (j[:, None] // m != j[None, :] // m)
                                for m in (1, 2, 4, 8, 16, 32)]) for b in before])
    no_start = np.broadcast_to(np.arange(S) % CH != 0, (P, S))
    tt = np.linspace(0.0, 1.0, S)
    bands = (EMB - 1) // 2
    turn = (2.0 * np.pi / S) * np.arange(S)[:, None] * np.linspace(1e-4, bands - 1, bands)[None, :]
    pos_features = np.concatenate([tt[:, None], np.cos(turn), -np.sin(turn)], 1)
    deltas = np.abs(np.linspace(np.log(1e-2) / 1.5, np.log(1e-2) / 0.3, E))
    omega = np.pi / S * np.arange(S)[:, None] * (np.arange(S) + 0.5)[None, :]
    dft = np.concatenate([np.cos(omega), np.sin(omega)], 1)
    idft = np.concatenate([np.cos(omega), -np.sin(omega)], 1).T / S
    return {
        "k_pos": np.ascontiguousarray(pos_features.T).astype(f),
        "k_window": np.exp(-tt[:, None] * deltas[None, :]).astype(f),
        "k_dft": np.ascontiguousarray(dft.reshape(NT, P, 2 * S).transpose(1, 0, 2)).astype(f),
        "k_idft": np.ascontiguousarray(idft.reshape(4, P, S).transpose(1, 0, 2)).astype(f),
        "k_strict": strict.transpose(1, 0, 2, 3).astype(f),
        "k_level": level.transpose(2, 0, 1, 3).astype(f),
        "k_no_start": no_start.astype(f),
        "k_same_head": same.astype(f),
        "k_head_mean": (same / CH).astype(f),
        "k_ident": np.eye(P, dtype=f),
        "k_rope": np.ascontiguousarray(rope.reshape(2, 2, NT, P, P).transpose(3, 0, 1, 2, 4)).astype(f),
        "k_decay": decay.astype(f),
        "k_xi": np.broadcast_to(np.exp(log_g[:, None] * (idx + 1.0)), (P, CHEADS, P)).astype(f),
        "k_zeta": np.exp(log_g[None, :] * (P - 1 - idx)[:, None]).astype(f),
        "k_causal": (diff >= 0).astype(f),
    }


_INS = ["x", "c", "ctx", "c_ctx", "ada_w", "ada_b", "norm_pre", "norm_post", "w_out",
        "l0_w_in", "l0_mu", "l0_w0", "l0_w2", "l0_a0", "l0_a2", "l0_k_k", "l0_k_a", "l0_r_k", "l0_ln_w", "l0_ln_b",
        "l1_w_in", "l1_conv_w", "l1_conv_b", "l1_f_w1", "l1_f_b1", "l1_f_w2", "l1_f_b2", "l1_f_w3", "l1_f_b3", "l1_f_w4",
        "l1_sin_freq", "l1_filter_bias", "ffn1_norm_2", "ffn1_w_gate_2", "ffn1_w_up_2", "ffn1_w_down_2", "mix_norm_2",
        "w_in_2", "gmlp_v_norm_2", "gmlp_w_s_2", "gmlp_b_s_2", "conv_w_2", "ret_gn_2", "w_out_2", "ffn2_norm_2",
        "ffn2_w_gate_2", "ffn2_w_up_2", "ffn2_w_down_2", "final_norm_2"]


def kernel(**inputs):
    import concourse.bacc as bacc
    from concourse.bass_utils import run_bass_kernel_spmd

    nc = bacc.Bacc("TRN2", target_bir_lowering=False, num_devices=1)
    arrays, a = {}, {}
    given = {n: np.ascontiguousarray(inputs[n]) for n in _INS}
    for name, v in {**given, **constants()}.items():
        arrays[f"in_{name}"] = v
        a[name] = nc.dram_tensor(f"in_{name}", v.shape, mybir.dt.from_np(v.dtype), kind="ExternalInput").ap()
    out = nc.dram_tensor("out_0", (1, S, D), F32, kind="ExternalOutput").ap()
    build(nc, a, out)
    r = run_bass_kernel_spmd(nc, [arrays], core_ids=[0])
    return r.results[0]["out_0"]
```

```python
from contextlib import ExitStack

import numpy as np

import concourse.bass as bass
from concourse import mybir

ALU = mybir.AluOpType
ACT = mybir.ActivationFunctionType
F32 = mybir.dt.float32
F32R = mybir.dt.float32r

P = 128
D = 1024
KT = D // P
S = 256
NT = S // P
E = 2 * D
ET = E // P
HEAD = 64
LORA = 64
FF = 2816
FT = FF // P
WIDE = 512
EPS = 1e-6
GN_EPS = 64e-5
CH = 64
AW = 256
CW = 512
CHEADS = 4
PROJ = 2 * AW + 3 * AW + 4 * CW
EMB, HW = 33, 64
SLOTS = 4
SMALL = 16 * 14


class Phase:

    def __init__(self, nc, pool):
        self.nc, self.pool, self.used = nc, pool, {}
        self.stack = ExitStack()

    def __enter__(self):
        self.block = self.stack.enter_context(self.nc.Block())
        return self

    def __getitem__(self, name):
        if name not in self.used:
            self.used[name] = self.pool[len(self.used)]
        return self.used[name]

    def __exit__(self, *exc):
        self.stack.__exit__(*exc)
        if exc[0] is None:
            if self.used:
                self.nc.sync.sem_clear(range(self.pool[0].num, self.pool[len(self.used) - 1].num + 1))
            self.nc.all_engine_barrier()
        return False


class Ring:

    def __init__(self, ph, buf):
        self.ph, self.buf, self.pieces = ph, buf, []
        self.counts = [0] * SLOTS

    def load_first(self, sp, parts):
        slot = self.buf[:, 0, :].rearrange("p (k n) -> p k n", n=WIDE)
        for q in range(4):
            ks = slice(q * KT // 4, (q + 1) * KT // 4)
            self.first = 0
            for dst, src in parts(slot):
                sp.dma_start(dst[:, ks], src[:, ks]).then_inc(self.ph[f"quarter_landed_{q}"], 16)
                self.first += 16
        self.pieces.append(None)

    def wait_first(self, eng, q):
        eng.wait_ge(self.ph[f"quarter_landed_{q}"], self.first)
        return self.buf[:, 0, :]

    def load(self, sp, parts, free):
        i = len(self.pieces)
        slot = i % SLOTS
        if i >= SLOTS:
            sp.wait_ge(*free)
        for dst, src in parts(self.buf[:, slot, :]):
            sp.dma_start(dst, src).then_inc(self.ph[f"panel_landed_{slot}"], 16)
            self.counts[slot] += 16
        self.pieces.append(self.counts[slot])

    def wait(self, pe, i):
        pe.wait_ge(self.ph[f"panel_landed_{i % SLOTS}"], self.pieces[i])
        return self.buf[:, i % SLOTS, :]


def chan(v):
    return v.rearrange("(k p) -> p k", p=P)


class Program:
    def __init__(self, nc, ctx, a, out):
        self.nc, self.a, self.out, self.n = nc, a, out, 0

        def sb(name, *shape):
            return ctx.enter_context(nc.sbuf_tensor(name, [P, *shape], F32))

        self.sems = [ctx.enter_context(nc.semaphore(f"s{i}")) for i in range(90)]
        self.psum = ctx.enter_context(nc.psum_tensor("psum", [P, 8, WIDE], F32))
        self.ring = sb("ring", SLOTS, KT * WIDE)
        self.x = sb("x", NT, D)
        self.xn = sb("xn", NT, D)
        self.hT = sb("hT", KT, 2 * S)
        self.ident = sb("ident", P)
        self.half = sb("half", 16)
        self.ss = sb("ss", 8)
        self.ms = sb("ms", 8)
        self.rstd = sb("rstd", 8)
        self.gain = sb("gain", KT)
        self.cond = sb("cond", KT, 2)
        self.shift, self.scale = sb("shift", 2, KT), sb("scale", 2, KT)
        self.post = sb("post", D)
        self.ones = sb("ones", P)

    def phase(self):
        return Phase(self.nc, self.sems)

    def scratch(self, ctx):
        def sb(*shape):
            self.n += 1
            return ctx.enter_context(self.nc.sbuf_tensor(f"scratch{self.n}", [P, *shape], F32))
        return sb

    def split_pair(self, ctx, *shape):
        self.n += 1
        return [ctx.enter_context(self.nc.sbuf_tensor(f"part{self.n}{c}", [P, *shape], F32R)) for c in "hl"]

    def load_start(self):
        nc = self.nc
        with self.phase() as ph:
            @ph.block.sync
            def _(sp):
                sp.dma_start(self.x[:, :, :], self.a["x"][0].rearrange("(t p) d -> p t d", p=P)).then_inc(ph["start"], 16)
                sp.dma_start(self.ident[:, :], self.a["k_ident"]).then_inc(ph["start"], 16)
                sp.wait_ge(ph["start"], 32)

            @ph.block.vector
            def _(dve):
                dve.memset(self.half[:, :], -0.5).then_inc(ph["constants_set"], 1)
                dve.memset(self.ones[:, :], 1.0).then_inc(ph["constants_set"], 1)
                dve.wait_ge(ph["constants_set"], 2)

            @ph.block.scalar
            def _(act):
                with nc.allow_non_contiguous_dma(reason="the two condition vectors, once"):
                    act.dma_start(self.cond[:, :, 0], chan(self.a["c"][0])).then_inc(ph["cond_in"], 16)
                    act.dma_start(self.cond[:, :, 1], chan(self.a["c_ctx"])).then_inc(ph["cond_in"], 16)
                act.wait_ge(ph["cond_in"], 32)
                act.activation(self.cond[:, :, :], self.cond[:, :, :], ACT.Silu).then_inc(ph["cond_ready"], 1)

    def norm_dve_stats(self, ph, dve, x, n=NT):
        for t in range(n):
            dve.tensor_tensor_reduce(out=self.xn[:, t, :], in0=x[:, t, :], in1=x[:, t, :], scale=1.0, scalar=0.0,
                                     op0=ALU.mult, op1=ALU.add, accum_out=self.ss[:, t:t + 1]).then_inc(ph["squares"], 1)
        dve.wait_ge(ph["squares"], n)
        dve.tensor_scalar(self.ms[:, 0:n], self.ss[:, 0:n], 1.0 / D, EPS, ALU.mult, ALU.add).then_inc(ph["mean_square"], 1)

    def norm_pool(self, ph, pool, n=NT):
        pool.wait_ge(ph["mean_square"], 1)
        pool.tensor_tensor(self.rstd[:, 0:n], self.ms[:, 0:n], self.half[:, 0:n], ALU.pow).then_inc(ph["rstd_ready"], 1)

    def norm_dve_scale(self, ph, dve, x, n=NT):
        dve.wait_ge(ph["rstd_ready"], 1)
        for t in range(n):
            dve.tensor_scalar(self.xn[:, t, :], x[:, t, :], self.rstd[:, t:t + 1], None, ALU.mult).then_inc(ph["xn_ready"], 1)

    def norm_pe(self, ph, pe, bank=4):
        pe.wait_ge(ph["xn_ready"], NT)
        for k in range(KT):
            for t in range(NT):
                mm = pe.transpose(self.psum[:, bank + k // 2, (k % 2) * S + t * P:(k % 2) * S + (t + 1) * P],
                                  self.xn[:, t, k * P:(k + 1) * P], self.ident[:, :])
            mm.then_inc(ph["turned"], 1)

    def mixer(self, l):
        a, psum, hT, ident = self.a, self.psum, self.hT, self.ident
        kp = "a (k p) n -> p (a k) n"
        order = [1280, 1792, 2304, 2816, 0, 512, 1024]
        width = [WIDE] * 6 + [AW]
        with ExitStack() as ctx:
            sb = self.scratch(ctx)
            rope = sb(2, 2, NT, P)
            gain_c, gain_a = sb(CW), sb(AW)
            decay, xi, zeta = sb(CHEADS, P), sb(CHEADS, P), sb(CHEADS)
            causal, w_s, wsT, b_s = sb(P), sb(4, P), sb(4, P), sb(2, P)
            conv = sb(2, 3)
            m1, m2 = self.post[:, 0:CW], self.post[:, CW:2 * CW]
            qk = sb(2, NT, CW)
            qkT = hT[:, :, S:2 * S].rearrange("p (i h) s -> p i h s", i=2)
            qx = sb(CHEADS, P)
            kz, kv = sb(CW), sb(CW)
            v, sg = sb(NT, CW), sb(NT, CW)
            pT = self.xn[:, :, 0:CW].rearrange("p t (h s) -> p t h s", h=CHEADS)
            bn, mv = sb(16, 6), sb(16, 2)
            var, rs = sb(16), sb(16)
            ret = self.xn[:, :, CW:2 * CW]
            uT, va = sb(2, S), sb(NT, AW)
            bcx = sb(6, S)
            z, yb = sb(2, S + 2), sb(2, S)
            yT = qk[:, 0, :, :].rearrange("p t (k s) -> p (t k) s", s=S)
            BUFS = 4
            w_hi, w_lo = self.split_pair(ctx, BUFS, D)
            h_hi, h_lo = self.split_pair(ctx, KT, S)
            y_hi, y_lo = h_hi, h_lo
            IN = 24
            banks_out = (0, 1, 6, 7)

            def source(g):
                if g < 16:
                    i, at = g // 4, slice(g % 4 * 2, g % 4 * 2 + 2)
                    return i, lambda slot: slot.rearrange("p (k n) -> p k n", n=WIDE)[:, at, :]
                if g < IN:
                    i, c = [(4, 0), (4, 1), (5, 0), (5, 1), (5, 2), (5, 3), (6, 0), (6, 1)][g - 16]
                    return i, lambda slot: slot.rearrange("p (k n) -> p k n", n=WIDE)[:, :, c * P:(c + 1) * P]
                return 7 + (g - IN) // 4, lambda slot: slot.rearrange("p (k n) -> p k n", n=D)[:, (g - IN) % 4, :]

            def part(w, g):
                v = w[:, g % BUFS, :]
                return v.rearrange("p (k n) -> p k n", n=WIDE) if g < 16 else v.rearrange("p (k n) -> p k n", n=P) if g < IN else v
            with self.phase() as ph:
                ring = Ring(ph, self.ring)

                @ph.block.sync
                def _(sp):
                    def load_small():
                        loads = [(conv[:, c, :], a["conv_w_2"][bass.ds(l, 1), :, c * P:(c + 1) * P].rearrange("a i p -> p (a i)")) for c in range(2)]
                        loads += [
                            (rope[:, :, :, :, :], a["k_rope"]),
                            (decay[:, :, :], a["k_decay"]), (xi[:, :, :], a["k_xi"]), (zeta[:, :], a["k_zeta"]), (causal[:, :], a["k_causal"]),
                            (w_s[:, :, :], a["gmlp_w_s_2"][bass.ds(l, 1)].rearrange("a g t s -> t (a g) s")),
                            (gain_c[:, :], a["ret_gn_2"][bass.ds(l, 1)].partition_broadcast(P).rearrange("p a n -> p (a n)")),
                            (gain_a[:, :], a["gmlp_v_norm_2"][bass.ds(l, 1)].partition_broadcast(P).rearrange("p a n -> p (a n)"))]
                        for g in range(4):
                            loads.append((b_s[HEAD * (g % 2):HEAD * (g % 2) + HEAD, g // 2, :],
                                          a["gmlp_b_s_2"][bass.ds(l, 1), g, :].partition_broadcast(HEAD).rearrange("p a n -> p (a n)")))
                        for dst, src in loads:
                            sp.dma_start(dst, src).then_inc(ph["small_in"], 16)
                        assert SMALL == 16 * len(loads)

                    for i, (c, w) in enumerate(zip(order, width)):
                        if i == 2:
                            with self.nc.allow_non_contiguous_dma(reason="small vectors"):
                                load_small()
                        def parts(slot):
                            yield slot[:, :, 0:w], a["w_in_2"][bass.ds(l, 1)].rearrange(kp, p=P)[:, :, c:c + w]
                        if i == 0:
                            ring.load_first(sp, parts)
                            continue

                        def panel(slot):
                            return parts(slot.rearrange("p (k n) -> p k n", n=WIDE))
                        ring.load(sp, panel, (ph["w_split"], 4 * (i - SLOTS + 1)))
                    for i in range(2):
                        def parts(slot):
                            yield (slot.rearrange("p (k n) -> p k n", n=D),
                                   a["w_out_2"][bass.ds(l, 1)].rearrange(kp, p=P)[:, 4 * i:4 * i + 4, :])
                        ring.load(sp, parts, [(ph["w_split"], 16), (ph["va_made"], 1)][i])

                @ph.block.scalar
                def _(act):
                    with self.nc.allow_non_contiguous_dma(reason="small vectors"):
                        act.dma_start(self.gain[:, :], a["mix_norm_2"][bass.ds(l, 1)].rearrange("a (k p) -> p (a k)", p=P)).then_inc(ph["gain_in"], 16)

                    def round_weights(g):
                        i, view = source(g)
                        w = view(ring.wait_first(act, g) if g < 4 else ring.wait(act, i))
                        if g >= BUFS:
                            act.wait_ge(ph["w_used"], g - BUFS + 1)
                        act.activation(part(w_hi, g), w, ACT.Copy).then_inc(ph["w_rounded"], 1)
                    round_weights(0)
                    act.wait_ge(ph["gain_in"], 16)
                    for k in range(KT):
                        act.wait_ge(ph["turned"], (k // 2 + 1) * 2)
                        act.activation(h_hi[:, k, :], psum[:, 4 + k // 2, k % 2 * S:(k % 2 + 1) * S], ACT.Copy, scale=self.gain[:, k:k + 1]).then_inc(ph["h_rounded"], 1)
                    for g in range(1, 16):
                        round_weights(g)
                    for t in range(NT):
                        act.wait_ge(ph["w_used"], 12)
                        act.activation(v[:, t, :], psum[:, t, :], ACT.Copy).then_inc(ph["v_ready"], 1)
                    for g in range(16, 20):
                        round_weights(g)
                    for t in range(NT):
                        act.wait_ge(ph["w_used"], 16)
                        act.activation(sg[:, t, :], psum[:, 2 + t, :], ACT.Silu).then_inc(ph["gate_ready"], 1)
                    for g in range(20, 22):
                        round_weights(g)
                    act.wait_ge(ph["w_used"], 18)
                    act.activation(uT[:, :, :], psum[:, 0, :].rearrange("p (c s) -> p c s", c=2), ACT.Gelu_apprx_tanh).then_inc(ph["u_ready"], 1)
                    round_weights(22)
                    act.wait_ge(ph["va_made"], 1)
                    act.activation(va[:, :, :], psum[:, 1, :].rearrange("p (t n) -> p t n", t=NT), ACT.Gelu_apprx_tanh).then_inc(ph["va_ready"], 1)
                    for i in range(3):
                        for g in ([23], [24, 25], [26, 27])[i]:
                            round_weights(g)
                        act.wait_ge(ph["w_used"], 20 + 2 * i)
                        act.activation(bcx[:, 2 * i:2 * i + 2, :], psum[:, [2, 3, 0][i], :].rearrange("p (c s) -> p c s", c=2), ACT.Copy).then_inc(ph["bcx_ready"], 1)
                    act.wait_ge(ph["ya_ready"], 1)
                    act.activation(y_hi[:, 0:2, :], yT[:, 0:2, :], ACT.Copy).then_inc(ph["y_rounded"], 1)
                    act.wait_ge(ph["yb_ready"], 1)
                    act.activation(y_hi[:, 2:4, :], yT[:, 2:4, :], ACT.Copy).then_inc(ph["y_rounded"], 1)
                    for g in range(28, 31):
                        round_weights(g)
                    for t in range(NT):
                        act.wait_ge(ph["yc_turned"], t + 1)
                        act.activation(y_hi[:, 4:8, t * P:(t + 1) * P], psum[:, 4 + t, :].rearrange("p (h s) -> p h s", h=CHEADS), ACT.Copy).then_inc(ph["y_rounded"], 1)
                    round_weights(31)

                @ph.block.gpsimd
                def _(pool):
                    self.norm_pool(ph, pool)
                    pool.memset(z[:, :, 0:2], 0.0).then_inc(ph["z_edge"], 1)
                    pool.wait_ge(ph["small_in"], SMALL)
                    for n, (var_in, out_sem, cnt) in enumerate(((ph["var_a"], ph["rs_a"], 8), (ph["var_c"], ph["rs_c"], 8))):
                        pool.wait_ge(var_in, 1)
                        pool.tensor_tensor(rs[:, 8 * n:8 * n + 8], var[:, 8 * n:8 * n + 8], self.half[:, 0:8], ALU.pow).then_inc(out_sem, 1)

                @ph.block.vector
                def _(dve):
                    self.norm_dve_stats(ph, dve, self.x)
                    self.norm_dve_scale(ph, dve, self.x)

                    def rest_of_weights(*granules):
                        for g in granules:
                            i, view = source(g)
                            dve.wait_ge(ph["w_rounded"], g + 1)
                            dve.tensor_tensor(part(w_lo, g), view(self.ring[:, i % SLOTS, :]), part(w_hi, g), ALU.subtract).then_inc(ph["w_split"], 1)
                    rest_of_weights(0)
                    dve.wait_ge(ph["gain_in"], 16)
                    for k in range(KT):
                        dve.wait_ge(ph["h_rounded"], (k // 2 + 1) * 2)
                        dve.scalar_tensor_tensor(out=h_lo[:, k, :], in0=psum[:, 4 + k // 2, k % 2 * S:(k % 2 + 1) * S], scalar=self.gain[:, k:k + 1],
                                                 in1=h_hi[:, k, :], op0=ALU.mult, op1=ALU.subtract).then_inc(ph["h_split"], 1)
                    rest_of_weights(1, 2, 3)
                    for k in range(KT):
                        dve.tensor_scalar(hT[:, k, 0:S], psum[:, 4 + k // 2, k % 2 * S:(k % 2 + 1) * S], self.gain[:, k:k + 1], None, ALU.mult).then_inc(ph["h_whole"], 1)
                    rest_of_weights(4, 5, 6, 7)
                    dve.wait_ge(ph["small_in"], SMALL)
                    dve.wait_ge(ph["ws_turned"], 1)
                    dve.tensor_tensor(wsT[:, :, :], psum[:, 7, :].rearrange("p (g t) -> p g t", g=4),
                                      causal[:, :].unsqueeze(1).to_broadcast([P, 4, P]), ALU.mult).then_inc(ph["ws_ready"], 1)
                    for i in range(2):
                        for t in range(NT):
                            n = 2 * i + t
                            dve.wait_ge(ph["w_used"], 4 * (i + 1))
                            src = psum[:, n, :].rearrange("p (h d) -> p h d", h=CHEADS)
                            m1v, m2v = (m[:, :].rearrange("p (h d) -> p h d", h=CHEADS) for m in (m1, m2))
                            if n:
                                dve.wait_ge(ph["rotated"], n)
                            dve.tensor_tensor(m1v, src, rope[:, i, 0, t, :].unsqueeze(1).to_broadcast([P, CHEADS, P]), ALU.mult).then_inc(ph["rope_parts"], 1)
                            for o in (0, HEAD):
                                dve.tensor_tensor(m2v[:, :, o:o + HEAD], src[:, :, HEAD - o:P - o],
                                                  rope[:, i, 1, t, o:o + HEAD].unsqueeze(1).to_broadcast([P, CHEADS, HEAD]), ALU.mult).then_inc(ph["rope_parts"], 1)
                            dve.wait_ge(ph["rope_parts"], 3 * (n + 1))
                            dve.tensor_tensor(qk[:, i, t, :], m1[:, :], m2[:, :], ALU.add).then_inc(ph["rotated"], 1)
                        rest_of_weights(*range(8 + 4 * i, 12 + 4 * i))
                    dve.wait_ge(ph["rotated"], 4)
                    dve.tensor_tensor(kz[:, :].rearrange("p (h d) -> p h d", h=CHEADS), qk[:, 1, 0, :].rearrange("p (h d) -> p h d", h=CHEADS),
                                      zeta[:, :].unsqueeze(2).to_broadcast([P, CHEADS, P]), ALU.mult).then_inc(ph["kz_ready"], 1)
                    rest_of_weights(16, 17, 18, 19)
                    for i in range(2):
                        for t in range(NT):
                            n = 2 * i + t
                            dve.wait_ge(ph["qk_turned"], n + 1)
                            dve.tensor_copy(qkT[:, i, :, t * P:(t + 1) * P], psum[:, 4 + n, :].rearrange("p (h s) -> p h s", h=CHEADS)).then_inc(ph["qkT_ready"], 1)
                    dve.wait_ge(ph["qkT_ready"], 4)
                    dve.tensor_tensor(qx[:, :, :], qkT[:, 0, :, P:S], xi[:, :, :], ALU.mult).then_inc(ph["qx_ready"], 1)
                    rest_of_weights(20, 21, 22, 23)
                    dve.wait_ge(ph["va_ready"], 1)
                    vg = va[:, :, :].rearrange("p t (g d) -> p (t g) d", g=4)
                    self.group_stats(ph, dve, [vg[:, j, :] for j in range(8)], bn, mv, var, 0, ph["var_a"])
                    dve.wait_ge(ph["rs_a"], 1)
                    for j in range(8):
                        dve.tensor_scalar(vg[:, j, :], vg[:, j, :], mv[:, j, 0:1], rs[:, j:j + 1], ALU.subtract, ALU.mult).then_inc(ph["va_scaled"], 1)
                    dve.wait_ge(ph["va_scaled"], 8)
                    dve.tensor_tensor(va[:, :, :], va[:, :, :], gain_a[:, :].unsqueeze(1).to_broadcast([P, NT, AW]), ALU.mult).then_inc(ph["va_normed"], 1)
                    rest_of_weights(24, 25, 26, 27)
                    for t in range(NT):
                        dve.wait_ge(ph["scores_ready"], t + 1)
                        dve.tensor_tensor(pT[:, t, :, :], psum[:, 4 + t, :].rearrange("p (h s) -> p h s", h=CHEADS), decay[:, :, :], ALU.mult).then_inc(ph["pT_ready"], 1)
                    dve.wait_ge(ph["kv_ready"], 1)
                    dve.tensor_copy(kv[:, :], psum[:, 6, :]).then_inc(ph["kv_copied"], 1)
                    dve.wait_ge(ph["spatial_ready"], 1)
                    sv = psum[:, 7, :].rearrange("p (c s) -> p c s", c=2)
                    for t in range(NT):
                        dve.tensor_tensor(yT[:, 0:2, t * P:(t + 1) * P], sv[:, :, t * P:(t + 1) * P], b_s[:, :, :], ALU.add).then_inc(ph["sv_ready"], 1)
                    dve.wait_ge(ph["sv_ready"], 2)
                    dve.wait_ge(ph["u_ready"], 1)
                    dve.tensor_tensor(yT[:, 0:2, :], yT[:, 0:2, :], uT[:, :, :], ALU.mult).then_inc(ph["ya_ready"], 1)
                    dve.wait_ge(ph["bcx_ready"], 3)
                    dve.wait_ge(ph["z_edge"], 1)
                    dve.tensor_tensor(z[:, :, 2:S + 2], bcx[:, 2:4, :], bcx[:, 4:6, :], ALU.mult).then_inc(ph["z_ready"], 1)
                    dve.wait_ge(ph["z_ready"], 1)
                    for c in range(2):
                        dve.tensor_scalar(yb[:, c, :], z[:, c, 0:S], conv[:, c, 0:1], None, ALU.mult).then_inc(ph["taps"], 1)
                    for i in range(1, 3):
                        for c in range(2):
                            dve.wait_ge(ph["taps"], 2 * i + c - 1)
                            dve.scalar_tensor_tensor(out=yb[:, c, :], in0=z[:, c, i:i + S], scalar=conv[:, c, i:i + 1], in1=yb[:, c, :],
                                                     op0=ALU.mult, op1=ALU.add).then_inc(ph["taps"], 1)
                    dve.wait_ge(ph["taps"], 6)
                    dve.tensor_tensor(yT[:, 2:4, :], yb[:, :, :], bcx[:, 0:2, :], ALU.mult).then_inc(ph["yb_ready"], 1)
                    for i in range(2):
                        dve.wait_ge(ph["y_rounded"], i + 1)
                        dve.tensor_tensor(y_lo[:, 2 * i:2 * i + 2, :], yT[:, 2 * i:2 * i + 2, :], y_hi[:, 2 * i:2 * i + 2, :], ALU.subtract).then_inc(ph["y_split"], 1)
                    for t in range(NT):
                        dve.wait_ge(ph["ret_ready"], t + 1)
                    rg = [psum[:, 2 + t, h * P:(h + 1) * P] for t in range(NT) for h in range(CHEADS)]
                    self.group_stats(ph, dve, rg, bn, mv, var, 8, ph["var_c"])
                    dve.wait_ge(ph["rs_c"], 1)
                    for j in range(8):
                        dve.tensor_scalar(ret[:, j // 4, (j % 4) * P:(j % 4 + 1) * P], rg[j], mv[:, 8 + j, 0:1], rs[:, 8 + j:9 + j],
                                          ALU.subtract, ALU.mult).then_inc(ph["ret_scaled"], 1)
                    dve.wait_ge(ph["gate_ready"], 2)
                    for t in range(NT):
                        dve.wait_ge(ph["ret_scaled"], 4 * t + 4)
                        dve.tensor_tensor(ret[:, t, :], ret[:, t, :], gain_c[:, :], ALU.mult).then_inc(ph["ret_gained"], 1)
                        dve.wait_ge(ph["ret_gained"], t + 1)
                        dve.tensor_tensor(ret[:, t, :], ret[:, t, :], sg[:, t, :], ALU.mult).then_inc(ph["ret_gated"], 1)
                    rest_of_weights(28, 29, 30)
                    for t in range(NT):
                        dve.wait_ge(ph["y_rounded"], 3 + t)
                        dve.tensor_tensor(y_lo[:, 4:8, t * P:(t + 1) * P], psum[:, 4 + t, :].rearrange("p (h s) -> p h s", h=CHEADS),
                                          y_hi[:, 4:8, t * P:(t + 1) * P], ALU.subtract).then_inc(ph["y_split"], 1)
                    rest_of_weights(31)
                    for t in range(NT):
                        for n in range(2):
                            dve.wait_ge(ph["out_ready"], 2 * t + n + 1)
                            xs = self.x[:, t, n * WIDE:(n + 1) * WIDE]
                            dve.tensor_tensor(xs, psum[:, banks_out[2 * t + n], :], xs, ALU.add).then_inc(ph["x_ready"], 1)

                @ph.block.tensor
                def _(pe):
                    self.norm_pe(ph, pe)

                    def passes(dst, left, right, first, last):
                        for n, (a, b) in enumerate(((0, 0), (0, 1), (1, 0))):
                            mm = pe.matmul(dst, left[a], right[b], start=first and n == 0, stop=last and n == 2)
                        return mm

                    def by_token(i, bank):
                        for g in range(4 * i, 4 * i + 4):
                            pe.wait_ge(ph["w_split"], g + 1)
                            for kk in range(2):
                                k = g % 4 * 2 + kk
                                if i == 0:
                                    pe.wait_ge(ph["h_split"], k + 1)
                                for t in range(NT):
                                    mm = passes(psum[:, bank + t, :], [h[:, k, t * P:(t + 1) * P] for h in (h_hi, h_lo)],
                                                [part(w, g)[:, kk, :] for w in (w_hi, w_lo)], k == 0, k == KT - 1)
                            mm.then_inc(ph["w_used"], 1)

                    def by_channel(g, bank):
                        for c in range(2):
                            pe.wait_ge(ph["w_split"], g + c + 1)
                            for k in range(KT):
                                mm = passes(psum[:, bank, c * S:(c + 1) * S], [part(w, g + c)[:, k, :] for w in (w_hi, w_lo)],
                                            [h[:, k, :] for h in (h_hi, h_lo)], k == 0, k == KT - 1)
                            mm.then_inc(ph["w_used"], 1)

                    by_token(0, 0)
                    pe.wait_ge(ph["small_in"], SMALL)
                    pe.wait_ge(ph["h_whole"], KT)
                    for g in range(4):
                        mm = pe.transpose(psum[:, 7, g * P:(g + 1) * P], w_s[:, g, :], ident[:, :])
                    mm.then_inc(ph["ws_turned"], 1)
                    by_token(1, 2)
                    pe.wait_ge(ph["rotated"], 2)
                    by_token(2, 0)
                    pe.wait_ge(ph["rotated"], 4)
                    by_token(3, 2)
                    pe.wait_ge(ph["ws_ready"], 1)
                    for i in range(2):
                        for t in range(NT):
                            for h in range(CHEADS):
                                mm = pe.transpose(psum[:, 4 + 2 * i + t, h * P:(h + 1) * P], qk[:, i, t, h * P:(h + 1) * P], ident[:, :])
                            mm.then_inc(ph["qk_turned"], 1)
                    pe.wait_ge(ph["v_ready"], 2)
                    by_channel(16, 0)
                    w = ring.wait(pe, 4).rearrange("p (k n) -> p k n", n=WIDE)
                    for t in range(NT):
                        for k in range(KT):
                            mm = pe.matmul(psum[:, 1, t * AW:(t + 1) * AW], hT[:, k, t * P:(t + 1) * P], w[:, k, AW:2 * AW], start=(k == 0), stop=(k == KT - 1))
                    mm.then_inc(ph["va_made"], 1)
                    pe.wait_ge(ph["gate_ready"], 2)
                    by_channel(18, 2)
                    by_channel(20, 3)
                    pe.wait_ge(ph["u_ready"], 1)
                    by_channel(22, 0)
                    pe.wait_ge(ph["qkT_ready"], 4)
                    for t in range(NT):
                        for h in range(CHEADS):
                            mm = pe.matmul(psum[:, 4 + t, h * P:(h + 1) * P], qkT[:, 1, h, t * P:(t + 1) * P], qkT[:, 0, h, t * P:(t + 1) * P],
                                           start=True, stop=True)
                        mm.then_inc(ph["scores_ready"], 1)
                    pe.wait_ge(ph["kz_ready"], 1)
                    for h in range(CHEADS):
                        mm = pe.matmul(psum[:, 6, h * P:(h + 1) * P], kz[:, h * P:(h + 1) * P], v[:, 0, h * P:(h + 1) * P], start=True, stop=True)
                    mm.then_inc(ph["kv_ready"], 1)
                    pe.wait_ge(ph["va_normed"], 1)
                    for t in range(NT):
                        for g in range(4):
                            o = HEAD * (g % 2)
                            mm = pe.matmul(psum[o:o + HEAD, 7, (g // 2) * S + t * P:(g // 2) * S + (t + 1) * P],
                                           va[:, t, g * HEAD:(g + 1) * HEAD], wsT[:, g, :], start=True, stop=True)
                    mm.then_inc(ph["spatial_ready"], 1)
                    pe.wait_ge(ph["bcx_ready"], 2)
                    pe.wait_ge(ph["pT_ready"], 2)
                    pe.wait_ge(ph["kv_copied"], 1)
                    pe.wait_ge(ph["qx_ready"], 1)
                    for t in range(NT):
                        for h in range(CHEADS):
                            hs = slice(h * P, (h + 1) * P)
                            mm = pe.matmul(psum[:, 2 + t, hs], pT[:, t, h, :], v[:, t, hs], start=True, stop=(t == 0))
                            if t:
                                mm = pe.matmul(psum[:, 2 + t, hs], qx[:, h, :], kv[:, hs], start=False, stop=True)
                        mm.then_inc(ph["ret_ready"], 1)
                    def out_rows(k):
                        g = IN + k
                        pe.wait_ge(ph["w_split"], g + 1)
                        for t in range(NT):
                            for n in range(2):
                                mm = passes(psum[:, banks_out[2 * t + n], :], [y[:, k, t * P:(t + 1) * P] for y in (y_hi, y_lo)],
                                            [part(w, g)[:, n * WIDE:(n + 1) * WIDE] for w in (w_hi, w_lo)], k == 0, k == KT - 1)
                                if k == KT - 1:
                                    mm.then_inc(ph["out_ready"], 1)
                        if k < KT - 1:
                            mm.then_inc(ph["w_used"], 1)
                    pe.wait_ge(ph["bcx_ready"], 3)
                    pe.wait_ge(ph["va_ready"], 1)
                    pe.wait_ge(ph["sv_ready"], 2)
                    for k in range(3):
                        pe.wait_ge(ph["y_split"], k // 2 + 1)
                        out_rows(k)
                    for t in range(NT):
                        pe.wait_ge(ph["ret_gated"], t + 1)
                        for h in range(CHEADS):
                            mm = pe.transpose(psum[:, 4 + t, h * P:(h + 1) * P], ret[:, t, h * P:(h + 1) * P], ident[:, :])
                        mm.then_inc(ph["yc_turned"], 1)
                    out_rows(3)
                    pe.wait_ge(ph["y_split"], 4)
                    for k in range(4, KT):
                        out_rows(k)

    def group_stats(self, ph, dve, groups, bn, mv, var, at, done):
        n = len(groups)
        for j, g in enumerate(groups):
            dve.bn_stats(bn[:, at + j, :], g).then_inc(ph[f"stats_{at}"], 1)
        for j in range(n):
            dve.wait_ge(ph[f"stats_{at}"], j + 1)
            dve.bn_aggr(mv[:, at + j, :], bn[:, at + j, :]).then_inc(ph[f"aggregated_{at}"], 1)
        dve.wait_ge(ph[f"aggregated_{at}"], n)
        dve.tensor_scalar(var[:, at:at + n], mv[:, at:at + n, 1], EPS, None, ALU.add).then_inc(done, 1)

    def finish(self):
        x, a = self.x, self.a
        with ExitStack() as ctx:
            gain = ctx.enter_context(self.nc.sbuf_tensor([P, D], F32))
            with self.phase() as ph:
                @ph.block.sync
                def _(sp):
                    sp.dma_start(gain[:, :], a["final_norm_2"].partition_broadcast(P)).then_inc(ph["gain_in"], 16)
                    for t in range(NT):
                        sp.wait_ge(ph["y_ready"], t + 1)
                        sp.dma_start(self.out[0, t * P:(t + 1) * P, :], self.xn[:, t, :]).then_inc(ph["stored"], 16)
                    sp.wait_ge(ph["stored"], 16 * NT)

                @ph.block.gpsimd
                def _(pool):
                    self.norm_pool(ph, pool)

                @ph.block.vector
                def _(dve):
                    self.norm_dve_stats(ph, dve, x)
                    dve.wait_ge(ph["rstd_ready"], 1)
                    dve.wait_ge(ph["gain_in"], 16)
                    for t in range(NT):
                        dve.scalar_tensor_tensor(out=self.xn[:, t, :], in0=x[:, t, :], scalar=self.rstd[:, t:t + 1], in1=gain[:, :],
                                                 op0=ALU.mult, op1=ALU.mult).then_inc(ph["y_ready"], 1)

    def ffn(self, l, norm, wg, wu, wd):
        a, psum = self.a, self.psum
        kp = "a (k p) n -> p (a k) n"
        GRAN, BUFS = D, 4
        panels, per = FF // S, KT * WIDE // GRAN
        granules = panels * per + FT
        with ExitStack() as ctx:
            w_hi, w_lo = self.split_pair(ctx, BUFS, GRAN)
            h_hi, h_lo = self.split_pair(ctx, KT, S)
            hid_hi, hid_lo = self.split_pair(ctx, FT, S)
            sb = self.scratch(ctx)
            sg, hid = sb(2, S), sb(2, S)
            with self.phase() as ph:
                ring = Ring(ph, self.ring)

                @ph.block.sync
                def _(sp):
                    for j in range(panels):
                        def parts(slot):
                            for w, o in ((wg, 0), (wu, S)):
                                yield slot[:, :, o:o + S], a[w][bass.ds(l, 1)].rearrange(kp, p=P)[:, :, j * S:(j + 1) * S]
                        if j == 0:
                            ring.load_first(sp, parts)
                            continue

                        def panel(slot):
                            return parts(slot.rearrange("p (k n) -> p k n", n=WIDE))
                        ring.load(sp, panel, (ph["w_split"], per * (j - SLOTS + 1)))
                    for q, f0 in enumerate(range(0, FT, per)):
                        n = min(per, FT - f0)

                        def parts(slot):
                            yield (slot[:, 0:n * D].rearrange("p (k n) -> p k n", n=D),
                                   a[wd][bass.ds(l, 1)].rearrange(kp, p=P)[:, f0:f0 + n, :])
                        ring.load(sp, parts, (ph["w_split"], per * (panels + q - SLOTS + 1)))

                @ph.block.scalar
                def _(act):
                    with self.nc.allow_non_contiguous_dma(reason="a gain vector"):
                        act.dma_start(self.gain[:, :], a[norm][bass.ds(l, 1)].rearrange("a (k p) -> p (a k)", p=P)).then_inc(ph["gain_in"], 16)

                    def round_weights(g):
                        w = ring.wait_first(act, g) if g < per else ring.wait(act, g // per)
                        if g >= BUFS:
                            act.wait_ge(ph["w_used"], g - BUFS + 1)
                        act.activation(w_hi[:, g % BUFS, :], w[:, g % per * GRAN:(g % per + 1) * GRAN], ACT.Copy).then_inc(ph["w_rounded"], 1)
                    round_weights(0)
                    act.wait_ge(ph["gain_in"], 16)
                    for k in range(KT):
                        act.wait_ge(ph["turned"], (k // 2 + 1) * 2)
                        act.activation(h_hi[:, k, :], psum[:, 4 + k // 2, k % 2 * S:(k % 2 + 1) * S], ACT.Copy, scale=self.gain[:, k:k + 1]).then_inc(ph["h_rounded"], 1)
                    for g in range(1, granules):
                        j = g // per - 1
                        if g % per == per - 1 and 0 <= j < panels:
                            act.wait_ge(ph["w_used"], per * (j + 1))
                            if j:
                                act.wait_ge(ph["hid_made"], 2 * j)
                            for i in range(2):
                                act.activation(sg[:, i, :], psum[:, j % 2 * 4 + 2 * i, 0:S], ACT.Silu).then_inc(ph["silu_ready"], 1)
                        round_weights(g)

                @ph.block.gpsimd
                def _(pool):
                    self.norm_pool(ph, pool)

                @ph.block.vector
                def _(dve):
                    def rest_of_weights(g):
                        dve.wait_ge(ph["w_rounded"], g + 1)
                        w = self.ring[:, g // per % SLOTS, g % per * GRAN:(g % per + 1) * GRAN]
                        dve.tensor_tensor(w_lo[:, g % BUFS, :], w, w_hi[:, g % BUFS, :], ALU.subtract).then_inc(ph["w_split"], 1)
                    self.norm_dve_stats(ph, dve, self.x)
                    self.norm_dve_scale(ph, dve, self.x)
                    rest_of_weights(0)
                    dve.wait_ge(ph["gain_in"], 16)
                    for k in range(KT):
                        dve.wait_ge(ph["h_rounded"], (k // 2 + 1) * 2)
                        dve.scalar_tensor_tensor(out=h_lo[:, k, :], in0=psum[:, 4 + k // 2, k % 2 * S:(k % 2 + 1) * S], scalar=self.gain[:, k:k + 1],
                                                 in1=h_hi[:, k, :], op0=ALU.mult, op1=ALU.subtract).then_inc(ph["h_split"], 1)
                    for g in range(1, granules):
                        j = g // per - 1
                        if g % per == per - 1 and 0 <= j < panels:
                            for i in range(2):
                                f = 2 * j + i
                                dve.wait_ge(ph["silu_ready"], f + 1)
                                if j:
                                    dve.wait_ge(ph["hid_split"], f - 1)
                                dve.tensor_tensor(hid[:, i, :], sg[:, i, :], psum[:, j % 2 * 4 + 2 * i + 1, 0:S], ALU.mult).then_inc(ph["hid_made"], 1)
                            for i in range(2):
                                f = 2 * j + i
                                dve.wait_ge(ph["hid_made"], f + 1)
                                dve.tensor_copy(hid_hi[:, f, :], hid[:, i, :]).then_inc(ph["hid_rounded"], 1)
                            for i in range(2):
                                f = 2 * j + i
                                dve.wait_ge(ph["hid_rounded"], f + 1)
                                dve.tensor_tensor(hid_lo[:, f, :], hid[:, i, :], hid_hi[:, f, :], ALU.subtract).then_inc(ph["hid_split"], 1)
                        rest_of_weights(g)
                    for t in range(NT):
                        for n in range(2):
                            dve.wait_ge(ph["down_ready"], 2 * t + n + 1)
                            dve.scalar_tensor_tensor(out=self.x[:, t, n * WIDE:(n + 1) * WIDE], in0=psum[:, 4 + 2 * t + n, :],
                                                     scalar=0.5, in1=self.x[:, t, n * WIDE:(n + 1) * WIDE],
                                                     op0=ALU.mult, op1=ALU.add).then_inc(ph["x_ready"], 1)

                @ph.block.tensor
                def _(pe):
                    self.norm_pe(ph, pe)
                    for j in range(panels):
                        for q in range(per):
                            g = j * per + q
                            hi, lo = (w[:, g % BUFS, :].rearrange("p (k n) -> p k n", n=WIDE) for w in (w_hi, w_lo))
                            pe.wait_ge(ph["w_split"], g + 1)
                            if q == 0 and j >= 2:
                                pe.wait_ge(ph["hid_made"], 2 * (j - 1))
                            for kk in range(2):
                                k = 2 * q + kk
                                if j == 0:
                                    pe.wait_ge(ph["h_split"], k + 1)
                                for i in range(2):
                                    for o in (0, S):
                                        at = slice(o + i * P, o + (i + 1) * P)
                                        for n, (w, h) in enumerate(((hi, h_hi), (hi, h_lo), (lo, h_hi))):
                                            mm = pe.matmul(psum[:, j % 2 * 4 + 2 * i + o // S, 0:S], w[:, kk, at], h[:, k, :],
                                                           start=(k == 0 and n == 0), stop=(k == KT - 1 and n == 2))
                            mm.then_inc(ph["w_used"], 1)
                    for f in range(FT):
                        g = panels * per + f
                        pe.wait_ge(ph["w_split"], g + 1)
                        pe.wait_ge(ph["hid_split"], f + 1)
                        if f == 0:
                            pe.wait_ge(ph["hid_made"], FT - 2)
                        for t in range(NT):
                            for n in range(2):
                                ws = slice(n * WIDE, (n + 1) * WIDE)
                                for m, (h, w) in enumerate(((hid_hi, w_hi), (hid_hi, w_lo), (hid_lo, w_hi))):
                                    mm = pe.matmul(psum[:, 4 + 2 * t + n, :], h[:, f, t * P:(t + 1) * P], w[:, g % BUFS, ws],
                                                   start=(f == 0 and m == 0), stop=(f == FT - 1 and m == 2))
                                if f == FT - 1:
                                    mm.then_inc(ph["down_ready"], 1)
                        if f < FT - 1:
                            mm.then_inc(ph["w_used"], 1)

    def turn_rows(self, sb, jobs):
        work = []
        loads = []
        for rows, cols in jobs:
            total = sum(r.shape[0] for r in rows)
            tiles = [sb(P) for _ in range((total + P - 1) // P)]
            work += [(t, min(P, total - i * P), cols[:, i * P:min((i + 1) * P, total)]) for i, t in enumerate(tiles)]
            at = 0
            for r in rows:
                done = 0
                while done < r.shape[0]:
                    k = min(r.shape[0] - done, P - at % P)
                    loads.append((tiles[at // P][at % P:at % P + k, :], r[done:done + k, :]))
                    done, at = done + k, at + k

        class Side:
            @staticmethod
            def load(ph, eng):
                for dst, src in loads:
                    eng.dma_start(dst, src).then_inc(ph["rows_in"], 16)

            @staticmethod
            def tensor(ph, pe):
                pe.wait_ge(ph["rows_in"], 16 * len(loads))
                for i, (tile, n, cols) in enumerate(work):
                    pe.transpose(self.psum[:, 7, i * P:i * P + n], tile[0:n, :], self.ident[0:n, 0:n]).then_inc(ph["rows_turned"], 1)
                yield

            @staticmethod
            def vector(ph, dve):
                dve.wait_ge(ph["rows_turned"], len(work))
                for i, (tile, n, cols) in enumerate(work):
                    dve.tensor_copy(cols, self.psum[:, 7, i * P:i * P + n]).then_inc(ph["cols_ready"], 1)
                yield

            @staticmethod
            def scalar(ph, act):
                pass
            tiles = len(work)
        return Side

    def adaln(self, l, conds, sides=()):
        a, psum = self.a, self.psum
        with ExitStack() as ctx:
            sb = self.scratch(ctx)
            bias, ada = sb(3 * D), sb(3 * D)
            panels = 3 * D // WIDE
            with self.phase() as ph:
                ring = Ring(ph, self.ring)

                @ph.block.sync
                def _(sp):
                    for j in range(panels):
                        def parts(slot):
                            yield slot, a["ada_w"][l].rearrange("(k p) n -> p k n", p=P)[:, :, j * WIDE:(j + 1) * WIDE]
                        if j == 0:
                            ring.load_first(sp, parts)
                            continue

                        def panel(slot):
                            return parts(slot.rearrange("p (k n) -> p k n", n=WIDE))
                        ring.load(sp, panel, (ph["ada_ready"], j - SLOTS + 1))

                @ph.block.scalar
                def _(act):
                    for side in sides:
                        side.load(ph, act)
                    act.dma_start(bias[0:2, :], a["ada_b"][l].partition_broadcast(2)).then_inc(ph["bias_in"], 16)
                    act.dma_start(self.post[:, :], a["norm_post"][l].partition_broadcast(P)).then_inc(ph["post_in"], 16)
                    with self.nc.allow_non_contiguous_dma(reason="a gain vector"):
                        act.dma_start(self.gain[:, :], chan(a["norm_pre"][l])).then_inc(ph["gain_in"], 16)
                    for side in sides:
                        side.scalar(ph, act)

                @ph.block.tensor
                def _(pe):
                    beside = [side.tensor(ph, pe) for side in sides]
                    for j in range(panels):
                        if j >= panels // 2:
                            for work in beside:
                                next(work, None)
                        w = (ring.wait(pe, j) if j else ring.buf[:, 0, :]).rearrange("p (k n) -> p k n", n=WIDE)
                        for k in range(KT):
                            if j == 0 and k % 2 == 0:
                                ring.wait_first(pe, k // 2)
                            mm = pe.matmul(psum[0:2, j, :], self.cond[:, k, :], w[:, k, :], start=(k == 0), stop=(k == KT - 1))
                        mm.then_inc(ph["ada_ready"], 1)
                    pe.wait_ge(ph["biased"], panels)
                    for k in range(2 * KT):
                        mm = pe.transpose(psum[:, 6, 2 * k:2 * k + 2], ada[0:2, k * P:(k + 1) * P], self.ident[0:2, 0:2])
                    mm.then_inc(ph["ada_turned"], 1)
                    for n in range(2):
                        mm = pe.matmul(psum[:, n, :], self.ones[0:1, :], ada[0:1, 2 * D + n * WIDE:2 * D + (n + 1) * WIDE], start=True, stop=True)
                    mm.then_inc(ph["gate_spread"], 1)

                @ph.block.vector
                def _(dve):
                    dve.wait_ge(ph["bias_in"], 16)
                    beside = [side.vector(ph, dve) for side in sides]
                    for j in range(panels):
                        if j >= panels // 2:
                            for work in beside:
                                next(work, None)
                        dve.wait_ge(ph["ada_ready"], j + 1)
                        dve.tensor_tensor(ada[0:2, j * WIDE:(j + 1) * WIDE], psum[0:2, j, :], bias[0:2, j * WIDE:(j + 1) * WIDE], ALU.add).then_inc(ph["biased"], 1)
                    dve.wait_ge(ph["ada_turned"], 1)
                    dve.wait_ge(ph["gain_in"], 16)
                    cols = psum[:, 6, 0:4 * KT].rearrange("p (k c) -> p c k", c=2)
                    for c in range(conds):
                        dve.tensor_copy(self.shift[:, c, :], cols[:, c, 0:KT]).then_inc(ph["shift_ready"], 1)
                        dve.scalar_tensor_tensor(out=self.scale[:, c, :], in0=cols[:, c, KT:2 * KT], scalar=1.0, in1=self.gain[:, :],
                                                 op0=ALU.add, op1=ALU.mult).then_inc(ph["scale_ready"], 1)
                    dve.wait_ge(ph["gate_spread"], 1)
                    dve.wait_ge(ph["post_in"], 16)
                    for n in range(2):
                        s = slice(n * WIDE, (n + 1) * WIDE)
                        dve.tensor_tensor(self.post[:, s], self.post[:, s], psum[:, n, :], ALU.mult).then_inc(ph["post_ready"], 1)

    def norm_first(self, jobs, parts=None):
        xns = [self.xn] + [x for x, c, at in jobs[1:]]
        n = len(jobs)
        with self.phase() as ph:
            @ph.block.vector
            def _(dve):
                for j in reversed(range(n)):
                    x = jobs[j][0]
                    for t in range(NT):
                        dve.tensor_tensor_reduce(out=self.xn[:, t, :], in0=x[:, t, :], in1=x[:, t, :], scale=1.0, scalar=0.0, op0=ALU.mult,
                                                 op1=ALU.add, accum_out=self.ss[:, NT * j + t:NT * j + t + 1]).then_inc(ph["squares"], 1)
                    if j:
                        dve.wait_ge(ph["squares"], NT * (n - j))
                dve.wait_ge(ph["squares"], NT * n)
                dve.tensor_scalar(self.ms[:, 0:NT * n], self.ss[:, 0:NT * n], 1.0 / D, EPS, ALU.mult, ALU.add).then_inc(ph["mean_square"], 1)
                dve.wait_ge(ph["rstd_ready"], 1)
                for j in range(n):
                    for t in range(NT):
                        dve.tensor_scalar(xns[j][:, t, :], jobs[j][0][:, t, :], self.rstd[:, NT * j + t:NT * j + t + 1], None, ALU.mult).then_inc(ph["xn_ready"], 1)
                for j, (x, c, at) in enumerate(jobs):
                    for k in range(KT):
                        if k // 2 % 2 == 1:
                            dve.wait_ge(ph["turned"], KT * j + (k // 2 + 1) * 2)
                            src = self.psum[:, 4 - 4 * j + k // 2, k % 2 * S:(k % 2 + 1) * S]
                            dve.tensor_scalar(self.hT[:, k, at:at + S], src, self.scale[:, c, k:k + 1], self.shift[:, c, k:k + 1], ALU.mult, ALU.add).then_inc(ph["h_odd"], 1)
                if parts:
                    for q in range(KT // 2):
                        dve.wait_ge(ph["h_rounded"], q + 1)
                        dve.tensor_tensor(parts[1][:, 2 * q:2 * q + 2, :], self.hT[:, 2 * q:2 * q + 2, 0:S], parts[0][:, 2 * q:2 * q + 2, :],
                                          ALU.subtract).then_inc(ph["h_split"], 1)

            @ph.block.gpsimd
            def _(pool):
                self.norm_pool(ph, pool, NT * n)

            @ph.block.tensor
            def _(pe):
                for j in range(n):
                    pe.wait_ge(ph["xn_ready"], NT * (j + 1))
                    for k in range(KT):
                        for t in range(NT):
                            mm = pe.transpose(self.psum[:, 4 - 4 * j + k // 2, k % 2 * S + t * P:k % 2 * S + (t + 1) * P],
                                              xns[j][:, t, k * P:(k + 1) * P], self.ident[:, :])
                        mm.then_inc(ph["turned"], 1)

            @ph.block.scalar
            def _(act):
                for j, (x, c, at) in enumerate(jobs):
                    for k in range(KT):
                        if k // 2 % 2 == 0:
                            act.wait_ge(ph["turned"], KT * j + (k // 2 + 1) * 2)
                            act.activation(self.hT[:, k, at:at + S], self.psum[:, 4 - 4 * j + k // 2, k % 2 * S:(k % 2 + 1) * S], ACT.Identity,
                                           scale=self.scale[:, c, k:k + 1], bias=self.shift[:, c, k:k + 1]).then_inc(ph["h_even"], 1)
                if parts:
                    for q in range(KT // 2):
                        act.wait_ge(ph["h_odd" if q % 2 else "h_even"], 2 * (q // 2 + 1))
                        act.activation(parts[0][:, 2 * q:2 * q + 2, :], self.hT[:, 2 * q:2 * q + 2, 0:S], ACT.Copy).then_inc(ph["h_rounded"], 1)

    def out_first(self, l, uT, stored=None):
        a, psum = self.a, self.psum
        BUFS = 4
        with ExitStack() as ctx, self.phase() as ph:
            w_hi, w_lo = self.split_pair(ctx, BUFS, D)
            u_hi, u_lo = self.split_pair(ctx, ET, S)
            o = self.scratch(ctx)(NT, D)

            @ph.block.sync
            def _(sp):
                wv = a["w_out"][l].rearrange("(k p) n -> p k n", p=P)
                for q in range(ET // 4):
                    slot = self.ring[:, q, :].rearrange("p (k n) -> p k n", n=D)
                    if stored is not None:
                        sp.dma_start(uT[:, 4 * q:4 * q + 4, :], stored[:, 4 * q:4 * q + 4, :]).then_inc(ph[f"u_in_{q}"], 16)
                    if q == 0:
                        for e in range(4):
                            sp.dma_start(slot[:, e, :], wv[:, e, :]).then_inc(ph[f"row_landed_{e}"], 16)
                    else:
                        sp.dma_start(slot, wv[:, 4 * q:4 * q + 4, :]).then_inc(ph[f"rows_landed_{q}"], 16)
                if stored is not None:
                    sp.dma_start(self.x[:, :, :], a["x"][0].rearrange("(t p) d -> p t d", p=P)).then_inc(ph["x_in"], 16)

            @ph.block.scalar
            def _(act):
                for e in range(ET):
                    if stored is not None and e % 4 == 0:
                        act.wait_ge(ph[f"u_in_{e // 4}"], 16)
                    act.activation(u_hi[:, e, :], uT[:, e, :], ACT.Copy).then_inc(ph["u_rounded"], 1)
                    w = self.ring[:, e // 4, :]
                    if e < 4:
                        act.wait_ge(ph[f"row_landed_{e}"], 16)
                    elif e % 4 == 0:
                        act.wait_ge(ph[f"rows_landed_{e // 4}"], 16)
                    if e >= BUFS:
                        act.wait_ge(ph["w_used"], e - BUFS + 1)
                    act.activation(w_hi[:, e % BUFS, :], w[:, e % 4 * D:(e % 4 + 1) * D], ACT.Copy).then_inc(ph["w_rounded"], 1)

            @ph.block.tensor
            def _(pe):
                for e in range(ET):
                    pe.wait_ge(ph["u_split"], e + 1)
                    pe.wait_ge(ph["w_split"], e + 1)
                    for t in range(NT):
                        for n in range(2):
                            for m, (u, w) in enumerate(((u_hi, w_hi), (u_hi, w_lo), (u_lo, w_hi))):
                                mm = pe.matmul(psum[:, 2 * t + n, :], u[:, e, t * P:(t + 1) * P], w[:, e % BUFS, n * WIDE:(n + 1) * WIDE],
                                               start=(e == 0 and m == 0), stop=(e == ET - 1 and m == 2))
                            if e == ET - 1:
                                mm.then_inc(ph["out_ready"], 1)
                    if e < ET - 1:
                        mm.then_inc(ph["w_used"], 1)

            @ph.block.gpsimd
            def _(pool):
                self.norm_pool(ph, pool)

            @ph.block.vector
            def _(dve):
                for e in range(ET):
                    dve.wait_ge(ph["u_rounded"], e + 1)
                    dve.tensor_tensor(u_lo[:, e, :], uT[:, e, :], u_hi[:, e, :], ALU.subtract).then_inc(ph["u_split"], 1)
                    dve.wait_ge(ph["w_rounded"], e + 1)
                    dve.tensor_tensor(w_lo[:, e % BUFS, :], self.ring[:, e // 4, e % 4 * D:(e % 4 + 1) * D], w_hi[:, e % BUFS, :], ALU.subtract).then_inc(ph["w_split"], 1)
                for t in range(NT):
                    for n in range(2):
                        dve.wait_ge(ph["out_ready"], 2 * t + n + 1)
                        dve.tensor_copy(o[:, t, n * WIDE:(n + 1) * WIDE], psum[:, 2 * t + n, :]).then_inc(ph["out_copied"], 1)
                dve.wait_ge(ph["out_copied"], 4)
                self.norm_dve_stats(ph, dve, o)
                dve.wait_ge(ph["rstd_ready"], 1)
                for t in range(NT):
                    dve.scalar_tensor_tensor(out=o[:, t, :], in0=o[:, t, :], scalar=self.rstd[:, t:t + 1], in1=self.post[:, :],
                                             op0=ALU.mult, op1=ALU.mult).then_inc(ph["out_scaled"], 1)
                if stored is not None:
                    dve.wait_ge(ph["x_in"], 16)
                for t in range(NT):
                    dve.wait_ge(ph["out_scaled"], t + 1)
                    dve.tensor_tensor(self.x[:, t, :], self.x[:, t, :], o[:, t, :], ALU.add).then_inc(ph["x_ready"], 1)

    def rwkv_mixes(self, mix, lora, cols):
        a, psum, hT = self.a, self.psum, self.hT
        groups = [(4, "w", 2 * S), (1, "k", 2 * S), (5, "a", 2 * S), (0, "r", S)]
        shared = [(2, "v", 2 * S), (3, "g", S)]
        with ExitStack() as ctx:
            sb = self.scratch(ctx)
            xx = sb(KT, 2 * S)
            loras = {"w": sb(KT, 2 * S)}
            loras["a"] = loras["w"]
            wl = self.ring[:, 0, 0:KT * 256].rearrange("p (k n) -> p k n", n=256)
            with self.phase() as ph:
                @ph.block.sync
                def _(sp):
                    sp.dma_start(wl, a["l0_w_in"].rearrange("(k p) n -> p k n", p=P)[:, :, 4 * E:4 * E + 4 * LORA]).then_inc(ph["lora_in"], 16)
                    for dst, name in ((self.strict[:, :, :, :], "k_strict"), (self.level[:, :, :, :], "k_level"), (self.no_start[:, :], "k_no_start"),
                                      (self.same_head[:, :], "k_same_head"), (self.head_mean[:, :], "k_head_mean")):
                        sp.dma_start(dst, a[name]).then_inc(ph["constants_in"], 16)
                    sp.wait_ge(ph["constants_in"], 80)

                @ph.block.vector
                def _(dve):
                    n = 0

                    def diff(dst, other, own):
                        nonlocal n
                        dve.tensor_tensor(dst, other, own, ALU.subtract).then_inc(ph["shifted"], 1)
                        n += 1

                    def edge(dst, own):
                        nonlocal n
                        dve.tensor_scalar(dst, own, -1.0, None, ALU.mult).then_inc(ph["shifted"], 1)
                        n += 1
                    for q in range(4):
                        for k in (2 * q, 2 * q + 1):
                            h, d = hT[:, k, 0:S], xx[:, k, 0:S]
                            hg, dg = (v.rearrange("p (r c) -> p r c", c=64) for v in (h, d))
                            if q == 0:
                                diff(dg[:, :, 1:], hg[:, :, 0:63], hg[:, :, 1:])
                                edge(dg[:, :, 0:1], hg[:, :, 0:1])
                            elif q == 1:
                                diff(dg[:, :, 0:63], hg[:, :, 1:], hg[:, :, 0:63])
                                edge(dg[:, :, 63:64], hg[:, :, 63:64])
                            elif q == 2:
                                diff(d[:, 64:], h[:, 0:S - 64], h[:, 64:])
                                edge(d[:, 0:64], h[:, 0:64])
                            else:
                                diff(d[:, 0:S - 64], h[:, 64:], h[:, 0:S - 64])
                                edge(d[:, S - 64:], h[:, S - 64:])
                    dve.wait_ge(ph["shifted"], n)
                    dve.wait_ge(ph["context_shifted"], 2 * KT)
                    for g, name, w in groups:
                        dst = loras[name] if name in loras else mix[name]
                        if name == "a":
                            dve.wait_ge(ph["lora_ready"], 1)
                        for k in range(KT):
                            dve.scalar_tensor_tensor(out=dst[:, k, 0:w], in0=xx[:, k, 0:w], scalar=cols[:, g * KT + k:g * KT + k + 1],
                                                     in1=hT[:, k, 0:w], op0=ALU.mult, op1=ALU.add).then_inc(ph["mixed"], 1)
                    dve.wait_ge(ph["lora_ready"], 2)
                    dve.tensor_copy(lora["a"][:, :], psum[:, 1, :]).then_inc(ph["lora_a"], 1)

                @ph.block.tensor
                def _(pe):
                    pe.wait_ge(ph["lora_in"], 16)
                    for i in range(2):
                        pe.wait_ge(ph["mixed"], KT * (2 * i + 1))
                        for k in range(KT):
                            mm = pe.matmul(psum[:, i, :], wl[:, k, i * P:(i + 1) * P], loras["w"][:, k, :], start=(k == 0), stop=(k == KT - 1))
                        mm.then_inc(ph["lora_ready"], 1)

                @ph.block.scalar
                def _(act):
                    act.wait_ge(ph["shifted"], 2 * KT)
                    act.wait_ge(ph["context_shifted"], 2 * KT)
                    for g, name, w in shared:
                        if name == "g":
                            act.wait_ge(ph["lora_ready"], 1)
                            act.activation(lora["w"][:, :], psum[:, 0, :], ACT.Tanh).then_inc(ph["lora_w"], 1)
                        for k in range(KT):
                            act.activation(mix[name][:, k, 0:w], xx[:, k, 0:w], ACT.Copy, scale=cols[:, g * KT + k:g * KT + k + 1]).then_inc(ph["weighted"], 1)

                @ph.block.gpsimd
                def _(pool):
                    pool.memset(self.gn_eps[:, :], GN_EPS).then_inc(ph["eps_set"], 1)
                    n = 0
                    for k in range(KT):
                        h, d = hT[:, k, S:2 * S], xx[:, k, S:2 * S]
                        if k < KT // 2:
                            inner, other, own, edge = d[:, 1:], h[:, 0:S - 1], h[:, 1:], slice(0, 1)
                        else:
                            inner, other, own, edge = d[:, 0:S - 1], h[:, 1:], h[:, 0:S - 1], slice(S - 1, S)
                        pool.tensor_tensor(inner, other, own, ALU.subtract).then_inc(ph["context_shifted"], 1)
                        pool.tensor_scalar(d[:, edge], h[:, edge], -1.0, None, ALU.mult).then_inc(ph["context_shifted"], 1)
                    for g, name, w in shared:
                        for k in range(KT):
                            n += 1
                            pool.wait_ge(ph["weighted"], n)
                            pool.tensor_tensor(mix[name][:, k, 0:w], mix[name][:, k, 0:w], hT[:, k, 0:w], ALU.add).then_inc(ph["summed"], 1)

    def rwkv_room(self, sb):
        C, XC, BD = self.C, self.XC, self.BD
        room = [self.ring[:, 2:SLOTS, :].rearrange("p s n -> p (s n)"), self.x[:, :, :].rearrange("p t d -> p (t d)")]
        left = [2 * KT * WIDE, NT * D]
        at = [0, 0]

        def carve(*shape):
            n = int(np.prod(shape))
            q = 0 if at[0] + n <= left[0] else 1
            if at[q] + n > left[q]:
                return sb(*shape)[(slice(None),) * (1 + len(shape))]
            v = room[q][:, at[q]:at[q] + n]
            at[q] += n
            names = "abc"[:len(shape)]
            if len(shape) > 1:
                v = v.rearrange(f"p ({' '.join(names)}) -> p {' '.join(names)}", **{c: n for c, n in zip(names, shape)})
            return v

        class Room:
            pass
        r = Room()
        r.w = self.ring[:, 1, :].rearrange("p (k j n) -> p k j n", j=4, n=P)
        bk = self.ring[:, 0, :].rearrange("p (q c n) -> p q c n", q=4, n=BD)
        r.btok, r.ktok = [bk[:, z] for z in range(2)], [bk[:, 2 + z] for z in range(2)]
        r.U = [self.hT[:, 2 * z:2 * z + 2, :].rearrange("p k (c n) -> p (k c) n", n=BD) for z in range(2)]
        r.T = [self.hT[:, 4 + 2 * z:6 + 2 * z, :].rearrange("p k (c n) -> p (k c) n", n=BD) for z in range(2)]
        r.R = [self.xn[:, z, :].rearrange("p (c n) -> p c n", n=BD) for z in range(2)]
        r.ar = [carve(XC, 2, BD) for _ in range(2)]
        r.ac = [carve(C - XC, BD) for _ in range(2)]
        r.ax = [carve(XC, 3, BD) for _ in range(2)]
        r.akc = [carve(C - XC, BD) for _ in range(2)]
        r.bbd, r.kbd = [carve(C, BD) for _ in range(2)], [carve(C, BD) for _ in range(2)]
        r.B = r.bbd
        r.Vt = carve(C, BD)
        r.vbd = r.kbd[0]
        r.K, r.KK = carve(2 * S), carve(2 * S)
        r.L, r.sig, r.al, r.kd, r.E3 = ([carve(2 * S) for _ in range(2)] for _ in range(5))
        r.E1, r.E2 = r.L, r.sig
        r.kw, r.kn = self.xn[:, 1, 0:2 * S], self.xn[:, 1, 2 * S:4 * S]
        r.Rr, r.V, r.G, r.Gs, r.Gh, r.BV = (carve(S) for _ in range(6))
        r.prod = [carve(S) for _ in range(2)]
        r.cur, r.ln, r.D = sb(10), sb(2), sb(2, C)
        r.St, r.DS, r.Rs, r.Us = ([r.T[0][:, 2 * q + z, :] for z in range(2)] for q in range(4))
        r.y, r.cen, r.yn = (r.T[1][:, 2 * q:2 * q + 2, :].rearrange("p c n -> p (c n)") for q in range(3))
        r.w2, r.a2 = r.T[1][:, 6, :], r.T[1][:, 7, :]
        r.uo = r.cen
        return r

    def rwkv_step(self, r, head, tail, mix, lora, prm, uT):
        a, psum, ident = self.a, self.psum, self.ident
        C, XC, BD = self.C, self.XC, self.BD
        DECAY = float(np.exp(-0.5))
        LEVELS = 5
        order = [list(range(XC, C)) + list(range(XC)), list(range(C - 1, XC - 1, -1)) + list(range(XC - 1, -1, -1))]
        heads = (slice(0, CH), slice(CH, P))
        doing_head, doing_tail = head is not None, tail is not None
        W0, A0, KKW, KA, RK, LNW, OMK = 0, 2, 4, 5, 6, 7, 9

        def col(j):
            return r.cur[:, j:j + 1]

        def a_of(z, c):
            return r.ar[z][:, c, 0, :] if c < XC else r.ac[z][:, c - XC, :]

        def four(v, half):
            return v[:, 4 * half:4 * half + 4, :]

        def bank(b):
            return psum[:, b, :].rearrange("p (c n) -> p c n", n=BD)

        def chunks(v):
            return v.rearrange("p (c s) -> p c s", s=CH)

        with self.phase() as ph:
            def load_weights(sp):
                wv = a["l0_w_in"].rearrange("(k p) n -> p k n", p=P)
                for j in (1, 0, 3, 2):
                    sp.dma_start(r.w[:, :, j, :], wv[:, :, bass.ds(tail * P + j * E, P)]).then_inc(ph[f"w{j}_in"], 16)
                    if j == 2:
                        if doing_head:
                            sp.wait_ge(ph["u_made"], 4 * LEVELS)
                        sp.dma_start(r.w2, a["l0_w2"].rearrange("z r e -> (z r) e")[:, bass.ds(tail * P, P)]).then_inc(ph["lora_in"], 16)
                        sp.dma_start(r.a2, a["l0_a2"].rearrange("z r e -> (z r) e")[:, bass.ds(tail * P, P)]).then_inc(ph["lora_in"], 16)

            @ph.block.sync
            def _(sp):
                if doing_tail:
                    load_weights(sp)
                if doing_head:
                    sp.wait_ge(ph["u_out"], 1)
                    sp.dma_start(uT[:, bass.ds(head, 1), :].rearrange("p a s -> p (a s)"), r.uo).then_inc(ph["u_stored"], 16)
                    sp.wait_ge(ph["u_stored"], 16)

            @ph.block.tensor
            def _(pe):
                def project():
                    def whole(j, name, b, o, n):
                        for k in range(KT):
                            if k == 0:
                                pe.wait_ge(ph[f"w{j}_in"], 16)
                            mm = pe.matmul(psum[:, b, o:o + n], r.w[:, k, j, :], mix[name][:, k, 0:n], start=(k == 0), stop=(k == KT - 1))
                            if k == KT - 1:
                                mm.then_inc(ph["proj_ready"], 1)
                            if n == 2 * S or k % 2:
                                yield
                    def rank(what, z, b):
                        zs = slice(LORA * z, LORA * z + LORA)
                        pe.matmul(psum[:, b, :], {"w": r.w2, "a": r.a2}[what][zs, :], lora[what][zs, :], start=True, stop=True).then_inc(ph["lora_ready"], 1)

                    yield from whole(1, "k", 4, 0, 2 * S)
                    pe.wait_ge(ph["lora_in"], 32)
                    rank("w", 0, 7)
                    yield
                    yield from whole(0, "r", 5, 0, S)
                    gate = whole(3, "g", 5, S, S)
                    yield from gate
                    pe.wait_ge(ph["k_ready"], 1)
                    pe.wait_ge(ph["kk_squared"], 1)
                    pe.matmul(psum[:, 4, :], self.same_head[:, :], r.kn, start=True, stop=True).then_inc(ph["kk_summed"], 1)
                    yield
                    pe.wait_ge(ph["sig_ready"], 1)
                    rank("a", 0, 7)
                    yield
                    value = whole(2, "v", 6, 0, 2 * S)
                    for _ in range(2):
                        next(value)
                        yield
                    pe.wait_ge(ph["kk_floored"], 1)
                    rank("w", 1, 4)
                    yield
                    for _ in range(2):
                        next(value)
                        yield
                    pe.wait_ge(ph["sig_ready"], 2)
                    rank("a", 1, 7)
                    yield
                    yield from value

                work = project() if doing_tail else iter(())
                if doing_head:
                    for z in range(2):
                        mm = pe.matmul(psum[:, 7, 0:S], self.same_head[:, :], r.prod[z], start=(z == 0), stop=(z == 1))
                    mm.then_inc(ph["bonus_made"], 1)
                    for j in range(4):
                        z, half = j // 2, j % 2
                        for c in range(4):
                            mm = pe.transpose(psum[:, j, c * BD:(c + 1) * BD], r.R[z][:, 4 * half + c, :], ident[:, :])
                        mm.then_inc(ph["b_turned"], 1)
                    for j in range(4):
                        z, half = j // 2, j % 2
                        if j >= 2:
                            pe.wait_ge(ph["u_level"], j - 1)
                        if j == 3:
                            pe.wait_ge(ph["bonus_read"], 1)
                        for c in range(4):
                            mm = pe.transpose(psum[:, 4 + j, c * BD:(c + 1) * BD], r.U[z][:, 4 * half + c, :], ident[:, :])
                        mm.then_inc(ph["t_turned"], 1)
                    for m in range(LEVELS):
                        for j in range(4):
                            z, half = j // 2, j % 2
                            pe.wait_ge(ph["b_ready"], j + 1)
                            if m or j >= 2:
                                pe.wait_ge(ph["u_level"], 4 * m + j - 1)
                            pe.wait_ge(ph["t_level"], 4 * m + j + 1)
                            for c in range(4):
                                cc = 4 * half + c
                                mm = pe.matmul(psum[:, j, c * BD:(c + 1) * BD], r.B[z][:, cc, :], r.U[z][:, cc, :], start=True, stop=True)
                            mm.then_inc(ph["r_made"], 1)
                        for j in range(4):
                            z, half = j // 2, j % 2
                            pe.wait_ge(ph["r_level"], 4 * m + j + 1)
                            for c in range(4):
                                cc = 4 * half + c
                                mm = pe.matmul(psum[:, 4 + j, c * BD:(c + 1) * BD], r.T[z][:, cc, :], r.R[z][:, cc, :], start=True, stop=True)
                            mm.then_inc(ph["u_made"], 1)
                        if m < LEVELS - 1:
                            for j in range(4):
                                z, half = j // 2, j % 2
                                pe.wait_ge(ph["u_level"], 4 * (m + 1) + j - 1)
                                for c in range(4):
                                    mm = pe.transpose(psum[:, j, c * BD:(c + 1) * BD], r.U[z][:, 4 * half + c, :], ident[:, :])
                                mm.then_inc(ph["t_turned"], 1)
                    pe.wait_ge(ph["r_level"], 4 * LEVELS)
                    for n in range(C):
                        for z in range(2):
                            c = order[z][n]
                            ak = r.ax[z][:, c, 1, :] if c < XC else r.akc[z][:, c - XC, :]
                            if n:
                                pe.wait_ge(ph[f"state_{z}"], n)
                                pe.matmul(psum[:, z, 0:BD], a_of(z, c), r.St[z], start=True, stop=False)
                            pe.matmul(psum[:, z, 0:BD], ak, r.Vt[:, c, :], start=(n == 0), stop=True).then_inc(ph[f"rhs_made_{z}"], 1)
                        if n == 0:
                            pe.wait_ge(ph["u_level"], 4 * LEVELS + 2)
                        next(work, None)
                        for z in range(2):
                            c = order[z][n]
                            pe.wait_ge(ph[f"rhs_{z}"], n + 1)
                            pe.matmul(psum[:, z, BD:2 * BD], r.U[z][:, c, :], r.Rs[z], start=True, stop=True).then_inc(ph[f"u_made_{z}"], 1)
                        next(work, None)
                        next(work, None)
                        for z in range(2):
                            c = order[z][n]
                            pe.wait_ge(ph[f"u_{z}"], n + 1)
                            if n < C - 1:
                                pe.matmul(psum[:, z, 2 * BD:3 * BD], r.btok[z][:, c, :], r.Us[z], start=True, stop=False)
                                pe.matmul(psum[:, z, 2 * BD:3 * BD], r.ktok[z][:, c, :], r.Vt[:, c, :], start=False, stop=True).then_inc(ph[f"state_made_{z}"], 1)
                        for z in range(2):
                            c = order[z][n]
                            if c < XC:
                                ys = psum[:, 2 + z, c * BD:(c + 1) * BD]
                                pe.matmul(ys, r.St[z], r.ar[z][:, c, 1, :], start=True, stop=False)
                                pe.matmul(ys, r.Us[z], r.ax[z][:, c, 0, :], start=False, stop=False)
                                pe.matmul(ys, r.Vt[:, c, :], r.ax[z][:, c, 2, :], start=False, stop=True).then_inc(ph[f"y_made_{z}"], 1)
                        if n < 5:
                            next(work, None)
                for _ in work:
                    pass
                if doing_head:
                    pe.wait_ge(ph["y_ready"], 2)
                    pe.matmul(psum[:, 0, 0:S], self.head_mean[:, :], r.y, start=True, stop=True).then_inc(ph["mean_made"], 1)
                if doing_tail:
                    pe.wait_ge(ph["sig_ready"], 3)
                    pe.wait_ge(ph["g_ready"], 1)
                    pe.wait_ge(ph["v_ready"], 2)
                    for c in range(C):
                        mm = pe.transpose(psum[:, 4 + c // 4, (c % 4) * BD:(c % 4 + 1) * BD], r.vbd[:, c, :], ident[:, :])
                        if c % 4 == 3:
                            mm.then_inc(ph["v_turned"], 1)
                if doing_head:
                    pe.wait_ge(ph["squared"], 1)
                    pe.matmul(psum[:, 1, 0:S], self.head_mean[:, :], r.y, start=True, stop=True).then_inc(ph["var_made"], 1)
                if doing_tail:
                    for z in range(2):
                        if z == 0:
                            pe.wait_ge(ph["sig_ready"], 4)
                        else:
                            pe.wait_ge(ph["tok_ready"], 4)
                        for q, src in enumerate((r.bbd[z], r.kbd[z])):
                            pe.wait_ge(ph["bk"[q] + "_laid"], 2 * z + 2)
                            if z == 0 and q == 1:
                                pe.wait_ge(ph["vt_ready"], 2)
                            for c in range(C):
                                b = (7, 2, 4, 5)[2 * q + c // 4]
                                mm = pe.transpose(psum[:, b, (c % 4) * BD:(c % 4 + 1) * BD], src[:, c, :], ident[:, :])
                                if c % 4 == 3:
                                    mm.then_inc(ph["tok_turned"], 1)
                        pe.wait_ge(ph["ar_laid"], 7 * z + 7)
                        for c in range(C):
                            n = z * C + c
                            b = (0, 1, 6)[n % 3]
                            if n >= 3:
                                pe.wait_ge(ph["a_ready"], n - 2)
                            elif n == 0:
                                pe.wait_ge(ph["v_ready"], 3)
                                if doing_head:
                                    pe.wait_ge(ph["rooted"], 1)
                                    pe.wait_ge(ph["centred"], 1)
                            if c < XC:
                                ar = r.ar[z][:, c, :, :].rearrange("p q n -> p (q n)")
                                pe.matmul(psum[:, b, 0:2 * BD], r.bbd[z][:, c, :], ar, start=True, stop=True)
                                mm = pe.matmul(psum[:, b, 2 * BD:4 * BD], r.kbd[z][:, c, :], ar, start=True, stop=True)
                            else:
                                pe.matmul(psum[:, b, 0:BD], r.bbd[z][:, c, :], a_of(z, c), start=True, stop=True)
                                mm = pe.matmul(psum[:, b, 2 * BD:3 * BD], r.kbd[z][:, c, :], a_of(z, c), start=True, stop=True)
                            mm.then_inc(ph["a_made"], 1)

            @ph.block.scalar
            def _(act):
                def take():
                    act.wait_ge(ph["proj_ready"], 1)
                    act.activation(r.K, psum[:, 4, :], ACT.Copy).then_inc(ph["k_ready"], 1)
                    yield
                    act.wait_ge(ph["lora_ready"], 1)
                    act.wait_ge(ph["cur_ready"], 2)
                    act.activation(r.sig[0], psum[:, 7, :], ACT.Sigmoid, bias=col(W0)).then_inc(ph["sig_ready"], 1)
                    yield
                    act.wait_ge(ph["proj_ready"], 3)
                    if doing_head:
                        act.wait_ge(ph["gate_kept"], 1)
                    act.activation(r.Rr, psum[:, 5, 0:S], ACT.Copy).then_inc(ph["r_ready"], 1)
                    act.activation(r.G, psum[:, 5, S:2 * S], ACT.Copy).then_inc(ph["graw_ready"], 1)
                    act.activation(r.Gs, psum[:, 5, S:2 * S], ACT.Sigmoid).then_inc(ph["g_ready"], 1)
                    act.wait_ge(ph["lora_ready"], 2)
                    act.activation(r.al[0], psum[:, 7, :], ACT.Sigmoid, bias=col(A0)).then_inc(ph["sig_ready"], 1)
                    yield
                    act.wait_ge(ph["lora_ready"], 3)
                    act.activation(r.sig[1], psum[:, 4, :], ACT.Sigmoid, bias=col(W0 + 1)).then_inc(ph["sig_ready"], 1)
                    act.wait_ge(ph["kk_floored"], 1)
                    act.activation(r.KK, r.KK, ACT.Sqrt).then_inc(ph["kk_rooted"], 1)
                    yield
                    act.wait_ge(ph["lora_ready"], 4)
                    act.activation(r.al[1], psum[:, 7, :], ACT.Sigmoid, bias=col(A0 + 1)).then_inc(ph["sig_ready"], 1)
                    yield

                work = take() if doing_tail else iter(())
                if doing_head:
                    for j in range(4):
                        act.wait_ge(ph["b_turned"], j + 1)
                        act.activation(four(r.B[j // 2], j % 2), bank(j), ACT.Copy).then_inc(ph["b_ready"], 1)
                    for m in range(LEVELS):
                        for j in range(4):
                            z, half = j // 2, j % 2
                            act.wait_ge(ph["t_turned"], 4 * m + j + 1)
                            if m:
                                act.wait_ge(ph["u_made"], 4 * (m - 1) + j + 1)
                            act.activation(four(r.T[z], half), bank((4 if m == 0 else 0) + j), ACT.Copy).then_inc(ph["t_level"], 1)
                    for n in range(C):
                        for z in range(2):
                            c = order[z][n]
                            act.wait_ge(ph[f"rhs_made_{z}"], n + 1)
                            if n:
                                act.wait_ge(ph[f"u_made_{z}"], n)
                            act.activation(r.Rs[z], psum[:, z, 0:BD], ACT.Copy).then_inc(ph[f"rhs_{z}"], 1)
                        for z in range(2):
                            c = order[z][n]
                            if 0 < n < C - 1:
                                act.activation(r.DS[z], r.St[z], ACT.Copy, scale=r.D[:, z, c:c + 1]).then_inc(ph[f"ds_{z}"], 1)
                        if n in (2, 3, 5, 6, 7):
                            next(work, None)
                for _ in work:
                    pass
                if doing_tail:
                    act.wait_ge(ph["proj_ready"], 4)
                    act.wait_ge(ph["zeroed"], 1)
                    for h in range(2):
                        act.activation(r.vbd[heads[h], :, h * CH:(h + 1) * CH], chunks(psum[heads[h], 6, :]), ACT.Copy).then_inc(ph["v_ready"], 1)
                    if doing_head:
                        act.wait_ge(ph["bonus_read"], 1)
                    act.activation(r.V, psum[:, 6, 0:S], ACT.Copy).then_inc(ph["v_ready"], 1)
                    for z in range(2):
                        act.wait_ge(ph["l_ready"], 2 * z + 2)
                        act.activation(r.E3[z], r.L[z], ACT.Exp, scale=DECAY).then_inc(ph["e_ready"], 1)
                        act.wait_ge(ph["lex_ready"], z + 1)
                        act.activation(r.E1[z], r.L[z], ACT.Exp, scale=-DECAY).then_inc(ph["e_ready"], 1)
                        act.activation(r.E2[z], r.E2[z], ACT.Exp, scale=-DECAY).then_inc(ph["e_ready"], 1)
                    for q in range(2):
                        act.wait_ge(ph["v_turned"], q + 1)
                        act.activation(four(r.Vt, q), bank(4 + q), ACT.Copy).then_inc(ph["vt_ready"], 1)
                if doing_head:
                    act.wait_ge(ph["var_made"], 1)
                    act.activation(r.cen, psum[:, 1, 0:S], ACT.Sqrt, bias=self.gn_eps[:, 0:1]).then_inc(ph["rooted"], 1)
                if doing_tail:
                    for z in range(2):
                        for q in range(4):
                            act.wait_ge(ph["tok_turned"], 4 * z + q + 1)
                            act.activation(four((r.btok, r.ktok)[q // 2][z], q % 2), bank((7, 2, 4, 5)[q]), ACT.Copy).then_inc(ph["tok_ready"], 1)

            @ph.block.gpsimd
            def _(pool):
                if doing_head:
                    pool.tensor_tensor(r.Gh, r.G, r.Gs, ALU.mult).then_inc(ph["gate_kept"], 1)
                if not doing_tail:
                    return
                if doing_head:
                    pool.wait_ge(ph["r_made"], 4 * LEVELS)
                for t in r.bbd:
                    pool.memset(t[:, :, :], 0.0).then_inc(ph["zeroed"], 1)
                if not doing_head:
                    for t in (*r.kbd, r.ac[0], r.ac[1]):
                        pool.memset(t[:, :, :], 0.0).then_inc(ph["zeroed"], 1)
                    for t in (r.ar[0], r.ar[1]):
                        pool.memset(t[:, :, :, :], 0.0).then_inc(ph["zeroed"], 1)
                pool.wait_ge(ph["kk_weighted"], 1)
                pool.tensor_tensor(r.kn, r.kw, r.kw, ALU.mult).then_inc(ph["kk_squared"], 1)
                for z in range(2):
                    pool.wait_ge(ph["l_ready"], 2 * z + 2)
                    pool.tensor_tensor(r.E2[z], r.L[z], r.sig[z], ALU.subtract).then_inc(ph["lex_ready"], 1)
                    pool.wait_ge(ph["kd_scaled"], z + 1)
                    pool.tensor_tensor(r.kd[z], r.kd[z], r.K, ALU.mult).then_inc(ph["kd_ready"], 1)
                for z in range(2):
                    pool.wait_ge(ph["e_ready"], 3 * z + 1)
                    pool.wait_ge(ph["kd_ready"], z + 1)
                    if z == 0:
                        pool.wait_ge(ph["v_turned"], 2)
                        pool.wait_ge(ph["zeroed"], 2 if doing_head else 8)
                    for h in range(2):
                        hs, cs = heads[h], slice(h * CH, (h + 1) * CH)
                        if z or h:
                            pool.wait_ge(ph["k_laid"], 2 * z + h)
                        pool.tensor_tensor(r.kbd[z][hs, :, cs], chunks(r.kd[z][hs, :]), chunks(r.E3[z][hs, :]), ALU.mult).then_inc(ph["k_laid"], 1)
                pool.wait_ge(ph["k_laid"], 4)
                for z in range(2):
                    pool.wait_ge(ph["r_ready"], 1)
                    if doing_head:
                        pool.wait_ge(ph["bonus_made"], 1)
                    pool.tensor_tensor(r.prod[z], r.kd[z][:, 0:S], r.Rr, ALU.mult).then_inc(ph["prod_raw"], 1)
                for z in range(2):
                    pool.wait_ge(ph["prod_raw"], z + 1)
                    pool.tensor_scalar(r.prod[z], r.prod[z], col(RK), None, ALU.mult).then_inc(ph["prod_ready"], 1)
                pool.wait_ge(ph["aab_ready"], C)
                for j in (0, 1):
                    self.first_pair(ph, pool, r, j, "first_pairs")
                for j in (0, 1):
                    pool.wait_ge(ph["first_pairs"], j + 1)
                    self.add_identity(pool, r, j).then_inc(ph["u_begun"], 1)

            @ph.block.vector
            def _(dve):
                def prepare():
                    dve.tensor_copy(r.cur[:, 0:9], prm[:, 0:9, bass.ds(tail, 1)].rearrange("p j a -> p (j a)")).then_inc(ph["cur_ready"], 1)
                    dve.wait_ge(ph["cur_ready"], 1)
                    dve.tensor_scalar(r.cur[:, OMK:OMK + 1], r.cur[:, KA:KA + 1], -1.0, 1.0, ALU.mult, ALU.add).then_inc(ph["cur_ready"], 1)
                    dve.wait_ge(ph["cur_ready"], 2)
                    yield
                    dve.wait_ge(ph["k_ready"], 1)
                    dve.tensor_scalar(r.kw, r.K, col(KKW), None, ALU.mult).then_inc(ph["kk_weighted"], 1)
                    yield
                    dve.wait_ge(ph["kk_summed"], 1)
                    dve.tensor_scalar(r.KK, psum[:, 4, :], 1e-24, None, ALU.max).then_inc(ph["kk_floored"], 1)
                    yield
                    dve.wait_ge(ph["sig_ready"], 1)
                    self.decay_sums(ph, dve, r, 0)
                    yield
                    dve.wait_ge(ph["sig_ready"], 2)
                    dve.tensor_scalar(r.kd[0], r.al[0], col(KA), col(OMK), ALU.mult, ALU.add).then_inc(ph["kd_scaled"], 1)
                    dve.wait_ge(ph["kk_rooted"], 1)
                    dve.reciprocal(r.kn[:, 0:S], r.KK[:, 0:S]).then_inc(ph["kk_inverse"], 1)
                    yield
                    dve.reciprocal(r.kn[:, S:2 * S], r.KK[:, S:2 * S]).then_inc(ph["kk_inverse"], 1)
                    dve.wait_ge(ph["kk_inverse"], 2)
                    dve.tensor_tensor(r.KK, r.kw, r.kn, ALU.mult).then_inc(ph["kk_ready"], 1)
                    dve.wait_ge(ph["sig_ready"], 3)
                    self.decay_sums(ph, dve, r, 1)
                    yield
                    dve.wait_ge(ph["sig_ready"], 4)
                    dve.tensor_scalar(r.kd[1], r.al[1], col(KA), col(OMK), ALU.mult, ALU.add).then_inc(ph["kd_scaled"], 1)
                    yield

                work = prepare() if doing_tail else iter(())
                if doing_head:
                    dve.tensor_copy(r.ln[:, :], prm[:, LNW:LNW + 2, bass.ds(head, 1)].rearrange("p j a -> p (j a)")).then_inc(ph["ln_ready"], 1)
                    for j in (2, 3):
                        self.first_pair(ph, dve, r, j)
                    for j in (2, 3):
                        dve.wait_ge(ph["pairs"], j - 1)
                        self.add_identity(dve, r, j).then_inc(ph["u_level"], 1)
                    dve.wait_ge(ph["bonus_made"], 1)
                    dve.tensor_tensor(r.BV, psum[:, 7, 0:S], r.V, ALU.mult).then_inc(ph["bonus_read"], 1)
                    for m in range(LEVELS):
                        for j in range(4):
                            z, half = j // 2, j % 2
                            dve.wait_ge(ph["r_made"], 4 * m + j + 1)
                            dve.tensor_tensor(four(r.R[z], half), bank(j), self.level[:, z, m + 1, :].unsqueeze(1).to_broadcast([P, 4, BD]),
                                              ALU.mult).then_inc(ph["r_level"], 1)
                        for j in range(4):
                            z, half = j // 2, j % 2
                            dve.wait_ge(ph["u_made"], 4 * m + j + 1)
                            dve.tensor_tensor(four(r.U[z], half), bank(4 + j), four(r.U[z], half), ALU.add).then_inc(ph["u_level"], 1)
                    next(work, None)
                    for n in range(C):
                        for z in range(2):
                            dve.wait_ge(ph[f"u_made_{z}"], n + 1)
                            if n:
                                dve.wait_ge(ph[f"state_made_{z}"], n)
                                if order[z][n - 1] < XC:
                                    dve.wait_ge(ph[f"y_made_{z}"], n - XC)
                            dve.tensor_copy(r.Us[z], psum[:, z, BD:2 * BD]).then_inc(ph[f"u_{z}"], 1)
                        for z in range(2):
                            if n == C - 1:
                                continue
                            c = order[z][n]
                            dve.wait_ge(ph[f"state_made_{z}"], n + 1)
                            if c < XC:
                                dve.wait_ge(ph[f"y_made_{z}"], n - XC + 1)
                            if n == 0:
                                dve.tensor_scalar(r.St[z], psum[:, z, 2 * BD:3 * BD], r.D[:, z, c:c + 1], None, ALU.mult).then_inc(ph[f"state_{z}"], 1)
                            else:
                                dve.wait_ge(ph[f"ds_{z}"], n)
                                dve.scalar_tensor_tensor(out=r.St[z], in0=psum[:, z, 2 * BD:3 * BD], scalar=r.D[:, z, c:c + 1], in1=r.DS[z],
                                                         op0=ALU.mult, op1=ALU.add).then_inc(ph[f"state_{z}"], 1)
                        if n >= 3:
                            next(work, None)
                    for z in range(2):
                        dve.wait_ge(ph[f"y_made_{z}"], XC)
                    for h in range(2):
                        dve.tensor_copy(chunks(r.cen[heads[h], :]), bank(2)[heads[h], :, h * CH:(h + 1) * CH]).then_inc(ph["y_half"], 1)
                    for h in range(2):
                        dve.wait_ge(ph["y_half"], h + 1)
                        dve.tensor_tensor(chunks(r.y[heads[h], :]), bank(3)[heads[h], :, h * CH:(h + 1) * CH], chunks(r.cen[heads[h], :]), ALU.add).then_inc(ph["y_ready"], 1)
                for _ in work:
                    pass
                if doing_head:
                    dve.wait_ge(ph["mean_made"], 1)
                    dve.wait_ge(ph["y_ready"], 2)
                    dve.tensor_tensor(r.yn, r.y, psum[:, 0, 0:S], ALU.subtract).then_inc(ph["centred"], 1)
                    dve.wait_ge(ph["centred"], 1)
                    dve.tensor_tensor(r.y, r.yn, r.yn, ALU.mult).then_inc(ph["squared"], 1)
                if doing_tail:
                    dve.wait_ge(ph["kk_ready"], 1)
                    dve.wait_ge(ph["zeroed"], 2 if doing_head else 8)
                    for z in range(2):
                        dve.tensor_tensor(r.al[z], r.al[z], r.KK, ALU.mult).then_inc(ph["b_vec"], 1)
                    for z in range(2):
                        dve.wait_ge(ph["e_ready"], 3 * z + 1)
                        dve.wait_ge(ph["b_vec"], z + 1)
                        for h in range(2):
                            hs, cs = heads[h], slice(h * CH, (h + 1) * CH)
                            dve.tensor_tensor(r.bbd[z][hs, :, cs], chunks(r.al[z][hs, :]), chunks(r.E3[z][hs, :]), ALU.mult).then_inc(ph["b_laid"], 1)
                        dve.wait_ge(ph["e_ready"], 3 * z + 3)
                        for h in range(2):
                            hs, cs = heads[h], slice(h * CH, (h + 1) * CH)
                            for dst, o in ((r.ar[z][hs, :, 0, cs], 0), (r.ac[z][hs, :, cs], S)):
                                dve.scalar_tensor_tensor(out=dst, in0=chunks(r.KK[hs, o:o + S]), scalar=-1.0, in1=chunks(r.E2[z][hs, o:o + S]),
                                                         op0=ALU.mult, op1=ALU.mult).then_inc(ph["ar_laid"], 1)
                            dve.tensor_tensor(r.ar[z][hs, :, 1, cs], chunks(r.Rr[hs, :]), chunks(r.E1[z][hs, 0:S]), ALU.mult).then_inc(ph["ar_laid"], 1)
                        dve.tensor_copy(r.D[:, z, :], chunks(r.E1[z])[:, :, CH - 1 if z == 0 else 0]).then_inc(ph["ar_laid"], 1)
                    for z in range(2):
                        for c in range(C):
                            n = z * C + c
                            b = (0, 1, 6)[n % 3]
                            dve.wait_ge(ph["a_made"], n + 1)
                            dve.tensor_tensor(r.R[z][:, c, :], psum[:, b, 0:BD], self.strict[:, z, 1, :], ALU.mult).then_inc(ph["aab_ready"], 1)
                            if c < XC:
                                dve.tensor_tensor(r.ax[z][:, c, :, :], psum[:, b, BD:4 * BD].rearrange("p (q n) -> p q n", q=3), self.strict[:, z, :, :],
                                                  ALU.mult).then_inc(ph["a_ready"], 1)
                            else:
                                dve.tensor_tensor(r.akc[z][:, c - XC, :], psum[:, b, 2 * BD:3 * BD], self.strict[:, z, 1, :], ALU.mult).then_inc(ph["a_ready"], 1)
                        if z == 0 and doing_head:
                            self.rwkv_gate(ph, dve, r, head, uT)
                elif doing_head:
                    self.rwkv_gate(ph, dve, r, head, uT)

    def first_pair(self, ph, eng, r, j, done="pairs"):
        z, four = j // 2, slice(4 * (j % 2), 4 * (j % 2) + 4)
        eng.tensor_tensor(r.U[z][:, four, :], r.R[z][:, four, :], self.level[:, z, 0, :].unsqueeze(1).to_broadcast([P, 4, self.BD]),
                          ALU.mult).then_inc(ph[done], 1)

    def add_identity(self, eng, r, j):
        us = r.U[j // 2][:, 4 * (j % 2):4 * (j % 2) + 4, :]
        return eng.tensor_tensor(us, us, self.ident[:, :].unsqueeze(1).to_broadcast([P, 4, self.BD]), ALU.add)

    def decay_sums(self, ph, dve, r, z):
        for o in (0, S):
            out, sig = r.L[z][:, o:o + S], r.sig[z][:, o:o + S]
            if z:
                out, sig = out[:, ::-1], sig[:, ::-1]
            dve.tensor_tensor_scan(out, self.no_start[:, :], sig, 0.0, ALU.mult, ALU.add).then_inc(ph["l_ready"], 1)

    def rwkv_gate(self, ph, dve, r, head, uT):
        yn = r.yn
        dve.wait_ge(ph["rooted"], 1)
        dve.reciprocal(r.y, r.cen).then_inc(ph["gn_inverse"], 1)
        dve.wait_ge(ph["gn_inverse"], 1)
        dve.tensor_tensor(yn, yn, r.y, ALU.mult).then_inc(ph["gn_scaled"], 1)
        dve.wait_ge(ph["gn_scaled"], 1)
        dve.wait_ge(ph["ln_ready"], 1)
        dve.tensor_scalar(yn, yn, r.ln[:, 0:1], r.ln[:, 1:2], ALU.mult, ALU.add).then_inc(ph["gn_scaled"], 1)
        dve.wait_ge(ph["gn_scaled"], 2)
        dve.wait_ge(ph["bonus_read"], 1)
        dve.tensor_tensor(yn, yn, r.BV, ALU.add).then_inc(ph["gn_scaled"], 1)
        dve.wait_ge(ph["gn_scaled"], 3)
        dve.wait_ge(ph["gate_kept"], 1)
        dve.tensor_tensor(r.uo, yn, r.Gh, ALU.mult).then_inc(ph["u_out"], 1)

    def rwkv_layer(self):
        a = self.a
        self.C, self.XC, self.BD = 2 * S // CH, S // CH, 2 * CH
        with ExitStack() as ctx:
            u_dram = self.nc.dram_tensor("u_scratch", [P, ET, S], F32, kind="Internal").ap()
            with ExitStack() as inner:
                sb = self.scratch(inner)
                mu, prm = sb(6 * KT), sb(9 * ET)
                mix = {"r": sb(KT, S), "k": sb(KT, 2 * S), "v": sb(KT, 2 * S), "g": sb(KT, S)}
                lora = {"w": sb(2 * S), "a": sb(2 * S)}

                def rows(name):
                    v = a[name]
                    if len(v.shape) == 2:
                        v = v.rearrange("a b -> (a b)")
                    return v.rearrange("(n p) -> n p", p=P)
                with ExitStack() as early:
                    sb = self.scratch(early)
                    ctx_x = sb(NT, D)

                    class Context:
                        @staticmethod
                        def load(ph, eng):
                            eng.dma_start(ctx_x[:, :, :], a["ctx"][0].rearrange("(t p) d -> p t d", p=P)).then_inc(ph["ctx_in"], 16)

                        @staticmethod
                        def scalar(ph, act):
                            act.wait_ge(ph["ctx_in"], 16)

                        @staticmethod
                        def tensor(ph, pe):
                            yield

                        @staticmethod
                        def vector(ph, dve):
                            yield
                    turned = self.turn_rows(sb, [([rows("l0_mu")], mu), ([rows("l0_" + n) for n in ("w0", "a0", "k_k", "k_a", "r_k", "ln_w", "ln_b")], prm)])
                    self.adaln(0, 2, (turned, Context))
                    self.norm_first([(self.x, 0, 0), (ctx_x, 1, S)])
                with ExitStack() as cst:
                    sb = self.scratch(cst)
                    self.strict, self.level, self.no_start = sb(2, 3, P), sb(2, 6, P), sb(S)
                    self.same_head, self.head_mean, self.gn_eps = sb(P), sb(P), sb(1)
                    self.rwkv_mixes(mix, lora, mu)
                    room = self.rwkv_room(sb)
                    prm3 = prm[:, :].rearrange("p (j e) -> p j e", e=ET)
                    self.rwkv_step(room, None, 0, mix, lora, prm3, u_dram)
                    with self.nc.Fori(0, ET - 1) as i:
                        self.rwkv_step(room, i, i + 1, mix, lora, prm3, u_dram)
                    self.rwkv_step(room, ET - 1, None, mix, lora, prm3, u_dram)
            uT = self.scratch(ctx)(ET, S)
            self.out_first(0, uT, u_dram)

    def hyena_hidden(self, sb, hdn, dft, idft, turned):
        a, psum = self.a, self.psum
        W = HW
        TWO_PI, ROUND = float(2 * np.pi), 1.5 * 2.0 ** 23
        LIMIT = 3.1415925
        z, w1, w23 = sb(S), sb(W), sb(2, W)
        b, turns = sb(4), sb(S)
        allow = self.nc.allow_non_contiguous_dma

        class Side:
            @staticmethod
            def load(ph, eng):
                eng.dma_start(z[0:EMB, :], a["k_pos"]).then_inc(ph["hidden_in"], 16)
                eng.dma_start(w1[0:EMB, :], a["l1_f_w1"]).then_inc(ph["hidden_in"], 16)
                for j, name in enumerate(("l1_f_w2", "l1_f_w3")):
                    eng.dma_start(w23[0:W, j, :], a[name]).then_inc(ph["hidden_in"], 16)
                with allow(reason="64-element vectors"):
                    for j, name in enumerate(("l1_f_b1", "l1_f_b2", "l1_f_b3", "l1_sin_freq")):
                        eng.dma_start(b[0:W, j:j + 1], a[name].rearrange("(p a) -> p a", a=1)).then_inc(ph["hidden_in"], 16)
                eng.dma_start(dft[:, :, :], a["k_dft"]).then_inc(ph["dft_in"], 16)
                eng.dma_start(idft[:, :, :], a["k_idft"]).then_inc(ph["dft_in"], 16)

            @staticmethod
            def tensor(ph, pe):
                pe.wait_ge(ph["hidden_in"], 16 * 8)
                pe.wait_ge(ph["cols_ready"], turned.tiles)
                pe.matmul(psum[0:W, 7, 0:S], w1[0:EMB, :], z[0:EMB, :], start=True, stop=True).then_inc(ph["layer_made"], 1)
                yield
                for j in range(2):
                    pe.wait_ge(ph["layer_ready"], j + 1)
                    pe.matmul(psum[0:W, 7, 0:S], w23[0:W, j, :], hdn[0:W, :], start=True, stop=True).then_inc(ph["layer_made"], 1)
                    yield

            @staticmethod
            def vector(ph, dve):
                dve.wait_ge(ph["hidden_in"], 16 * 8)
                h, t = hdn[0:W, :], turns[0:W, :]
                n = 0

                def chained(ins):
                    nonlocal n
                    n += 1
                    ins.then_inc(ph["reduced"], 1)
                    dve.wait_ge(ph["reduced"], n)
                for j in range(3):
                    dve.wait_ge(ph["layer_made"], j + 1)
                    chained(dve.tensor_scalar(h, psum[0:W, 7, 0:S], b[0:W, j:j + 1], b[0:W, 3:4], ALU.add, ALU.mult))
                    chained(dve.tensor_scalar(t, h, 1.0 / TWO_PI, ROUND, ALU.mult, ALU.add))
                    chained(dve.tensor_scalar(t, t, -ROUND, -TWO_PI, ALU.add, ALU.mult))
                    chained(dve.tensor_tensor(h, h, t, ALU.add))
                    dve.tensor_scalar(h, h, LIMIT, -LIMIT, ALU.min, ALU.max).then_inc(ph["angle_ready"], 1)
                    yield

            @staticmethod
            def scalar(ph, act):
                for j in range(3):
                    act.wait_ge(ph["angle_ready"], j + 1)
                    act.activation(hdn[0:W, :], hdn[0:W, :], ACT.Sin).then_inc(ph["layer_ready"], 1)
                act.wait_ge(ph["dft_in"], 32)
        return Side

    def hyena_tiles(self, i, U, h_hi, h_lo, hdn, prm, dft, idft, uT):
        a, psum, ident = self.a, self.psum, self.ident
        BUFS = 4
        with ExitStack() as ctx:
            sb = self.scratch(ctx)
            w_hi, w_lo = self.split_pair(ctx, BUFS, KT, P)
            cur = sb(U, 13)
            fw, win = [sb(2, P) for _ in range(2)], [sb(NT, P) for _ in range(2)]
            pad = [sb(3, S + 2) for _ in range(2)]
            gate, conv = [sb(S) for _ in range(2)], [sb(3, S) for _ in range(2)]
            ut = [sb(NT, P) for _ in range(2)]
            hw, fsum, fdif = sb(NT, 2, P), sb(NT, P), sb(NT, P)
            AB, m1, m2, Y, Yf = sb(2, S), sb(2, S), sb(2, S), sb(2, S), sb(4, P)
            long = sb(S)
            w = self.ring[:, :, :].rearrange("p s (k j n) -> p s k j n", j=4, n=P)
            COL = (2, 1, 0, 3)
            with self.phase() as ph:
                @ph.block.sync
                def _(sp):
                    wv = a["l1_w_in"].rearrange("(k p) n -> p k n", p=P)
                    for u in range(U):
                        ct = i * U + u
                        for j in range(4):
                            if u >= SLOTS:
                                sp.wait_ge(ph["w_split"], 4 * (u - SLOTS) + j + 1)
                            sp.dma_start(w[:, u % SLOTS, :, j, :], wv[:, :, bass.ds(ct * P + COL[j] * E, P)]).then_inc(ph[f"w_in_{u % SLOTS}_{j}"], 16)
                        if u >= 2:
                            sp.wait_ge(ph["filter_made"], u - 1)
                            sp.wait_ge(ph["windowed"], u - 1)
                        sp.dma_start(fw[u % 2][0:HW, :, :], a["l1_f_w4"].rearrange("p (b n) -> p b n", b=2)[:, :, bass.ds(ct * P, P)]).then_inc(ph[f"filter_in_{u % 2}"], 16)
                        sp.dma_start(win[u % 2][:, :, :], a["k_window"].rearrange("(t p) n -> p t n", p=P)[:, :, bass.ds(ct * P, P)]).then_inc(ph[f"filter_in_{u % 2}"], 16)

                @ph.block.tensor
                def _(pe):
                    def piece(u, j):
                        if u >= U:
                            return
                        bank = 2 * (u % 2) + j // 2
                        pe.wait_ge(ph["w_split"], 4 * u + j + 1)
                        if u >= 2 and j % 2 == 0:
                            pe.wait_ge(ph["copied"], 3 * (u - 2) + (1, 3)[j // 2])
                        for k in range(KT):
                            for n, (wp, h) in enumerate(((w_hi, h_hi), (w_hi, h_lo), (w_lo, h_hi))):
                                mm = pe.matmul(psum[:, bank, (j % 2) * S:(j % 2 + 1) * S], wp[:, j, k, :], h[:, k, :],
                                               start=(k == 0 and n == 0), stop=(k == KT - 1 and n == 2))
                        mm.then_inc(ph["proj_ready"], 1)
                    for j in range(4):
                        piece(0, j)
                    for u in range(U):
                        pe.wait_ge(ph[f"filter_in_{u % 2}"], 32 * (u // 2 + 1))
                        if u:
                            pe.wait_ge(ph["yf_ready"], u)
                        for t in range(NT):
                            mm = pe.matmul(psum[:, 4, t * S:(t + 1) * S], hdn[0:HW, t * P:(t + 1) * P], fw[u % 2][0:HW, :, :].rearrange("p b n -> p (b n)"),
                                           start=True, stop=True)
                        mm.then_inc(ph["filter_made"], 1)
                        piece(u + 1, 0)
                        pe.wait_ge(ph["product_ready"], u + 1)
                        if u:
                            pe.wait_ge(ph["long_read"], u)
                        for t in range(NT):
                            mm = pe.transpose(psum[:, 5, t * P:(t + 1) * P], conv[u % 2][:, 0, t * P:(t + 1) * P], ident[:, :])
                        mm.then_inc(ph["ut_made"], 1)
                        piece(u + 1, 1)
                        pe.wait_ge(ph["fsum_ready"], u + 1)
                        pe.wait_ge(ph["fdif_ready"], u + 1)
                        pe.wait_ge(ph["ut_ready"], u + 1)
                        if u:
                            pe.wait_ge(ph["cd_read"], 2 * u)
                        for src, o in ((fsum, 0), (fdif, S)):
                            for t in range(NT):
                                mm = pe.matmul(psum[:, 7, o:o + S], src[:, t, :], dft[:, t, o:o + S], start=(t == 0), stop=(t == NT - 1))
                        mm.then_inc(ph["cd_made"], 1)
                        for t in range(NT):
                            mm = pe.matmul(psum[:, 6, :], ut[u % 2][:, t, :], dft[:, t, :], start=(t == 0), stop=(t == NT - 1))
                        mm.then_inc(ph["ab_made"], 1)
                        piece(u + 1, 2)
                        pe.wait_ge(ph["spectrum_ready"], 2 * u + 2)
                        for q in range(4):
                            mm = pe.transpose(psum[:, 4, q * P:(q + 1) * P], Y[:, q // 2, (q % 2) * P:(q % 2 + 1) * P], ident[:, :])
                        mm.then_inc(ph["yf_made"], 1)
                        piece(u + 1, 3)
                        pe.wait_ge(ph["yf_ready"], u + 1)
                        for q in range(4):
                            mm = pe.matmul(psum[:, 5, S:2 * S], Yf[:, q, :], idft[:, q, :], start=(q == 0), stop=(q == 3))
                        mm.then_inc(ph["long_made"], 1)

                @ph.block.scalar
                def _(act):
                    def load(u):
                        if u >= U:
                            return
                        b, d = 2 * (u % 2), u % 2
                        act.wait_ge(ph["edges"], 2)
                        act.wait_ge(ph["proj_ready"], 4 * u + 2)
                        if u >= 2:
                            act.wait_ge(ph["tile_done"], u - 1)
                        act.activation(pad[d][:, 0:2, 1:S + 1], psum[:, b, :].rearrange("p (j s) -> p j s", j=2), ACT.Copy).then_inc(ph["copied"], 1)
                        act.wait_ge(ph["proj_ready"], 4 * u + 4)
                        act.activation(pad[d][:, 2, 1:S + 1], psum[:, b + 1, 0:S], ACT.Copy).then_inc(ph["copied"], 1)
                        act.activation(gate[d][:, :], psum[:, b + 1, S:2 * S], ACT.Silu).then_inc(ph["copied"], 1)

                    def round_piece(u, j):
                        if u >= U:
                            return
                        act.wait_ge(ph[f"w_in_{u % SLOTS}_{j}"], 16 * (u // SLOTS + 1))
                        if u:
                            act.wait_ge(ph["proj_ready"], 4 * (u - 1) + j + 1)
                        act.activation(w_hi[:, j, :, :], w[:, u % SLOTS, :, j, :], ACT.Copy).then_inc(ph["w_rounded"], 1)
                    for j in range(4):
                        round_piece(0, j)
                    for j in range(2):
                        round_piece(1, j)
                    load(0)
                    for j in range(2, 4):
                        round_piece(1, j)
                    for u in range(U):
                        act.wait_ge(ph["ut_made"], u + 1)
                        act.activation(ut[u % 2][:, :, :], psum[:, 5, 0:S].rearrange("p (t n) -> p t n", t=NT), ACT.Copy).then_inc(ph["ut_ready"], 1)
                        round_piece(u + 2, 0)
                        act.wait_ge(ph["ab_made"], u + 1)
                        if u:
                            act.wait_ge(ph["cd_read"], 2 * u)
                        act.activation(AB[:, :, :], psum[:, 6, :].rearrange("p (q s) -> p q s", q=2), ACT.Copy).then_inc(ph["ab_ready"], 1)
                        round_piece(u + 2, 1)
                        act.wait_ge(ph["yf_made"], u + 1)
                        if u:
                            act.wait_ge(ph["long_made"], u)
                        act.activation(Yf[:, :, :], psum[:, 4, :].rearrange("p (q n) -> p q n", q=4), ACT.Copy).then_inc(ph["yf_ready"], 1)
                        round_piece(u + 2, 2)
                        load(u + 1)
                        round_piece(u + 2, 3)

                @ph.block.gpsimd
                def _(pool):
                    for d in range(2):
                        pool.memset(pad[d][:, :, 0:S + 2:S + 1], 0.0).then_inc(ph["edges"], 1)

                @ph.block.vector
                def _(dve):
                    for u in range(U):
                        dve.tensor_copy(cur[:, u, :], prm[:, :, bass.ds(i * U + u, 1)].rearrange("p j a -> p (j a)")).then_inc(ph["cur_ready"], 1)

                    def rest_of_piece(u, j):
                        if u >= U:
                            return
                        dve.wait_ge(ph["w_rounded"], 4 * u + j + 1)
                        dve.tensor_tensor(w_lo[:, j, :, :], w[:, u % SLOTS, :, j, :], w_hi[:, j, :, :], ALU.subtract).then_inc(ph["w_split"], 1)
                    def convolve(u):
                        if u >= U:
                            return
                        d = u % 2
                        for j in range(3):
                            if j < 2:
                                dve.wait_ge(ph["copied"], 3 * u + 1)
                            else:
                                dve.wait_ge(ph["copied"], 3 * u + 2)
                            tap = [cur[:, u, 3 * q + COL[j]:3 * q + COL[j] + 1] for q in range(4)]
                            dve.tensor_scalar(conv[d][:, j, :], pad[d][:, j, 1:S + 1], tap[1], tap[3], ALU.mult, ALU.add).then_inc(ph["taps"], 1)
                        for q, o in ((0, 0), (2, 2)):
                            for j in range(3):
                                dve.wait_ge(ph["taps"], 9 * u + (3 if q else 0) + j + 1)
                                tap = cur[:, u, 3 * q + COL[j]:3 * q + COL[j] + 1]
                                dve.scalar_tensor_tensor(out=conv[d][:, j, :], in0=pad[d][:, j, o:o + S], scalar=tap, in1=conv[d][:, j, :],
                                                         op0=ALU.mult, op1=ALU.add).then_inc(ph["taps"], 1)
                        dve.wait_ge(ph["taps"], 9 * u + 8)
                        dve.tensor_tensor(conv[d][:, 0, :], conv[d][:, 0, :], conv[d][:, 1, :], ALU.mult).then_inc(ph["product_ready"], 1)
                    for u in range(2):
                        for j in range(4 if u == 0 else 2):
                            rest_of_piece(u, j)
                    dve.wait_ge(ph["cur_ready"], U)
                    for u in range(U):
                        d = u % 2
                        dve.wait_ge(ph["filter_made"], u + 1)
                        dve.wait_ge(ph[f"filter_in_{u % 2}"], 32 * (u // 2 + 1))
                        dve.tensor_tensor(hw[:, :, :, :], psum[:, 4, :].rearrange("p (t b n) -> p t b n", t=NT, b=2),
                                          win[d][:, :, :].unsqueeze(2).to_broadcast([P, NT, 2, P]), ALU.mult).then_inc(ph["windowed"], 1)
                        dve.wait_ge(ph["windowed"], u + 1)
                        if u:
                            dve.wait_ge(ph["cd_made"], u)
                        dve.tensor_tensor(fsum[:, :, :], hw[:, :, 0, :], hw[:, :, 1, :], ALU.add).then_inc(ph["fsum_ready"], 1)
                        dve.tensor_tensor(fdif[:, :, :], hw[:, :, 1, :], hw[:, :, 0, :], ALU.subtract).then_inc(ph["fdif_ready"], 1)
                        if u == 0:
                            for j in range(2, 4):
                                rest_of_piece(1, j)
                            convolve(0)
                        rest_of_piece(u + 2, 0)
                        dve.wait_ge(ph["ab_ready"], u + 1)
                        dve.wait_ge(ph["cd_made"], u + 1)
                        if u:
                            dve.wait_ge(ph["spectrum_ready"], 2 * u)
                        for m, o in ((m1, 0), (m2, S)):
                            dve.tensor_tensor(m[:, :, :], AB[:, :, :], psum[:, 7, o:o + S].unsqueeze(1).to_broadcast([P, 2, S]), ALU.mult).then_inc(ph["cd_read"], 1)
                        dve.wait_ge(ph["cd_read"], 2 * u + 2)
                        if u:
                            dve.wait_ge(ph["yf_made"], u)
                        dve.tensor_tensor(Y[:, 0, :], m1[:, 0, :], m2[:, 1, :], ALU.add).then_inc(ph["spectrum_ready"], 1)
                        dve.tensor_tensor(Y[:, 1, :], m2[:, 0, :], m1[:, 1, :], ALU.subtract).then_inc(ph["spectrum_ready"], 1)
                        rest_of_piece(u + 2, 1)
                        rest_of_piece(u + 2, 2)
                        convolve(u + 1)
                        dve.wait_ge(ph["product_ready"], u + 1)
                        dve.wait_ge(ph["long_made"], u + 1)
                        dve.scalar_tensor_tensor(out=long[:, :], in0=conv[d][:, 0, :], scalar=cur[:, u, 12:13], in1=psum[:, 5, S:2 * S],
                                                 op0=ALU.mult, op1=ALU.add).then_inc(ph["long_read"], 1)
                        dve.wait_ge(ph["long_read"], u + 1)
                        dve.wait_ge(ph["taps"], 9 * u + 9)
                        dve.tensor_tensor(long[:, :], long[:, :], conv[d][:, 2, :], ALU.mult).then_inc(ph["long_gated"], 1)
                        dve.wait_ge(ph["long_gated"], u + 1)
                        dve.wait_ge(ph["copied"], 3 * u + 3)
                        dve.tensor_tensor(uT[:, bass.ds(i * U + u, 1), :].rearrange("p a s -> p (a s)"), long[:, :], gate[d][:, :], ALU.mult).then_inc(ph["tile_done"], 1)
                        rest_of_piece(u + 2, 3)
                    dve.wait_ge(ph["tile_done"], U)

    def hyena_layer(self):
        a = self.a
        U = 8
        uT = self.hT[:, :, :].rearrange("p k (a s) -> p (k a) s", s=S)
        with ExitStack() as ctx:
            sb = self.scratch(ctx)
            prm, hdn = sb(13 * ET), sb(S)
            dft, idft = sb(NT, 2 * S), sb(4, S)
            h_hi, h_lo = self.split_pair(ctx, KT, S)

            def rows(name):
                v = a[name]
                if len(v.shape) == 2:
                    v = v.rearrange("a b -> (a b)")
                return v.rearrange("(n p) -> n p", p=P)
            with ExitStack() as early:
                sb = self.scratch(early)
                turned = self.turn_rows(sb, [([rows("l1_" + n) for n in ("conv_w", "conv_b", "filter_bias")], prm)])
                self.adaln(1, 1, (turned, self.hyena_hidden(sb, hdn, dft, idft, turned)))
            self.norm_first([(self.x, 0, 0)], (h_hi, h_lo))
            prm3 = prm[:, :].rearrange("p (j e) -> p j e", e=ET)
            with self.nc.Fori(0, ET // U) as i:
                self.hyena_tiles(i, U, h_hi, h_lo, hdn, prm3, dft, idft, uT)
        self.out_first(1, uT)


def build(nc, a, out):
    with ExitStack() as ctx:
        prog = Program(nc, ctx, a, out)
        prog.load_start()
        prog.rwkv_layer()
        prog.hyena_layer()
        with nc.Fori(0, 2) as l:
            prog.ffn(l, "ffn1_norm_2", "ffn1_w_gate_2", "ffn1_w_up_2", "ffn1_w_down_2")
            prog.mixer(l)
            prog.ffn(l, "ffn2_norm_2", "ffn2_w_gate_2", "ffn2_w_up_2", "ffn2_w_down_2")
        prog.finish()


def constants():
    f = np.float32
    pos = np.arange(S, dtype=f)
    half = P // 2
    inv = (f(10000.0) ** (-np.arange(half, dtype=f) / f(half))).astype(f)
    ang = pos[:, None] * inv[None, :]
    cos = np.concatenate([np.cos(ang)] * 2, 1)
    sin = np.concatenate([-np.sin(ang), np.sin(ang)], 1)
    rope = np.stack([np.stack([cos, sin]), np.stack([cos, sin]) * P ** -0.5])
    log_g = np.log1p(-np.exp2(-5.0 - np.arange(CHEADS, dtype=np.float64)))
    idx = np.arange(P)
    diff = idx[None, :] - idx[:, None]
    decay = np.where(diff[:, None, :] >= 0, np.exp(log_g[None, :, None] * np.maximum(diff, 0)[:, None, :]), 0.0)
    t = np.arange(P)
    j, h = t % CH, t // CH
    same = h[:, None] == h[None, :]
    before = np.stack([j[:, None] < j[None, :], j[:, None] > j[None, :]])
    upto = np.stack([j[:, None] <= j[None, :], j[:, None] >= j[None, :]])
    strict = np.stack([upto & same, before & same, upto & same], 2)
    level = np.stack([np.stack([b & same & (j[:, None] // m // 2 == j[None, :] // m // 2) & (j[:, None] // m != j[None, :] // m)
                                for m in (1, 2, 4, 8, 16, 32)]) for b in before])
    no_start = np.broadcast_to(np.arange(S) % CH != 0, (P, S))
    tt = np.linspace(0.0, 1.0, S)
    bands = (EMB - 1) // 2
    turn = (2.0 * np.pi / S) * np.arange(S)[:, None] * np.linspace(1e-4, bands - 1, bands)[None, :]
    pos_features = np.concatenate([tt[:, None], np.cos(turn), -np.sin(turn)], 1)
    deltas = np.abs(np.linspace(np.log(1e-2) / 1.5, np.log(1e-2) / 0.3, E))
    omega = np.pi / S * np.arange(S)[:, None] * (np.arange(S) + 0.5)[None, :]
    dft = np.concatenate([np.cos(omega), np.sin(omega)], 1)
    idft = np.concatenate([np.cos(omega), -np.sin(omega)], 1).T / S
    return {
        "k_pos": np.ascontiguousarray(pos_features.T).astype(f),
        "k_window": np.exp(-tt[:, None] * deltas[None, :]).astype(f),
        "k_dft": np.ascontiguousarray(dft.reshape(NT, P, 2 * S).transpose(1, 0, 2)).astype(f),
        "k_idft": np.ascontiguousarray(idft.reshape(4, P, S).transpose(1, 0, 2)).astype(f),
        "k_strict": strict.transpose(1, 0, 2, 3).astype(f),
        "k_level": level.transpose(2, 0, 1, 3).astype(f),
        "k_no_start": no_start.astype(f),
        "k_same_head": same.astype(f),
        "k_head_mean": (same / CH).astype(f),
        "k_ident": np.eye(P, dtype=f),
        "k_rope": np.ascontiguousarray(rope.reshape(2, 2, NT, P, P).transpose(3, 0, 1, 2, 4)).astype(f),
        "k_decay": decay.astype(f),
        "k_xi": np.broadcast_to(np.exp(log_g[:, None] * (idx + 1.0)), (P, CHEADS, P)).astype(f),
        "k_zeta": np.exp(log_g[None, :] * (P - 1 - idx)[:, None]).astype(f),
        "k_causal": (diff >= 0).astype(f),
    }


_INS = ["x", "c", "ctx", "c_ctx", "ada_w", "ada_b", "norm_pre", "norm_post", "w_out",
        "l0_w_in", "l0_mu", "l0_w0", "l0_w2", "l0_a0", "l0_a2", "l0_k_k", "l0_k_a", "l0_r_k", "l0_ln_w", "l0_ln_b",
        "l1_w_in", "l1_conv_w", "l1_conv_b", "l1_f_w1", "l1_f_b1", "l1_f_w2", "l1_f_b2", "l1_f_w3", "l1_f_b3", "l1_f_w4",
        "l1_sin_freq", "l1_filter_bias", "ffn1_norm_2", "ffn1_w_gate_2", "ffn1_w_up_2", "ffn1_w_down_2", "mix_norm_2",
        "w_in_2", "gmlp_v_norm_2", "gmlp_w_s_2", "gmlp_b_s_2", "conv_w_2", "ret_gn_2", "w_out_2", "ffn2_norm_2",
        "ffn2_w_gate_2", "ffn2_w_up_2", "ffn2_w_down_2", "final_norm_2"]


def kernel(**inputs):
    import concourse.bacc as bacc
    from concourse.bass_utils import run_bass_kernel_spmd

    nc = bacc.Bacc("TRN2", target_bir_lowering=False, num_devices=1)
    arrays, a = {}, {}
    given = {n: np.ascontiguousarray(inputs[n]) for n in _INS}
    for name, v in {**given, **constants()}.items():
        arrays[f"in_{name}"] = v
        a[name] = nc.dram_tensor(f"in_{name}", v.shape, mybir.dt.from_np(v.dtype), kind="ExternalInput").ap()
    out = nc.dram_tensor("out_0", (1, S, D), F32, kind="ExternalOutput").ap()
    build(nc, a, out)
    r = run_bass_kernel_spmd(nc, [arrays], core_ids=[0])
    return r.results[0]["out_0"]
```
